# Optimizing a Trainium2 kernel written in Bass

```python
import jax, jax.numpy as jnp
from jax import lax
import numpy as np

D_MODEL = 1024
BATCH = 1
SEQ = 512
DEPTH = 2

HEAD_DIM = 64
N_HEADS_A = D_MODEL // (2 * HEAD_DIM)
N_HEADS_B = D_MODEL // (2 * HEAD_DIM)
N_KV_B = N_HEADS_B // 4
N_HEADS_C = D_MODEL // HEAD_DIM
WINDOW_B = 128
DILATION_PAIRS = ((128, 1), (512, 4), (2048, 16))
BLOCK = 128
D_FF = 4 * D_MODEL
EPS = 1e-6
EVEN_IN_WIDTH = 3 * N_HEADS_A * HEAD_DIM + N_HEADS_B * HEAD_DIM + 2 * N_KV_B * HEAD_DIM
EVEN_MIX_WIDTH = (N_HEADS_A + N_HEADS_B) * HEAD_DIM
ODD_IN_WIDTH = 3 * N_HEADS_C * HEAD_DIM + N_HEADS_C
ODD_MIX_WIDTH = N_HEADS_C * HEAD_DIM


def rms_norm(x, gain):
    xf = x.astype(jnp.float32)
    y = xf * lax.rsqrt(jnp.mean(xf * xf, axis=-1, keepdims=True) + EPS)
    return (y * gain.astype(jnp.float32)).astype(x.dtype)

def alibi_slopes(n):
    return jnp.asarray(2.0 ** (-8.0 * np.arange(1, n + 1) / n), dtype=jnp.float32)

def dilated_attention(q, k, v, slopes):
    bsz, seq, nh, dh = q.shape
    nblk = seq // BLOCK
    scale = dh ** -0.5
    q_blocks = jnp.moveaxis(q.reshape(bsz, nblk, BLOCK, nh, dh), 1, 0)
    slope_b = slopes[None, :, None, None]

    def block_fn(args):
        blk, qb = args
        t = blk * BLOCK + jnp.arange(BLOCK)
        parts = []
        for window, dil in DILATION_PAIRS:
            dist = jnp.arange(window // dil + 1) * dil
            idx = t[:, None] - dist[None, :]
            valid = idx >= 0
            idx = jnp.maximum(idx, 0)
            kg = k[:, idx]
            vg = v[:, idx]
            s = jnp.einsum("bqhd,bqjhd->bhqj", qb, kg).astype(jnp.float32) * scale
            s = s - slope_b * dist.astype(jnp.float32)
            s = jnp.where(valid[None, None], s, -jnp.inf)
            m = jnp.max(s, axis=-1, keepdims=True)
            p = jnp.exp(s - m)
            den = jnp.sum(p, axis=-1, keepdims=True)
            num = jnp.einsum("bhqj,bqjhd->bhqd", p.astype(v.dtype), vg).astype(jnp.float32)
            parts.append((m, num, den))
        m_all = parts[0][0]
        for m, _, _ in parts[1:]:
            m_all = jnp.maximum(m_all, m)
        num_all = 0.0
        den_all = 0.0
        for m, num, den in parts:
            w = jnp.exp(m - m_all)
            num_all = num_all + w * num
            den_all = den_all + w * den
        out = num_all / den_all
        return jnp.transpose(out, (0, 2, 1, 3)).astype(q.dtype)

    out = lax.map(block_fn, (jnp.arange(nblk), q_blocks))
    return jnp.moveaxis(out, 0, 1).reshape(bsz, seq, nh, dh)

def sliding_window_sink_attention(q, k, v, sinks, slopes):
    bsz, seq, nhq, dh = q.shape
    nkv = k.shape[2]
    grp = nhq // nkv
    nblk = seq // BLOCK
    scale = dh ** -0.5
    qb = q.reshape(bsz, nblk, BLOCK, nkv, grp, dh)
    pad = ((0, 0), (BLOCK, 0), (0, 0), (0, 0))
    kp = jnp.pad(k, pad).reshape(bsz, nblk + 1, BLOCK, nkv, dh)
    vp = jnp.pad(v, pad).reshape(bsz, nblk + 1, BLOCK, nkv, dh)
    kw = jnp.concatenate([kp[:, :-1], kp[:, 1:]], axis=2)
    vw = jnp.concatenate([vp[:, :-1], vp[:, 1:]], axis=2)
    s = jnp.einsum("bnqkgd,bnskd->bnkgqs", qb, kw).astype(jnp.float32) * scale
    qpos = jnp.arange(BLOCK)
    kpos = jnp.arange(2 * BLOCK)
    dist = qpos[:, None] - kpos[None, :] + BLOCK
    abs_k = jnp.arange(nblk)[:, None] * BLOCK + kpos[None, :] - BLOCK
    valid = ((dist >= 0) & (dist < WINDOW_B))[None] & (abs_k >= 0)[:, None, :]
    slope_kg = slopes.reshape(nkv, grp)[:, :, None, None]
    s = s - slope_kg * dist.astype(jnp.float32)
    s = jnp.where(valid[None, :, None, None], s, -jnp.inf)
    sink = sinks.astype(jnp.float32).reshape(nkv, grp)[:, :, None, None]
    m = jnp.maximum(jnp.max(s, axis=-1, keepdims=True), sink)
    p = jnp.exp(s - m)
    den = jnp.sum(p, axis=-1) + jnp.exp(sink - m)[..., 0]
    num = jnp.einsum("bnkgqs,bnskd->bnqkgd", p.astype(v.dtype), vw).astype(jnp.float32)
    out = num / jnp.transpose(den, (0, 1, 4, 2, 3))[..., None]
    return out.astype(q.dtype).reshape(bsz, seq, nhq, dh)

def forgetting_attention(q, k, v, log_f):
    bsz, seq, nh, dh = q.shape
    nblk = seq // BLOCK
    scale = dh ** -0.5
    c = jnp.cumsum(log_f, axis=1)
    c_k = jnp.transpose(c, (0, 2, 1))
    q_blocks = jnp.moveaxis(q.reshape(bsz, nblk, BLOCK, nh, dh), 1, 0)
    c_blocks = jnp.moveaxis(c.reshape(bsz, nblk, BLOCK, nh), 1, 0)
    key_pos = jnp.arange(seq)

    def block_fn(args):
        blk, qb, cq = args
        t = blk * BLOCK + jnp.arange(BLOCK)
        s = jnp.einsum("bqhd,bshd->bhqs", qb, k).astype(jnp.float32) * scale
        s = s + jnp.transpose(cq, (0, 2, 1))[..., None] - c_k[:, :, None, :]
        s = jnp.where((key_pos[None, :] <= t[:, None])[None, None], s, -jnp.inf)
        p = jax.nn.softmax(s, axis=-1)
        return jnp.einsum("bhqs,bshd->bqhd", p.astype(v.dtype), v)

    out = lax.map(block_fn, (jnp.arange(nblk), q_blocks, c_blocks))
    return jnp.moveaxis(out, 0, 1).reshape(bsz, seq, nh, dh)

def even_mixer(h, w_in, a_q_gain, a_k_gain, b_q_gain, b_k_gain, b_sinks, w_out):
    bsz, seq, _ = h.shape
    proj = jnp.einsum("bsd,de->bse", h, w_in)
    widths = [N_HEADS_A * HEAD_DIM] * 3 + [N_HEADS_B * HEAD_DIM, N_KV_B * HEAD_DIM, N_KV_B * HEAD_DIM]
    offs = np.cumsum(widths)[:-1].tolist()
    aq, ak, av, bq, bk, bv = jnp.split(proj, offs, axis=-1)
    aq = rms_norm(aq.reshape(bsz, seq, N_HEADS_A, HEAD_DIM), a_q_gain)
    ak = rms_norm(ak.reshape(bsz, seq, N_HEADS_A, HEAD_DIM), a_k_gain)
    av = av.reshape(bsz, seq, N_HEADS_A, HEAD_DIM)
    bq = rms_norm(bq.reshape(bsz, seq, N_HEADS_B, HEAD_DIM), b_q_gain)
    bk = rms_norm(bk.reshape(bsz, seq, N_KV_B, HEAD_DIM), b_k_gain)
    bv = bv.reshape(bsz, seq, N_KV_B, HEAD_DIM)
    slopes = alibi_slopes(N_HEADS_B + N_HEADS_A)
    a_out = dilated_attention(aq, ak, av, slopes[N_HEADS_B:])
    b_out = sliding_window_sink_attention(bq, bk, bv, b_sinks, slopes[:N_HEADS_B])
    y = jnp.concatenate([a_out.reshape(bsz, seq, -1), b_out.reshape(bsz, seq, -1)], axis=-1)
    return jnp.einsum("bse,ed->bsd", y, w_out)

def odd_mixer(h, w_in, b_forget, c_q_gain, c_k_gain, w_out):
    bsz, seq, _ = h.shape
    proj = jnp.einsum("bsd,de->bse", h, w_in)
    w = N_HEADS_C * HEAD_DIM
    q = rms_norm(proj[..., :w].reshape(bsz, seq, N_HEADS_C, HEAD_DIM), c_q_gain)
    k = rms_norm(proj[..., w:2 * w].reshape(bsz, seq, N_HEADS_C, HEAD_DIM), c_k_gain)
    v = proj[..., 2 * w:3 * w].reshape(bsz, seq, N_HEADS_C, HEAD_DIM)
    f_logit = proj[..., 3 * w:].astype(jnp.float32) + b_forget.astype(jnp.float32)
    log_f = jax.nn.log_sigmoid(f_logit)
    y = forgetting_attention(q, k, v, log_f)
    return jnp.einsum("bse,ed->bsd", y.reshape(bsz, seq, w), w_out)

def squared_relu_mlp(h, w_up, w_down):
    u = jnp.einsum("bsd,df->bsf", h, w_up)
    return jnp.einsum("bsf,fd->bsd", jnp.square(jax.nn.relu(u)), w_down)

def first_inputs(seed: int = 0) -> dict:
    key = jax.random.key(seed)
    ks = jax.random.split(key, 18)
    n_even = (DEPTH + 1) // 2
    n_odd = DEPTH // 2
    d = D_MODEL

    def nrm(k, shape, fan_in):
        return jax.random.normal(k, shape, jnp.float32) * fan_in ** -0.5

    def gain(k, shape):
        return 1.0 + 0.02 * jax.random.normal(k, shape, jnp.float32)

    return {
        "x": jax.random.normal(ks[0], (BATCH, SEQ, d), jnp.float32),
        "g_mix": gain(ks[1], (DEPTH, d)),
        "g_mlp": gain(ks[2], (DEPTH, d)),
        "w_in_even": nrm(ks[3], (n_even, d, EVEN_IN_WIDTH), d),
        "a_q_gain": gain(ks[4], (n_even, HEAD_DIM)),
        "a_k_gain": gain(ks[5], (n_even, HEAD_DIM)),
        "b_q_gain": gain(ks[6], (n_even, HEAD_DIM)),
        "b_k_gain": gain(ks[7], (n_even, HEAD_DIM)),
        "b_sinks": 0.5 * jax.random.normal(ks[8], (n_even, N_HEADS_B), jnp.float32),
        "w_out_even": nrm(ks[9], (n_even, EVEN_MIX_WIDTH, d), EVEN_MIX_WIDTH),
        "w_in_odd": nrm(ks[10], (n_odd, d, ODD_IN_WIDTH), d),
        "b_forget": jax.random.uniform(ks[11], (n_odd, N_HEADS_C), jnp.float32, 2.0, 6.0),
        "c_q_gain": gain(ks[12], (n_odd, HEAD_DIM)),
        "c_k_gain": gain(ks[13], (n_odd, HEAD_DIM)),
        "w_out_odd": nrm(ks[14], (n_odd, ODD_MIX_WIDTH, d), ODD_MIX_WIDTH),
        "w_up": nrm(ks[15], (DEPTH, d, D_FF), d),
        "w_down": nrm(ks[16], (DEPTH, D_FF, d), D_FF),
    }

def first_block(x, g_mix, g_mlp, w_in_even, a_q_gain, a_k_gain, b_q_gain, b_k_gain, b_sinks,
              w_out_even, w_in_odd, b_forget, c_q_gain, c_k_gain, w_out_odd, w_up, w_down):
    for layer in range(DEPTH):
        i = layer // 2
        h = rms_norm(x, g_mix[layer])
        if layer % 2 == 0:
            x = x + even_mixer(h, w_in_even[i], a_q_gain[i], a_k_gain[i], b_q_gain[i],
                               b_k_gain[i], b_sinks[i], w_out_even[i])
        else:
            x = x + odd_mixer(h, w_in_odd[i], b_forget[i], c_q_gain[i], c_k_gain[i], w_out_odd[i])
        h = rms_norm(x, g_mlp[layer])
        x = x + squared_relu_mlp(h, w_up[layer], w_down[layer])
    return x


CHUNK = 64
MEM_LEN = 256
N_A_LAYERS = DEPTH // 2
N_B_LAYERS = DEPTH - N_A_LAYERS
MEM_HEADS = 4
MEM_HEAD_DIM = 64
MEM_W = MEM_HEADS * MEM_HEAD_DIM
MAIN_W = D_MODEL - MEM_W
CONV_W = MAIN_W
CONV_K = 3
DIFF_HEAD_DIM = 64
DIFF_HEADS = MAIN_W // (2 * DIFF_HEAD_DIM)
DIFF_QK = DIFF_HEADS * DIFF_HEAD_DIM
ROPE_DIM = DIFF_HEAD_DIM // 4
ROPE_THETA = 500000.0
D_FF_2 = 4 * D_MODEL
Q_BLOCK = 128
SUBLN_EPS = 1e-5


def rmsnorm(x, g, eps=EPS):
    xf = x.astype(jnp.float32)
    y = xf * lax.rsqrt(jnp.mean(xf * xf, axis=-1, keepdims=True) + eps)
    return (y * g.astype(jnp.float32)).astype(x.dtype)

def rope_tables(seq):
    inv = 1.0 / (ROPE_THETA ** (jnp.arange(0, ROPE_DIM, 2, dtype=jnp.float32) / ROPE_DIM))
    ang = jnp.arange(seq, dtype=jnp.float32)[:, None] * inv[None, :]
    return jnp.cos(ang), jnp.sin(ang)

def partial_rope(x, cos, sin):
    half = ROPE_DIM // 2
    c = cos[None, :, None, :].astype(x.dtype)
    s = sin[None, :, None, :].astype(x.dtype)
    x1, x2, xp = x[..., :half], x[..., half:ROPE_DIM], x[..., ROPE_DIM:]
    return jnp.concatenate([x1 * c - x2 * s, x1 * s + x2 * c, xp], axis=-1)

def short_conv_mixer(h, gate_b, gate_c, w_conv):
    u = gate_c * h
    s_len = u.shape[1]
    up = jnp.pad(u, ((0, 0), (CONV_K - 1, 0), (0, 0)))
    y = w_conv[0] * up[:, 0:s_len]
    for k in range(1, CONV_K):
        y = y + w_conv[k] * up[:, k:k + s_len]
    return gate_b * y

def memory_attention(q, mem_n, w_mem_kv, q_gain, k_gain):
    b, s, _ = q.shape
    m = mem_n.shape[1]
    kv = jnp.einsum('bmd,de->bme', mem_n, w_mem_kv)
    k = kv[..., :MEM_W].reshape(b, m, MEM_HEADS, MEM_HEAD_DIM)
    v = kv[..., MEM_W:].reshape(b, m, MEM_HEADS, MEM_HEAD_DIM)
    qh = rmsnorm(q.reshape(b, s, MEM_HEADS, MEM_HEAD_DIM), q_gain)
    k = rmsnorm(k, k_gain)
    sc = jnp.einsum('bshd,bmhd->bhsm', qh, k).astype(jnp.float32) * (MEM_HEAD_DIM ** -0.5)
    p = jax.nn.softmax(sc, axis=-1).astype(v.dtype)
    o = jnp.einsum('bhsm,bmhd->bshd', p, v)
    return o.reshape(b, s, MEM_W)

def diff_attention(q1, q2, k1, k2, v, lam):
    b, s, h, dh = q1.shape
    nblk = s // Q_BLOCK
    scale = dh ** -0.5
    key_chunk = jnp.arange(s) // CHUNK
    qb1 = jnp.moveaxis(q1.reshape(b, nblk, Q_BLOCK, h, dh), 1, 0)
    qb2 = jnp.moveaxis(q2.reshape(b, nblk, Q_BLOCK, h, dh), 1, 0)

    def one_block(args):
        a1, a2, i = args
        q_chunk = (i * Q_BLOCK + jnp.arange(Q_BLOCK)) // CHUNK
        mask = (key_chunk[None, :] <= q_chunk[:, None])[None, None]
        s1 = jnp.einsum('bqhd,bkhd->bhqk', a1, k1).astype(jnp.float32) * scale
        s2 = jnp.einsum('bqhd,bkhd->bhqk', a2, k2).astype(jnp.float32) * scale
        p1 = jax.nn.softmax(jnp.where(mask, s1, -jnp.inf), axis=-1)
        p2 = jax.nn.softmax(jnp.where(mask, s2, -jnp.inf), axis=-1)
        p = (p1 - lam * p2).astype(v.dtype)
        return jnp.einsum('bhqk,bkhe->bqhe', p, v)

    out = lax.map(one_block, (qb1, qb2, jnp.arange(nblk)))
    return jnp.moveaxis(out, 0, 1).reshape(b, s, h, 2 * dh)

def sqrelu_mlp(h, w_up, w_down):
    u = jnp.einsum('bsd,df->bsf', h, w_up)
    return jnp.einsum('bsf,fd->bsd', jnp.square(jax.nn.relu(u)), w_down)

def second_inputs(seed: int = 0) -> dict:
    key = jax.random.key(seed)
    ks = jax.random.split(key, 24)
    f32 = jnp.float32
    nrm = lambda k, shp, sc: jax.random.normal(k, shp, f32) * sc
    gain = lambda k, shp: 1.0 + 0.02 * jax.random.normal(k, shp, f32)
    return {
        "x": nrm(ks[0], (BATCH, SEQ, D_MODEL), 1.0),
        "mem": nrm(ks[1], (BATCH, MEM_LEN, D_MODEL), 1.0),
        "norm_mix": gain(ks[2], (DEPTH, D_MODEL)),
        "norm_mlp": gain(ks[3], (DEPTH, D_MODEL)),
        "a_w_in": nrm(ks[4], (N_A_LAYERS, D_MODEL, 3 * CONV_W + MEM_W), D_MODEL ** -0.5),
        "a_conv": nrm(ks[5], (N_A_LAYERS, CONV_K, CONV_W), CONV_K ** -0.5),
        "b_w_q": nrm(ks[6], (N_B_LAYERS, D_MODEL, 2 * DIFF_QK + MEM_W), D_MODEL ** -0.5),
        "b_q_norm": gain(ks[7], (N_B_LAYERS, DIFF_HEAD_DIM)),
        "b_lam": nrm(ks[8], (N_B_LAYERS, 4, DIFF_HEAD_DIM), 0.1),
        "b_subln": gain(ks[9], (N_B_LAYERS, 2 * DIFF_HEAD_DIM)),
        "kv_norm": gain(ks[10], (D_MODEL,)),
        "w_kv": nrm(ks[11], (D_MODEL, 2 * DIFF_QK + MAIN_W), D_MODEL ** -0.5),
        "k_norm": gain(ks[12], (DIFF_HEAD_DIM,)),
        "mem_norm": gain(ks[13], (D_MODEL,)),
        "w_mem_kv": nrm(ks[14], (DEPTH, D_MODEL, 2 * MEM_W), D_MODEL ** -0.5),
        "mem_q_norm": gain(ks[15], (DEPTH, MEM_HEAD_DIM)),
        "mem_k_norm": gain(ks[16], (DEPTH, MEM_HEAD_DIM)),
        "w_o": nrm(ks[17], (DEPTH, MAIN_W + MEM_W, D_MODEL), (MAIN_W + MEM_W) ** -0.5),
        "w_up": nrm(ks[18], (DEPTH, D_MODEL, D_FF_2), D_MODEL ** -0.5),
        "w_down": nrm(ks[19], (DEPTH, D_FF_2, D_MODEL), 0.5 * D_FF_2 ** -0.5),
    }

def second_block(x, mem, norm_mix, norm_mlp, a_w_in, a_conv, b_w_q, b_q_norm, b_lam, b_subln,
              kv_norm, w_kv, k_norm, mem_norm, w_mem_kv, mem_q_norm, mem_k_norm,
              w_o, w_up, w_down):
    b, s, _ = x.shape
    cos, sin = rope_tables(s)
    mem_n = rmsnorm(mem, mem_norm)
    k1 = k2 = v = None
    for l in range(DEPTH):
        h = rmsnorm(x, norm_mix[l])
        if l < N_A_LAYERS:
            proj = jnp.einsum('bsd,de->bse', h, a_w_in[l])
            gate_b = proj[..., :CONV_W]
            gate_c = proj[..., CONV_W:2 * CONV_W]
            hv = proj[..., 2 * CONV_W:3 * CONV_W]
            qm = proj[..., 3 * CONV_W:]
            main = short_conv_mixer(hv, gate_b, gate_c, a_conv[l])
        else:
            j = l - N_A_LAYERS
            proj = jnp.einsum('bsd,de->bse', h, b_w_q[j])
            q1 = proj[..., :DIFF_QK].reshape(b, s, DIFF_HEADS, DIFF_HEAD_DIM)
            q2 = proj[..., DIFF_QK:2 * DIFF_QK].reshape(b, s, DIFF_HEADS, DIFF_HEAD_DIM)
            qm = proj[..., 2 * DIFF_QK:]
            q1 = partial_rope(rmsnorm(q1, b_q_norm[j]), cos, sin)
            q2 = partial_rope(rmsnorm(q2, b_q_norm[j]), cos, sin)
            lam_init = 0.8 - 0.6 * float(np.exp(-0.3 * l))
            lp = b_lam[j].astype(jnp.float32)
            lam = (jnp.exp(jnp.sum(lp[0] * lp[1])) - jnp.exp(jnp.sum(lp[2] * lp[3]))
                   + lam_init)
            o = diff_attention(q1, q2, k1, k2, v, lam)
            o = rmsnorm(o, b_subln[j], SUBLN_EPS) * (1.0 - lam_init)
            main = o.reshape(b, s, MAIN_W)
        mo = memory_attention(qm, mem_n, w_mem_kv[l], mem_q_norm[l], mem_k_norm[l])
        x = x + jnp.einsum('bse,ed->bsd', jnp.concatenate([main, mo], axis=-1), w_o[l])
        x = x + sqrelu_mlp(rmsnorm(x, norm_mlp[l]), w_up[l], w_down[l])
        if l == N_A_LAYERS - 1:
            kvh = rmsnorm(x, kv_norm)
            kv = jnp.einsum('bsd,de->bse', kvh, w_kv)
            k1 = kv[..., :DIFF_QK].reshape(b, s, DIFF_HEADS, DIFF_HEAD_DIM)
            k2 = kv[..., DIFF_QK:2 * DIFF_QK].reshape(b, s, DIFF_HEADS, DIFF_HEAD_DIM)
            v = kv[..., 2 * DIFF_QK:].reshape(b, s, DIFF_HEADS, 2 * DIFF_HEAD_DIM)
            k1 = partial_rope(rmsnorm(k1, k_norm), cos, sin)
            k2 = partial_rope(rmsnorm(k2, k_norm), cos, sin)
    return x


def setup_inputs(seed=0):
    out = dict(first_inputs(seed))
    for name, value in second_inputs(seed + 1).items():
        if name != "x":
            out[name + "_2"] = value
    return out


def reference(
    x, g_mix, g_mlp, w_in_even, a_q_gain, a_k_gain, b_q_gain, b_k_gain, b_sinks, w_out_even,
    w_in_odd, b_forget, c_q_gain, c_k_gain, w_out_odd, w_up, w_down, mem_2, norm_mix_2,
    norm_mlp_2, a_w_in_2, a_conv_2, b_w_q_2, b_q_norm_2, b_lam_2, b_subln_2, kv_norm_2, w_kv_2,
    k_norm_2, mem_norm_2, w_mem_kv_2, mem_q_norm_2, mem_k_norm_2, w_o_2, w_up_2, w_down_2,
):
    x = first_block(
        x, g_mix, g_mlp, w_in_even, a_q_gain, a_k_gain, b_q_gain, b_k_gain, b_sinks, w_out_even,
        w_in_odd, b_forget, c_q_gain, c_k_gain, w_out_odd, w_up, w_down,
    )
    return second_block(
        x, mem_2, norm_mix_2, norm_mlp_2, a_w_in_2, a_conv_2, b_w_q_2, b_q_norm_2, b_lam_2,
        b_subln_2, kv_norm_2, w_kv_2, k_norm_2, mem_norm_2, w_mem_kv_2, mem_q_norm_2,
        mem_k_norm_2, w_o_2, w_up_2, w_down_2,
    )


_drawn_inputs = setup_inputs


def setup_inputs(seed=0):
    import zlib

    import numpy as np

    out = dict(_drawn_inputs(seed))
    spreads = {}
    factors = {'g_mix': 4.006,
     'a_q_gain': 8.0,
     'a_k_gain': 8.0,
     'b_q_gain': 8.0,
     'b_k_gain': 8.0,
     'c_q_gain': 8.0,
     'c_k_gain': 8.0,
     'norm_mix_2': 4.42,
     'norm_mlp_2': 29.199,
     'b_q_norm_2': 200.0,
     'b_lam_2': 7.976,
     'b_subln_2': 200.0,
     'kv_norm_2': 200.0,
     'k_norm_2': 200.0,
     'mem_norm_2': 38.057,
     'mem_q_norm_2': 51.21,
     'mem_k_norm_2': 36.452,
     'b_sinks': 64.0}
    for name, (base, spread) in spreads.items():
        noise = np.random.default_rng([zlib.crc32(name.encode()), seed]).standard_normal(out[name].shape)
        drawn = base * np.exp(spread * noise) if base else spread * noise
        out[name] = __import__('jax').numpy.asarray(drawn.astype(out[name].dtype))
    for name, factor in factors.items():
        out[name] = (out[name] * factor).astype(out[name].dtype)
    return out
```

```python
import numpy as np
import concourse.bass as bass
from concourse import mybir
from contextlib import ExitStack

F32 = mybir.dt.float32
F32R = mybir.dt.float32r
BF16 = mybir.dt.bfloat16
ALU = mybir.AluOpType
ACT = mybir.ActivationFunctionType
AX = mybir.AxisListType

P = 128
D = 1024
SEQ = 512
MEM = 256
FF = 4096
KT = D // P
TB = SEQ // P
HD = 64
TILE = 512
EPS = 1e-6
SUBLN_EPS = 1e-5
BIG = 1e30
LAM_INIT = 0.8 - 0.6 * float(np.exp(-0.3 * 1))
RING = 8
PAIRS = 4
HALVES = 2
HID = FF // HALVES // P

C_IDENT, C_MEAN, C_DELTA, C_LOGW, C_WIN, C_TRI, C_CAUSAL, C_CHUNK, C_COS, C_SIN = (
    0, 128, 256, 768, 1280, 1536, 2048, 2176, 2304, 2336)
C_ALL = 2368
V_GAIN = {n: 8 * i for i, n in enumerate(
    ["mix0", "mix1", "mlp0", "mlp1", "mixb0", "mixb1", "mlpb0", "mlpb1", "kv", "mem"])}
V_CONV = 80
V_SUB = 98
V_HEAD = {n: 99 + HD * i for i, n in enumerate(
    ["aq", "ak", "bq", "bk", "cq", "ck", "dq", "dk", "mq0", "mq1", "mk0", "mk1"])}
V_SINK = 99 + 12 * HD
V_FORGET = V_SINK + 8
V_LAM = V_FORGET + 16
V_ALL = V_LAM + 256
DILATIONS = ((128, 1), (512, 4), (2048, 16))


def constants():
    c = np.zeros((P, C_ALL), np.float32)
    p = np.arange(P)[:, None]
    c[:, C_IDENT:C_IDENT + P] = np.eye(P)
    c[:, C_MEAN:C_MEAN + P] = 1.0 / D
    dist = p - np.arange(512)[None] + 384
    c[:, C_DELTA:C_DELTA + 512] = dist
    times = sum(((dist % d == 0) & (dist <= w)).astype(np.float64) for w, d in DILATIONS)
    ok = (dist >= 0) & (times > 0)
    c[:, C_LOGW:C_LOGW + 512] = np.where(ok, -np.log(np.maximum(times, 1)), BIG)
    near = p - np.arange(256)[None] + 128
    c[:, C_WIN:C_WIN + 256] = np.where((near >= 0) & (near < 128), 0.0, BIG)
    c[:, C_TRI:C_TRI + 512] = p <= np.arange(512)[None]
    f = np.arange(P)[None]
    c[:, C_CAUSAL:C_CAUSAL + P] = np.where(f > p, BIG, 0.0)
    c[:, C_CHUNK:C_CHUNK + P] = np.where(f // 64 > p // 64, BIG, 0.0)
    half = 8
    inv = (1.0 / (np.float32(500000.0) ** (np.arange(0, 16, 2, dtype=np.float32) / np.float32(16)))).astype(np.float32)
    ang = (np.arange(SEQ, dtype=np.float32)[:, None] * inv[None]).astype(np.float32)
    for at, fn in ((C_COS, np.cos), (C_SIN, np.sin)):
        c[:, at:at + TB * half] = fn(ang).astype(np.float32).reshape(TB, P, half).transpose(1, 0, 2).reshape(P, -1)
    return c


class Group:

    def __init__(self, form, width=TILE, heads=0, gains=(), rope=0, qk=(), scale=1.0, v=None, t=None):
        self.form = form
        self.width = width
        self.slots = 8 if width == TILE else 4
        self.heads = heads
        self.gains = gains
        self.rope = rope
        self.qk = qk
        self.scale = scale
        self.v = v
        self.t = t


class Stage:
    def __init__(self, kind, **kw):
        self.kind = kind
        self.norm = kw.get("norm")
        self.groups = kw.get("groups", [])
        self.mem = kw.get("mem", False)
        self.rbc = kw.get("rbc", False)
        self.forget = kw.get("forget", False)
        self.units = kw.get("units", [])
        self.diff = kw.get("diff", False)
        self.src = kw.get("src")
        self.last = kw.get("last", False)


class Unit:

    def __init__(self, qs, ks, vs, y, bias=None, head=None, mask=None, sink=None, forget=None):
        self.qs, self.ks = qs, ks
        self.vs = vs
        self.y = y
        self.n = P * len(vs)
        self.bias, self.head, self.mask, self.sink, self.forget = bias, head, mask, sink, forget


MLP_TILES = 64
MLP_GROUPS = 6
TURN = dict(tile=MLP_TILES, group=MLP_GROUPS, free=24, stat=1, var=1, hid=HID, bc=1,
            rn=1)
DVE_STEPS_A_TURN = 7


def build(nc, w_all, w_f, x_t, mem_t, consts_d, vecs_d, out_t):
    ctx = ExitStack()
    with ctx:
        def sb(name, shape, dt=F32, where=ctx):
            return where.enter_context(nc.sbuf_tensor(name, shape, dt))

        def sem(name):
            return ctx.enter_context(nc.semaphore(name))

        xT = sb("xT", [P, KT, SEQ])
        stage_w = sb("stage_w", [P, PAIRS, 2, TILE])
        w_hi = sb("w_hi", [P, RING, TILE], F32R)
        w_lo = sb("w_lo", [P, RING, TILE], F32R)
        cst = sb("cst", [P, C_ALL])
        vec = sb("vec", [P, V_ALL])
        mem_kT = sb("mem_kT", [P, 2, 2, MEM])
        mem_v = sb("mem_v", [P, 2, 2, MEM])
        rms_bc = sb("rms_bc", [P, SEQ])
        ssum = sb("ssum", [P, SEQ])
        sqb = sb("sqb", [P, 2, SEQ])
        wf_in = sb("wf_in", [P, P])
        wf_hi = sb("wf_hi", [P, P], F32R)
        wf_lo = sb("wf_lo", [P, P], F32R)
        c_hi = sb("c_hi", [16, SEQ], F32R)
        c_lo = sb("c_lo", [16, SEQ], F32R)
        ident_r = sb("ident_r", [P, 16], F32R)
        ident_b = sb("ident_b", [P, P], BF16)
        causal_b = sb("causal_b", [P, P], BF16)
        chunk_b = sb("chunk_b", [P, P], BF16)
        rn = sb("rn", [P, TB])
        var = sb("var", [P, 32])
        root = sb("root", [P, 32])
        inv = sb("inv", [P, 32])
        newt = sb("newt", [P, 32])
        hsum = sb("hsum", [P, 32])
        fz = sb("fz", [P, 64])
        fa = sb("fa", [P, 64])
        fe = sb("fe", [P, 64])
        fl = sb("fl", [P, 64])
        mneg = sb("mneg", [P, 8])
        den = sb("den", [P, 8])
        rden = sb("rden", [P, 8])
        esink = sb("esink", [P, 8])
        nsink = sb("nsink", [P, 8])
        lam = sb("lam", [P, 8])
        h_hi = sb("h_hi", [P, KT, SEQ], F32R)
        only = ExitStack()
        h_lo = sb("h_lo", [P, KT, SEQ], F32R, only)
        only.close()
        scr = sb("scr", [P, KT * SEQ])
        prob = scr[:, 0:2048].rearrange("p (r n) -> p r n", r=4)
        probT = scr[:, 2048:3072].rearrange("p (r n) -> p r n", r=2)
        bias_t = scr[:, 3072:4096].rearrange("p (r n) -> p r n", r=2)
        only = ExitStack()
        hid_hi = sb("hid_hi", [P, HID, SEQ], F32R, only)
        hid_lo = sb("hid_lo", [P, HID, SEQ], F32R, only)
        relu = sb("relu", [P, 2, SEQ], F32, only)
        hsq = sb("hsq", [P, 2, SEQ], F32, only)
        only.close()
        qT = sb("qT", [P, KT, SEQ])
        kT = sb("kT", [P, KT, SEQ])
        vN = sb("vN", [P, TB, D])
        tn = sb("tn", [P, 2, TB, TILE])
        yN = tn[:, :, :, :].rearrange("p a b c -> p (a b c)").rearrange("p (t d) -> p t d", t=TB)
        uP = vN[:, :, :].rearrange("p a b -> p (a b)")[:, 0:6 * 514].rearrange("p (j n) -> p j n", j=6)

        ps = [ctx.enter_context(nc.psum_tensor(f"ps{i}", [P, 512], F32)) for i in range(8)]

        ident = cst[:, C_IDENT:C_IDENT + P]
        mean_w = cst[:, C_MEAN:C_MEAN + P]

        s_in = [sem(f"s_in{i}") for i in range(5)]
        s_load = [sem(f"s_load{i}") for i in range(PAIRS)]
        s_whi = sem("s_whi")
        s_wlo = sem("s_wlo")
        s_used = sem("s_used")
        s_free = sem("s_free")
        s_hhi = sem("s_hhi")
        s_hlo = sem("s_hlo")
        s_sq = sem("s_sq")
        s_sqc = sem("s_sqc")
        s_stat = sem("s_stat")
        s_var = sem("s_var")
        s_root = sem("s_root")
        s_rn = sem("s_rn")
        s_diag = sem("s_diag")
        s_bc = sem("s_bc")
        s_rbc = sem("s_rbc")
        s_t = sem("s_t")
        s_tr = sem("s_tr")
        s_tra = sem("s_tra")
        s_trv = sem("s_trv")
        s_score = sem("s_score")
        s_max = sem("s_max")
        s_prob = sem("s_prob")
        s_pc = sem("s_pc")
        s_pt = sem("s_pt")
        s_pta = sem("s_pta")
        s_ptv = sem("s_ptv")
        s_pv = sem("s_pv")
        s_o = sem("s_o")
        s_y = sem("s_y")
        s_hsq = sem("s_hsq")
        s_hidhi = sem("s_hidhi")
        s_hid = sem("s_hid")
        s_fmm = sem("s_fmm")
        s_fabs = sem("s_fabs")
        s_fln = sem("s_fln")
        s_flog = sem("s_flog")
        s_cmm = sem("s_cmm")
        s_chi = sem("s_chi")
        s_clo = sem("s_clo")
        s_set = sem("s_set")
        s_seta = sem("s_seta")
        s_act = sem("s_act")
        s_dve = sem("s_dve")
        s_out = sem("s_out")

        def tiles(tensor, first, n):
            return [tensor[:, first + j, :] for j in range(n)]

        def v_to(first):
            return lambda b, w: vN[:, b, first:first + w]

        ATT = -(HD ** -0.5)
        stages = []
        stages.append(Stage("proj", norm="mem", mem=True, groups=[
            Group("N", heads=4, gains=((0, 4, f"mk{l}"),), qk=[mem_kT[:, l, c, :] for c in range(2)],
                  v=(lambda l: lambda b, w: mem_v[:, l, b, :])(l)) for l in range(2)]))
        stages.append(Stage("proj", norm="mix0", groups=[
            Group("N", width=256, heads=2, gains=((0, 2, "bk"),), qk=tiles(kT, 4, 1), v=v_to(512)),
            Group("N", heads=8, gains=((0, 8, "aq"),), qk=tiles(qT, 0, 4), scale=ATT),
            Group("N", heads=8, gains=((0, 8, "ak"),), qk=tiles(kT, 0, 4)),
            Group("N", heads=8, gains=((0, 8, "bq"),), qk=tiles(qT, 4, 4), scale=ATT),
            Group("N", v=v_to(0))]))

        def rows(tensor, tile, base, a, b):
            return tensor[base:base + HD, tile, a:b]

        slopes = [float(np.float32(2.0 ** (-8.0 * i / 16))) for i in range(1, 17)]
        units = []
        for h in range(8):
            for i in range(TB):
                units.append(Unit([rows(qT, h // 2, HD * (h % 2), P * i, P * i + P)],
                                  [rows(kT, h // 2, HD * (h % 2), 0, P * i + P)],
                                  [vN[:, j, HD * h:HD * h + HD] for j in range(i + 1)],
                                  yN[:, i, HD * h:HD * h + HD],
                                  bias=((3 - i) * P, 512, "dilated"), head=(h, slopes[8 + h], i == 0)))
        for h in range(8):
            g = h // 4
            for i in range(TB):
                lo = max(0, i - 1)
                units.append(Unit([rows(qT, 4 + h % 4, HD * g, P * i, P * i + P)],
                                  [rows(kT, 4, HD * g, P * lo, P * i + P)],
                                  [vN[:, j, 512 + HD * g:512 + HD * g + HD] for j in range(lo, i + 1)],
                                  yN[:, i, 512 + HD * h:512 + HD * h + HD],
                                  bias=((1 - (i - lo)) * P, 256, "window"), head=(8 + h, slopes[h], i == 0),
                                  sink=h))
        stages.append(Stage("attn", units=units))
        natural = [("y", c, None) for c in range(8)]
        stages.append(Stage("out", src=natural))
        stages.append(Stage("mlp", norm="mlp0"))
        stages.append(Stage("proj", norm="mix1", forget=True, groups=[
            Group("N", heads=8, gains=((0, 8, "cq"),), qk=tiles(qT, 0, 4), scale=ATT),
            Group("N", heads=8, gains=((0, 8, "cq"),), qk=tiles(qT, 4, 4), scale=ATT),
            Group("N", heads=8, gains=((0, 8, "ck"),), qk=tiles(kT, 0, 4)),
            Group("N", heads=8, gains=((0, 8, "ck"),), qk=tiles(kT, 4, 4)),
            Group("N", v=v_to(0)), Group("N", v=v_to(512))]))
        units = []
        for h in range(16):
            for i in range(TB):
                units.append(Unit([rows(qT, h // 2, HD * (h % 2), P * i, P * i + P)],
                                  [rows(kT, h // 2, HD * (h % 2), 0, P * i + P)],
                                  [vN[:, j, HD * h:HD * h + HD] for j in range(i + 1)],
                                  yN[:, i, HD * h:HD * h + HD], mask=causal_b, forget=h))
        stages.append(Stage("attn", units=units))
        stages.append(Stage("out", src=natural))
        stages.append(Stage("mlp", norm="mlp1"))

        def memory_units(layer, first):
            return [Unit([rows(qT, first + h // 2, HD * (h % 2), P * i, P * i + P)],
                         [mem_kT[HD * (h % 2):HD * (h % 2) + HD, layer, h // 2, :]],
                         [mem_v[:, layer, j, HD * h:HD * h + HD] for j in range(2)],
                         yN[:, i, 768 + HD * h:768 + HD * h + HD]) for h in range(4) for i in range(TB)]

        c_t = [("c", j) for j in range(6)] + [("h", j) for j in range(6)] + [("b", j) for j in range(6)]
        stages.append(Stage("proj", norm="mixb0", rbc=True, groups=[
            Group("N", width=256, heads=4, gains=((0, 4, "mq0"),), qk=tiles(qT, 6, 2), scale=ATT),
            Group("T", t=c_t[0:4]), Group("T", t=c_t[4:8]), Group("T", t=c_t[8:12]),
            Group("T", t=c_t[12:16]), Group("T", width=256, t=c_t[16:18])]))
        stages.append(Stage("attn", units=memory_units(0, 6)))
        stages.append(Stage("out", src=[("z", c, None) for c in range(6)] + natural[6:]))
        stages.append(Stage("mlp", norm="mlpb0"))
        stages.append(Stage("proj", norm="kv", groups=[
            Group("N", heads=8, gains=((0, 8, "dk"),), rope=8, qk=tiles(kT, 0, 4)),
            Group("N", heads=4, gains=((0, 4, "dk"),), rope=4, qk=tiles(kT, 4, 2), v=v_to(0)),
            Group("N", v=v_to(256))]))
        stages.append(Stage("proj", norm="mixb1", groups=[
            Group("N", heads=8, gains=((0, 8, "dq"),), rope=8, qk=tiles(qT, 0, 4), scale=ATT),
            Group("N", heads=8, gains=((0, 4, "dq"), (4, 4, "mq1")), rope=4, qk=tiles(qT, 4, 4), scale=ATT)]))
        units = []
        for h in range(6):
            for i in range(TB):
                units.append(Unit([rows(qT, 3 * s + h // 2, HD * (h % 2), P * i, P * i + P) for s in range(2)],
                                  [rows(kT, 3 * s + h // 2, HD * (h % 2), 0, P * i + P) for s in range(2)],
                                  [vN[:, j, P * h:P * h + P] for j in range(i + 1)],
                                  yN[:, i, P * h:P * h + P], mask=chunk_b))
        stages.append(Stage("attn", units=units + memory_units(1, 6), diff=True))
        stages.append(Stage("out", src=[("y", c, vec[:, V_SUB:V_SUB + 1]) for c in range(6)] + natural[6:]))
        stages.append(Stage("mlp", norm="mlpb1", last=True))

        at = dict(tile=0, group=0, free=0, norm=0, hin=0, sq=0, stat=0, var=0, bc=0, t=0, tra=0, trv=0,
                  sm=0, unit=0, pta=0, ptv=0, hid=0, tr=0)
        for s in stages:
            s.at = dict(at)
            if s.norm:
                at["hin"] += 8
                at["sq"] += 8
            if s.kind == "proj":
                at["stat"] += 1
                at["var"] += 1
                at["bc"] += s.rbc
                for g in s.groups:
                    g.blocks = (len(g.t) if g.form == "T" else 2 if s.mem else TB)
                    g.tile0, g.grp, g.free0, g.var, g.t0 = at["tile"], at["group"], at["free"], at["var"], at["t"]
                    g.tra0, g.trv0, g.sq0, g.tr0 = at["tra"], at["trv"], at["sq"], at["tr"]
                    g.end = g.tile0 + g.slots
                    at["tile"] += g.slots
                    at["group"] += 1
                    at["free"] += g.blocks
                    if g.heads:
                        at["sq"] += g.blocks
                        at["var"] += 1
                        at["t"] += 1
                        at["tr"] += 1
                        at["tra"] += (len(g.qk) + 1) // 2
                        at["trv"] += len(g.qk) // 2
            elif s.kind == "attn":
                for u in s.units:
                    u.sm, u.i = at["sm"], at["unit"]
                    u.even = at["unit"] % 2 == 0
                    u.copy = at["pta"] if u.even else at["ptv"]
                    at["sm"] += len(u.qs)
                    at["unit"] += 1
                    at["pta" if u.even else "ptv"] += 1
                if s.diff:
                    at["sq"] += 4 * 2
                    at["var"] += 1
            elif s.kind == "out":
                at["hin"] += 8
                at["tr"] += sum(x[0] == "y" for x in s.src)
                at["tile"] += 16
                at["group"] += 2
                at["free"] += 8
            else:
                for k, d in TURN.items():
                    if k in at:
                        at[k] += HALVES * d
        TOTAL = at["tile"]
        LOADED = TOTAL + 8
        assert LOADED == w_all.shape[0] * 2, (LOADED, w_all.shape)

        def y_wait(eng, s):
            if s.after_diff:
                eng.wait_ge(s_y, 1)
            else:
                eng.wait_ge(s_o, s.at["unit"])

        for n, s in enumerate(stages):
            s.after_diff = n > 0 and stages[n - 1].diff
            s.unit_of = {u.sm + m: u.i for u in s.units for m in range(len(u.qs))}

        class Order:

            def __init__(self, eng, step):
                self.eng, self.step, self.n, self.last, self.turn = eng, step, {}, None, None

            def enter(self, i, adds):
                self.turn = (i, {id(x): d for x, d in adds}, dict(self.n))

            def leave(self):
                _, adds, before = self.turn
                for x, n in self.n.items():
                    assert n - before.get(x, 0) == adds.get(x, 0), (n - before.get(x, 0), adds.get(x, 0))
                for x, d in adds.items():
                    self.n[x] += (HALVES - 1) * d
                self.turn = None

            def do(self, ins, signal=None):
                self.last = signal or self.step
                ins.then_inc(self.last, 1)
                self.n[id(self.last)] = self.n.get(id(self.last), 0) + 1

            def sync(self):
                n = self.n[id(self.last)]
                if self.turn and id(self.last) in self.turn[1]:
                    n = self.turn[0] * self.turn[1][id(self.last)] + n
                self.eng.wait_ge(self.last, n)

        block = ctx.enter_context(nc.Block())

        @block.sync
        def _(sp):
            sp.dma_start(vec[:], vecs_d).then_inc(s_in[1], 16)
            for q in range(PAIRS):
                sp.dma_start(stage_w[:, q], w_all[q]).then_inc(s_load[q], 16)
            sp.dma_start(wf_in[:], w_f).then_inc(s_in[4], 16)
            whole = LOADED // RING
            with sp.Fori(1, whole) as c:
                for q in range(PAIRS):
                    sp.wait_ge(s_wlo, c * RING + (2 * q + 2 - RING))
                    sp.dma_start(stage_w[:, q], w_all[c * PAIRS + q]).then_inc(s_load[q], 16)
            for q in range((LOADED - whole * RING) // 2):
                sp.wait_ge(s_wlo, (whole - 1) * RING + 2 * q + 2)
                sp.dma_start(stage_w[:, q], w_all[whole * PAIRS + q]).then_inc(s_load[q], 16)
            for n in range(KT):
                sp.wait_ge(s_free, at["free"] - 8 + n + 1)
                sp.dma_start(out_t[n * P:(n + 1) * P, :], xT[:, n, :]).then_inc(s_out, 16)
            sp.wait_ge(s_out, 16 * KT)

        @block.gpsimd
        def _(pool):
            def low(slot, ready):
                pool.wait_ge(s_whi, ready)
                nc.gpsimd.tensor_tensor(w_lo[:, slot], stage_w[:, slot // 2, slot % 2],
                                        w_hi[:, slot].bitcast(F32), ALU.subtract).then_inc(s_wlo, 1)

            whole = LOADED // RING
            with pool.Fori(0, whole) as c:
                for j in range(RING):
                    low(j, c * RING + (j + 1))
            for j in range(LOADED - whole * RING):
                low(j, whole * RING + j + 1)

        @block.tensor
        def _(pe):
            mm = nc.tensor.matmul
            passes = ((0, 0), (0, 1), (1, 0))

            def bank(group, b):
                return ps[4 * (group % 2) + b]

            def wait_weights(n, i=None, d=0):
                pe.wait_ge(s_wlo, n + 1 if i is None else i * d + (n + 1))

            def group_mm(s, g, k, slot, part, first, last):
                w = (w_hi, w_lo)
                h = (hid_hi, hid_lo) if s.mem else (h_hi, h_lo)
                ins = None
                for b in range(g.blocks):
                    out = bank(g.grp, b)
                    for n, (a, m) in enumerate(passes):
                        st, en = first and n == 0, last and n == 2
                        if g.form == "T":
                            ins = mm(out[:, :], w[a][:, slot, part * 256 + b * P:part * 256 + b * P + P],
                                     h[m][:, k, :], start=st, stop=en)
                        else:
                            ins = mm(out[:, 0:g.width], h[a][:, k, b * P:(b + 1) * P],
                                     w[m][:, slot, part * 256:part * 256 + g.width], start=st, stop=en)
                return ins

            def stat_mm(s, to):
                ins = None
                for b in range(2 if s.mem else TB):
                    ins = mm(to[:, b:b + 1], ssum[:, b * P:(b + 1) * P], mean_w[:, 0:1], start=True, stop=True)
                ins.then_inc(s_stat, 1)

            def bc_mm(to):
                for b in range(TB):
                    ins = mm(to[:, b * P:(b + 1) * P], mean_w, rms_bc[:, b * P:(b + 1) * P],
                             start=True, stop=True)
                ins.then_inc(s_bc, 1)

            def transposes(g):
                pe.wait_ge(s_t, g.t0 + 1)
                pe.wait_ge(s_free, g.free0 + g.blocks)
                for c in range(len(g.qk)):
                    for b in range(g.blocks):
                        ins = nc.tensor.transpose(bank(g.grp, c)[:, b * P:(b + 1) * P],
                                                  tn[:, g.grp % 2, b, c * P:(c + 1) * P], ident)
                ins.then_inc(s_tr, 1)

            def proj(s):
                A = s.at
                other = s.groups[0].grp + 1
                if A["tra"]:
                    pe.wait_ge(s_tra, A["tra"])
                if A["trv"]:
                    pe.wait_ge(s_trv, A["trv"])
                for gi, g in enumerate(s.groups):
                    prev = s.groups[gi - 1] if gi else None
                    before = s.groups[gi - 2] if gi > 1 else None
                    if g.free0:
                        pe.wait_ge(s_free, g.free0 - (prev.blocks if prev else 0))
                    if gi == 1:
                        pe.wait_ge(s_rn, A["stat"] + 1)
                        if s.rbc:
                            pe.wait_ge(s_rbc, A["bc"] + 1)
                        if s.forget:
                            pe.wait_ge(s_fabs, 1)
                    if before and before.heads:
                        pe.wait_ge(s_tra, before.tra0 + (len(before.qk) + 1) // 2)
                        if len(before.qk) > 1:
                            pe.wait_ge(s_trv, before.trv0 + len(before.qk) // 2)
                    parts = TILE // g.width
                    for j in range(g.slots):
                        wait_weights(g.tile0 + j)
                        for part in range(parts):
                            k = j * parts + part
                            if gi == 0:
                                pe.wait_ge(s_hlo, A["hin"] + k + 1)
                            ins = group_mm(s, g, k, (g.tile0 + j) % RING, part, k == 0, k == KT - 1)
                        ins.then_inc(s_used, 1)
                        if gi == 0 and j == g.slots // 2 - 1:
                            pe.wait_ge(s_sqc, A["sq"] + 8)
                            stat_mm(s, bank(other, 0))
                        if prev and prev.heads and j == g.slots * 3 // 4 - 1:
                            transposes(prev)
                        if s.forget and gi == 5 and j == 5:
                            pe.wait_ge(s_flog, 1)
                            pe.wait_ge(s_free, g.free0)
                            for b in range(TB):
                                cm = mm(bank(g.grp + 1, 0)[0:16, b * P:SEQ], fl[:, b * 16:(b + 1) * 16],
                                        cst[:, C_TRI:C_TRI + SEQ - b * P], start=b == 0, stop=b == TB - 1)
                            cm.then_inc(s_cmm, 1)
                    if gi == 0 and s.rbc:
                        pe.wait_ge(s_diag, A["bc"] + 1)
                        bc_mm(bank(other, 1))
                    if gi == 0 and s.forget:
                        for b in range(TB):
                            for k in range(KT):
                                for n, (a, m) in enumerate(passes):
                                    fm = mm(bank(other, 2)[:, b * 16:(b + 1) * 16],
                                            (h_hi, h_lo)[a][:, k, b * P:(b + 1) * P],
                                            (wf_hi, wf_lo)[m][:, k * 16:(k + 1) * 16],
                                            start=k == 0 and n == 0, stop=k == KT - 1 and n == 2)
                        fm.then_inc(s_fmm, 1)
                g = s.groups[-1]
                if g.heads:
                    transposes(g)

            def attention(s):
                units = s.units
                pe.wait_ge(s_free, s.at["free"])
                pe.wait_ge(s_tra, s.at["tra"])
                pe.wait_ge(s_trv, s.at["trv"])
                if units[0].forget is not None:
                    pe.wait_ge(s_clo, 1)

                def scores(u):
                    for n, (q, k) in enumerate(zip(u.qs, u.ks)):
                        sm = u.sm + n
                        out = ps[sm % 4]
                        if sm >= 4 and sm - 4 >= s.at["sm"]:
                            pe.wait_ge(s_prob, sm - 4 + 1)
                        more = u.mask is not None or u.forget is not None
                        ins = mm(out[:, 0:u.n], q, k, start=True, stop=not more)
                        if u.forget is not None:
                            sel = ident_r[0:16, u.forget:u.forget + 1].to_broadcast([16, P])
                            for c in (c_hi, c_lo):
                                ins = mm(out[:, 0:u.n], sel, c[:, 0:u.n], start=False, stop=False)
                        if u.mask is not None:
                            ins = mm(out[:, u.n - P:u.n], ident_b[:], u.mask[:], start=False, stop=True)
                        ins.then_inc(s_score, 1)

                def turn(u):
                    pe.wait_ge(s_pc, u.i + 1)
                    if u.i >= 2 and u.i - 2 >= s.at["unit"]:
                        v = units[u.i - 2 - s.at["unit"]]
                        pe.wait_ge(s_pta if v.even else s_ptv, v.copy + 1)
                    for j in range(len(u.vs)):
                        ins = nc.tensor.transpose(ps[4 + u.i % 2][:, j * P:(j + 1) * P],
                                                  prob[:, u.sm % 4, j * P:(j + 1) * P], ident)
                    ins.then_inc(s_pt, 1)

                def values(u):
                    pe.wait_ge(s_pta if u.even else s_ptv, u.copy + 1)
                    if u.i - 2 >= s.at["unit"]:
                        pe.wait_ge(s_o, u.i - 1)
                    w = u.vs[0].shape[-1]
                    for j, v in enumerate(u.vs):
                        ins = mm(ps[6 + u.i % 2][:, 0:w], probT[:, u.i % 2, j * P:(j + 1) * P], v,
                                 start=j == 0, stop=j == len(u.vs) - 1)
                    ins.then_inc(s_pv, 1)

                for n in range(len(units) + 3):
                    if n < len(units):
                        scores(units[n])
                    if 0 <= n - 2 < len(units):
                        turn(units[n - 2])
                    if 0 <= n - 3 < len(units):
                        values(units[n - 3])

            def out_proj(s):
                A = s.at
                g0 = A["group"]
                y_wait(pe, s)
                for n, (kind, c, _) in enumerate([x for x in s.src if x[0] == "y"]):
                    if n >= 4:
                        pe.wait_ge(s_hlo, A["hin"] + c - 4 + 1)
                    for b in range(TB):
                        ins = nc.tensor.transpose(bank(g0 + 1, c % 4)[:, b * P:(b + 1) * P],
                                                  yN[:, b, c * P:(c + 1) * P], ident)
                    ins.then_inc(s_tr, 1)
                for gi in range(2):
                    for j in range(KT):
                        n = A["tile"] + gi * 8 + j
                        wait_weights(n)
                        pe.wait_ge(s_hlo, A["hin"] + (j + 1 if gi == 0 else 8))
                        for b in range(4):
                            for m, (a, c) in enumerate(passes):
                                ins = mm(bank(g0 + gi, b)[:, :], (w_hi, w_lo)[a][:, n % RING, b * P:(b + 1) * P],
                                         (h_hi, h_lo)[c][:, j, :], start=j == 0 and m == 0,
                                         stop=j == KT - 1 and m == 2)
                        ins.then_inc(s_used, 1)

            def mlp(s):
                A = s.at
                g0 = A["group"]
                with pe.Fori(0, HALVES) as i:
                    for gi in range(MLP_GROUPS):
                        up = gi < 4
                        base = 8 * gi if up else 32 + 16 * (gi - 4)
                        for j in range(8 if up else 16):
                            t = base + j
                            n = A["tile"] + t
                            pe.wait_ge(s_wlo, i * MLP_TILES + (n + 1))
                            if gi == 0:
                                pe.wait_ge(s_hlo, A["hin"] + j + 1)
                            if gi == 4:
                                pe.wait_ge(s_hid, i * HID + (A["hid"] + j + 1))
                            src = (h_hi, h_lo) if up else (hid_hi, hid_lo)
                            for b in range(4):
                                if j == 0:
                                    pe.wait_ge(s_free, i * 24 + (A["free"] + 4 * gi - 8 + b + 1))
                                    if gi == 1 and b == 0:
                                        pe.wait_ge(s_rbc, i * 1 + (A["bc"] + 1))
                                for m, (a, c) in enumerate(passes):
                                    ins = mm(bank(g0 + gi, b)[:, :], (w_hi, w_lo)[a][:, n % RING, b * P:(b + 1) * P],
                                             src[c][:, j, :], start=j == 0 and m == 0,
                                             stop=j == (7 if up else 15) and m == 2)
                            ins.then_inc(s_used, 1)
                            if gi == 0 and j == 3:
                                pe.wait_ge(s_sqc, A["sq"] + 8)
                                pe.wait_ge(s_free, i * 24 + A["free"])
                                stat_mm(s, bank(g0 + 1, 0))
                            if gi == 0 and j == 7:
                                pe.wait_ge(s_diag, i * 1 + (A["bc"] + 1))
                                bc_mm(bank(g0 + 1, 1))

            pe.wait_ge(s_in[0], 16)
            pe.wait_ge(s_set, 1)
            for s in stages:
                {"proj": proj, "attn": attention, "out": out_proj, "mlp": mlp}[s.kind](s)

        def source(s):
            return (kT, MEM) if s.mem else (xT, SEQ)

        def hi_lo(s):
            return (hid_hi, hid_lo) if s.mem else (h_hi, h_lo)

        @block.scalar
        def _(act):
            order = Order(act, s_act)
            do, sync = order.do, order.sync
            act.dma_start(kT[:, :, 0:MEM], mem_t.rearrange("(k p) n -> p k n", p=P)).then_inc(s_in[2], 16)
            act.dma_start(cst[:], consts_d).then_inc(s_in[0], 16)
            act.dma_start(xT[:], x_t.rearrange("(k p) n -> p k n", p=P)).then_inc(s_in[3], 16)
            split = [0]

            def split_to(limit, i=None):
                while split[0] < limit:
                    n = split[0]
                    loads, used = 16 * (n // RING + 1), n - RING + 1
                    slot = s_load[n // 2 % PAIRS]
                    if i is None:
                        act.wait_ge(slot, loads)
                        if used > 0:
                            act.wait_ge(s_used, used)
                    else:
                        act.wait_ge(slot, i * (16 * MLP_TILES // RING) + loads)
                        act.wait_ge(s_used, i * MLP_TILES + used)
                    do(nc.scalar.activation(w_hi[:, n % RING], stage_w[:, n // 2 % PAIRS, n % 2], ACT.Copy), s_whi)
                    split[0] += 1

            def square(q, src, scale=1.0):
                if q >= 2:
                    act.wait_ge(s_sqc, q - 1)
                do(nc.scalar.activation(sqb[:, q % 2, 0:src.shape[-1]], src, ACT.Square, scale=scale), s_sq)

            def norm_input(s):
                A = s.at
                x, m = source(s)
                g = V_GAIN[s.norm]
                act.wait_ge(s_in[2] if s.mem else s_in[3], 16)
                if A["free"]:
                    act.wait_ge(s_free, A["free"])
                if A["tile"]:
                    act.wait_ge(s_used, A["tile"])
                for j in range(KT):
                    do(nc.scalar.activation(hi_lo(s)[0][:, j, 0:m], x[:, j, 0:m], ACT.Copy,
                                            scale=vec[:, g + j:g + j + 1]), s_hhi)
                    square(A["sq"] + j, x[:, j, 0:m])

            def take_root(v, w, i=None):
                act.wait_ge(s_var, v + 1 if i is None else i * 1 + (v + 1))
                do(nc.scalar.activation(root[:, 0:w], var[:, 0:w], ACT.Sqrt), s_root)

            def proj(s):
                A = s.at
                split_to(A["tile"] + RING)
                norm_input(s)
                g0 = s.groups[0]
                split_to(g0.tile0 + g0.slots // 2 + RING)
                take_root(A["var"], 2 if s.mem else TB)
                if s.forget:
                    split_to(g0.end + RING)
                    act.wait_ge(s_fabs, 1)
                    do(nc.scalar.activation(fe[:], fa[:], ACT.Exp, scale=-1.0))
                    sync()
                    do(nc.scalar.activation(fl[:], fe[:], ACT.Ln, bias=1.0), s_fln)
                for gi, g in enumerate(s.groups):
                    split_to(g.end + RING)
                    if not g.heads:
                        continue
                    act.wait_ge(s_used, g.end)
                    act.wait_ge(s_rn, A["stat"] + 1)
                    for b in range(g.blocks):
                        square(g.sq0 + b, ps[4 * (g.grp % 2) + b][:, 0:HD * g.heads], rn[:, b:b + 1])
                    take_root(g.var, g.heads * g.blocks)
                    if gi + 1 < len(s.groups):
                        nxt = s.groups[gi + 1]
                        split_to(nxt.tile0 + nxt.slots * 3 // 4 + RING)
                    for c in range(0, len(g.qk), 2):
                        act.wait_ge(s_tr, g.tr0 + 1)
                        do(nc.scalar.activation(g.qk[c], ps[4 * (g.grp % 2) + c][:, 0:P * g.blocks], ACT.Copy,
                                                scale=g.scale), s_tra)
                if s.forget:
                    act.wait_ge(s_cmm, 1)
                    do(nc.scalar.activation(c_hi[:], ps[4 * ((s.groups[5].grp + 1) % 2)][0:16, :], ACT.Copy), s_chi)

            def attention(s):
                units = s.units
                split_to(s.at["tile"] + RING)

                def exps(u):
                    for m in range(len(u.qs)):
                        sm = u.sm + m
                        act.wait_ge(s_max, sm + 1)
                        if sm - 4 in s.unit_of and u.bias is None:
                            act.wait_ge(s_pt, s.unit_of[sm - 4] + 1)
                        if u.sink is not None:
                            do(nc.scalar.activation(esink[:, sm % 8:sm % 8 + 1], nsink[:, u.sink:u.sink + 1],
                                                    ACT.Exp, scale=-1.0, bias=mneg[:, sm % 8:sm % 8 + 1]))
                        dst = prob[:, sm % 4, 0:u.n]
                        src = dst if u.bias is not None else ps[sm % 4][:, 0:u.n]
                        do(nc.scalar.activation(dst, src, ACT.Exp, scale=-1.0, bias=mneg[:, sm % 8:sm % 8 + 1],
                                                accum_out=den[:, sm % 8:sm % 8 + 1]), s_prob)

                def copy(u):
                    act.wait_ge(s_pt, u.i + 1)
                    if u.i - 2 >= s.at["unit"]:
                        act.wait_ge(s_pv, u.i - 1)
                    do(nc.scalar.activation(probT[:, 0, 0:u.n], ps[4][:, 0:u.n], ACT.Copy), s_pta)

                for n in range(len(units) + 2):
                    if n < len(units):
                        exps(units[n])
                    if 0 <= n - 2 and units[n - 2].even:
                        copy(units[n - 2])
                if s.diff:
                    act.wait_ge(s_o, units[-1].i + 1)
                    for b in range(TB):
                        for half in range(2):
                            square(s.at["sq"] + 2 * b + half, yN[:, b, 384 * half:384 * half + 384])
                    take_root(s.at["var"], 24)

            def out_proj(s):
                A = s.at
                split_to(A["tile"] + RING)
                y_wait(act, s)
                n = 0
                for kind, c, gain in s.src:
                    if kind == "y":
                        act.wait_ge(s_tr, A["tr"] + n + 1)
                        n += 1
                        src = ps[4 * ((A["group"] + 1) % 2) + c % 4][:, :]
                    else:
                        src = qT[:, c, :]
                    do(nc.scalar.activation(h_hi[:, c, :], src, ACT.Copy,
                                            scale=1.0 if gain is None else gain), s_hhi)
                split_to(A["tile"] + 16)

            def mlp(s):
                A = s.at
                split_to(A["tile"] + RING)
                norm_input(s)
                with act.Fori(0, HALVES) as i:
                    order.enter(i, [(s_whi, MLP_TILES), (s_root, 1), (s_hsq, HID), (s_hidhi, HID)])
                    t0 = A["tile"]
                    split_to(t0 + 4 + RING, i)
                    take_root(A["var"], TB, i)
                    for u in range(4):
                        split_to(t0 + 8 * (u + 1) + RING, i)
                        for b in range(4):
                            t = 4 * u + b
                            act.wait_ge(s_free, i * 24 + (A["free"] + t + 1))
                            if t >= 2:
                                act.wait_ge(s_hid, i * HID + (A["hid"] + t - 1))
                            do(nc.scalar.activation(hsq[:, t % 2], relu[:, t % 2], ACT.Square), s_hsq)
                            sync()
                            do(nc.scalar.activation(hid_hi[:, t], hsq[:, t % 2], ACT.Copy), s_hidhi)
                    split_to(t0 + MLP_TILES + RING, i)
                    order.leave()
                split[0] += (HALVES - 1) * MLP_TILES

            act.wait_ge(s_in[1], 16)
            for s in stages:
                if s.forget:
                    act.wait_ge(s_in[4], 16)
                    do(nc.scalar.activation(wf_hi[:], wf_in[:], ACT.Copy), s_seta)
                {"proj": proj, "attn": attention, "out": out_proj, "mlp": mlp}[s.kind](s)
                if s is stages[0]:
                    act.wait_ge(s_set, 2)
                    do(nc.scalar.activation(lam[:, 2:4], lam[:, 0:2], ACT.Exp), s_seta)

        @block.vector
        def _(dve):
            order = Order(dve, s_dve)
            do, sync = order.do, order.sync
            vt, vs, stt, tt = (nc.vector.tensor_tensor, nc.vector.tensor_scalar,
                               nc.vector.scalar_tensor_tensor, nc.vector.tensor_tensor)

            def norm_input(s):
                A = s.at
                x, m = source(s)
                hi, lo = hi_lo(s)
                g = V_GAIN[s.norm]
                for j in range(KT):
                    dve.wait_ge(s_hhi, A["hin"] + j + 1)
                    do(stt(lo[:, j, 0:m], x[:, j, 0:m], vec[:, g + j:g + j + 1], hi[:, j, 0:m].bitcast(F32),
                           ALU.mult, ALU.subtract), s_hlo)
                    q = A["sq"] + j
                    dve.wait_ge(s_sq, q + 1)
                    if j == 0:
                        do(nc.vector.tensor_copy(ssum[:, 0:m], sqb[:, q % 2, 0:m]), s_sqc)
                    else:
                        sync()
                        do(tt(ssum[:, 0:m], ssum[:, 0:m], sqb[:, q % 2, 0:m], ALU.add), s_sqc)

            def rsqrt(out, v, w, signal=None, i=None):
                dve.wait_ge(s_root, v + 1 if i is None else i * 1 + (v + 1))
                do(nc.vector.reciprocal(inv[:, 0:w], root[:, 0:w]))
                sync()
                do(tt(newt[:, 0:w], inv[:, 0:w], inv[:, 0:w], ALU.mult))
                sync()
                do(tt(newt[:, 0:w], newt[:, 0:w], var[:, 0:w], ALU.mult))
                sync()
                do(vs(newt[:, 0:w], newt[:, 0:w], -0.5, 1.5, ALU.mult, ALU.add))
                sync()
                do(tt(out, inv[:, 0:w], newt[:, 0:w], ALU.mult), signal)
                sync()

            def token_norm(s, other, i=None):
                A = s.at
                nb = 2 if s.mem else TB
                dve.wait_ge(s_stat, A["stat"] + 1 if i is None else i * 1 + (A["stat"] + 1))
                do(vs(var[:, 0:nb], ps[4 * (other % 2)][:, 0:nb], EPS, None, ALU.add), s_var)
                rsqrt(rn[:, 0:nb], A["var"], nb, s_rn, i)
                if s.rbc or s.kind == "mlp":
                    for b in range(TB):
                        do(vs(rms_bc[:, b * P:(b + 1) * P], ident, rn[:, b:b + 1], float(D), ALU.mult, ALU.mult),
                           s_diag if b == TB - 1 else None)
                    dve.wait_ge(s_bc, A["bc"] + 1 if i is None else i * 1 + (A["bc"] + 1))
                    do(nc.vector.tensor_copy(rms_bc[:], ps[4 * (other % 2) + 1][:, :]), s_rbc)
                    sync()

            def forget_gates(s):
                bank = ps[4 * ((s.groups[0].grp + 1) % 2) + 2]
                dve.wait_ge(s_fmm, 1)
                for b in range(TB):
                    do(stt(fz[:, 16 * b:16 * b + 16], bank[:, 16 * b:16 * b + 16], rn[:, b:b + 1],
                           vec[:, V_FORGET:V_FORGET + 16], ALU.mult, ALU.add))
                sync()
                do(stt(fa[:], fz[:], -1.0, fz[:], ALU.mult, ALU.max), s_fabs)
                dve.wait_ge(s_fln, 1)
                do(stt(fa[:], fz[:], 0.0, fl[:], ALU.min, ALU.subtract))
                sync()
                do(nc.vector.tensor_copy(fl[:], fa[:]), s_flog)

            def heads(s, g):
                nb, nh, par = g.blocks, g.heads, g.grp % 2
                w = nb * nh
                for b in range(nb):
                    q = g.sq0 + b
                    dve.wait_ge(s_sq, q + 1)
                    do(nc.vector.tensor_reduce(hsum[:, b * nh:(b + 1) * nh],
                                               sqb[:, q % 2, 0:nh * HD].rearrange("p (h d) -> p h d", d=HD),
                                               axis=AX.X, op=ALU.add), s_sqc)
                sync()
                do(vs(var[:, 0:w], hsum[:, 0:w], 1.0 / HD, EPS, ALU.mult, ALU.add), s_var)
                rsqrt(hsum[:, 0:w], g.var, w)
                do(tt(newt[:, 0:w].rearrange("p (b h) -> p b h", b=nb), hsum[:, 0:w].rearrange("p (b h) -> p b h", b=nb),
                      rn[:, 0:nb].unsqueeze(2).to_broadcast([P, nb, nh]), ALU.mult))
                sync()
                if g.tr0:
                    dve.wait_ge(s_tr, g.tr0)
                for b in range(nb):
                    bank = ps[4 * par + b]
                    do(tt(tn[:, par, b, 0:nh * HD].rearrange("p (h d) -> p h d", d=HD),
                          bank[:, 0:nh * HD].rearrange("p (h d) -> p h d", d=HD),
                          newt[:, b * nh:(b + 1) * nh].unsqueeze(2).to_broadcast([P, nh, HD]), ALU.mult),
                       None if g.v else s_free)
                    if g.v:
                        values(g, b)
                sync()
                for n, (first, count, name) in enumerate(g.gains):
                    t = tn[:, par, 0:nb, first * HD:(first + count) * HD].rearrange("p b (h d) -> p b h d", d=HD)
                    gain = vec[:, V_HEAD[name]:V_HEAD[name] + HD]
                    gain = gain.unsqueeze(1).unsqueeze(1).to_broadcast([P, nb, count, HD])
                    last = n == len(g.gains) - 1 and not g.rope
                    do(tt(t, t, gain, ALU.mult), s_t if last else None)
                if g.rope:
                    rope(g)

            def rope(g):
                sync()
                nr = g.rope
                t = tn[:, g.grp % 2, 0:TB, 0:nr * HD].rearrange("p b (h d) -> p b h d", d=HD)
                a, b = t[:, :, :, 0:8], t[:, :, :, 8:16]
                cos, sin = (cst[:, c:c + 32].rearrange("p (b d) -> p b d", b=TB).unsqueeze(2)
                            .to_broadcast([P, TB, nr, 8]) for c in (C_COS, C_SIN))
                m = [vN[:, k, 768:768 + 32 * nr].rearrange("p (b h d) -> p b h d", b=TB, h=nr) for k in range(4)]
                do(tt(m[0], a, cos, ALU.mult))
                do(tt(m[1], b, sin, ALU.mult))
                do(tt(m[2], a, sin, ALU.mult))
                do(tt(m[3], b, cos, ALU.mult))
                sync()
                do(tt(a, m[0], m[1], ALU.subtract))
                do(tt(b, m[2], m[3], ALU.add), s_t)

            def values(g, b):
                q = g.heads * HD
                do(vs(g.v(b, g.width - q), ps[4 * (g.grp % 2) + b][:, q:g.width], rn[:, b:b + 1], None, ALU.mult),
                   s_free)

            def features(g):
                for n, (kind, j) in enumerate(g.t):
                    bank = ps[4 * (g.grp % 2) + n]
                    if kind == "c":
                        do(tt(kT[:, j, :], bank[:, :], rms_bc[:], ALU.mult), s_free)
                        continue
                    tmp = relu[:, 0]
                    do(tt(tmp, bank[:, :], rms_bc[:], ALU.mult), s_free)
                    sync()
                    z = qT[:, j, :]
                    if kind == "b":
                        do(tt(z, z, tmp, ALU.mult))
                        sync()
                        continue
                    do(tt(uP[:, j, 2:514], tmp, kT[:, j, :], ALU.mult))
                    sync()
                    w = [vec[:, V_CONV + 6 * k + j:V_CONV + 6 * k + j + 1] for k in range(3)]
                    do(vs(z, uP[:, j, 0:512], w[0], None, ALU.mult))
                    sync()
                    for k in (1, 2):
                        do(stt(z, uP[:, j, k:k + 512], w[k], z, ALU.mult, ALU.add))
                        sync()

            def proj(s):
                A = s.at
                norm_input(s)
                token_norm(s, s.groups[0].grp + 1)
                if s.forget:
                    forget_gates(s)
                if s.rbc:
                    do(nc.vector.memset(uP[:, :, 0:2], 0.0))
                    sync()
                for g in s.groups:
                    dve.wait_ge(s_used, g.end)
                    if g.form == "T":
                        features(g)
                    elif g.heads:
                        heads(s, g)
                        for c in range(1, len(g.qk), 2):
                            dve.wait_ge(s_tr, g.tr0 + 1)
                            do(vs(g.qk[c], ps[4 * (g.grp % 2) + c][:, 0:P * g.blocks], g.scale, None, ALU.mult), s_trv)
                    else:
                        for b in range(g.blocks):
                            values(g, b)
                if s.forget:
                    dve.wait_ge(s_chi, 1)
                    do(tt(c_lo[:], ps[4 * ((s.groups[5].grp + 1) % 2)][0:16, :], c_hi[:].bitcast(F32),
                          ALU.subtract), s_clo)

            def attention(s):
                units = s.units
                dve.wait_ge(s_used, s.at["tile"])
                dve.wait_ge(s_tr, s.at["tr"])

                def row_min(u):
                    if u.bias is not None and u.head[2]:
                        h, slope, _ = u.head
                        w = u.bias[1]
                        log = C_LOGW if u.bias[2] == "dilated" else C_WIN
                        sync()
                        do(stt(bias_t[:, h % 2, 0:w], cst[:, C_DELTA + 512 - w:C_DELTA + 512], slope,
                               cst[:, log:log + w], ALU.mult, ALU.add))
                        sync()
                    for m in range(len(u.qs)):
                        sm = u.sm + m
                        low = mneg[:, sm % 8:sm % 8 + 1]
                        dve.wait_ge(s_score, sm + 1)
                        if u.bias is None:
                            do(nc.vector.tensor_reduce(low, ps[sm % 4][:, 0:u.n], axis=AX.X, op=ALU.min), s_max)
                            continue
                        if sm - 4 in s.unit_of:
                            dve.wait_ge(s_pt, s.unit_of[sm - 4] + 1)
                        do(nc.vector.tensor_tensor_reduce(
                            out=prob[:, sm % 4, 0:u.n], in0=ps[sm % 4][:, 0:u.n],
                            in1=bias_t[:, u.head[0] % 2, u.bias[0]:u.bias[0] + u.n], scale=1.0, scalar=3e38,
                            op0=ALU.add, op1=ALU.min, accum_out=low), None if u.sink is not None else s_max)
                        if u.sink is not None:
                            sync()
                            do(tt(low, low, nsink[:, u.sink:u.sink + 1], ALU.min), s_max)

                def denominators(u):
                    dve.wait_ge(s_prob, u.sm + len(u.qs))
                    r = rden[:, u.i % 8:u.i % 8 + 1]
                    d = den[:, u.sm % 8:u.sm % 8 + 1]
                    if u.sink is not None:
                        do(tt(d, d, esink[:, u.sm % 8:u.sm % 8 + 1], ALU.add))
                        sync()
                    if len(u.qs) == 1:
                        do(nc.vector.reciprocal(r, d), s_pc)
                        return
                    r2 = esink[:, u.i % 8:u.i % 8 + 1]
                    do(nc.vector.reciprocal(r, d))
                    do(nc.vector.reciprocal(r2, den[:, (u.sm + 1) % 8:(u.sm + 1) % 8 + 1]))
                    sync()
                    do(tt(r2, r2, lam[:, 4:5], ALU.mult))
                    p1, p2 = (prob[:, (u.sm + m) % 4, 0:u.n] for m in range(2))
                    do(vs(p1, p1, r, None, ALU.mult))
                    sync()
                    do(stt(p1, p2, r2, p1, ALU.mult, ALU.add), s_pc)

                def copy(u):
                    dve.wait_ge(s_pt, u.i + 1)
                    if u.i - 2 >= s.at["unit"]:
                        dve.wait_ge(s_pv, u.i - 1)
                    do(nc.vector.tensor_copy(probT[:, 1, 0:u.n], ps[5][:, 0:u.n]), s_ptv)

                def output(u):
                    dve.wait_ge(s_pv, u.i + 1)
                    src = ps[6 + u.i % 2][:, 0:u.vs[0].shape[-1]]
                    if len(u.qs) == 1:
                        do(vs(u.y, src, rden[:, u.i % 8:u.i % 8 + 1], None, ALU.mult), s_o)
                    else:
                        do(nc.vector.tensor_copy(u.y, src), s_o)

                for n in range(len(units) + 3):
                    if n < len(units):
                        row_min(units[n])
                    if 0 <= n - 1 < len(units):
                        denominators(units[n - 1])
                    if 0 <= n - 2 < len(units) and not units[n - 2].even:
                        copy(units[n - 2])
                    if 0 <= n - 3 < len(units):
                        output(units[n - 3])
                if s.diff:
                    for n in range(8):
                        q = s.at["sq"] + n
                        dve.wait_ge(s_sq, q + 1)
                        do(nc.vector.tensor_reduce(hsum[:, 3 * n:3 * n + 3],
                                                   sqb[:, q % 2, 0:384].rearrange("p (h d) -> p h d", d=P),
                                                   axis=AX.X, op=ALU.add), s_sqc)
                    sync()
                    do(vs(var[:, 0:24], hsum[:, 0:24], 1.0 / P, SUBLN_EPS, ALU.mult, ALU.add), s_var)
                    rsqrt(hsum[:, 0:24], s.at["var"], 24)
                    do(vs(newt[:, 0:24], hsum[:, 0:24], 1.0 - LAM_INIT, None, ALU.mult))
                    sync()
                    for b in range(TB):
                        y = yN[:, b, 0:768].rearrange("p (h d) -> p h d", d=P)
                        do(tt(y, y, newt[:, 6 * b:6 * b + 6].unsqueeze(2).to_broadcast([P, 6, P]), ALU.mult),
                           s_y if b == TB - 1 else None)

            def out_proj(s):
                A = s.at
                for kind, c, gain in s.src:
                    dve.wait_ge(s_hhi, A["hin"] + c + 1)
                    src = ps[4 * ((A["group"] + 1) % 2) + c % 4][:, :] if kind == "y" else qT[:, c, :]
                    hi = h_hi[:, c, :].bitcast(F32)
                    if gain is None:
                        do(tt(h_lo[:, c, :], src, hi, ALU.subtract), s_hlo)
                    else:
                        do(stt(h_lo[:, c, :], src, gain, hi, ALU.mult, ALU.subtract), s_hlo)
                for gi in range(2):
                    dve.wait_ge(s_used, A["tile"] + 8 * (gi + 1))
                    for b in range(4):
                        x = xT[:, 4 * gi + b, :]
                        do(tt(x, x, ps[4 * ((A["group"] + gi) % 2) + b][:, :], ALU.add), s_free)
                sync()

            def mlp(s):
                A = s.at
                norm_input(s)
                sync()
                with dve.Fori(0, HALVES) as i:
                    order.enter(i, [(s_free, 24), (s_var, 1), (s_rn, 1), (s_diag, 1), (s_rbc, 1), (s_hid, HID),
                                    (s_dve, DVE_STEPS_A_TURN)])
                    token_norm(s, A["group"] + 1, i)

                    def low(t):
                        dve.wait_ge(s_hidhi, i * HID + (A["hid"] + t + 1))
                        do(tt(hid_lo[:, t], hsq[:, t % 2], hid_hi[:, t].bitcast(F32), ALU.subtract), s_hid)

                    for u in range(4):
                        dve.wait_ge(s_used, i * MLP_TILES + (A["tile"] + 8 * (u + 1)))
                        for b in range(4):
                            t = 4 * u + b
                            if t >= 2:
                                dve.wait_ge(s_hsq, i * HID + (A["hid"] + t - 1))
                            do(stt(relu[:, t % 2], ps[4 * ((A["group"] + u) % 2) + b][:, :], 0.0, rms_bc[:],
                                   ALU.max, ALU.mult), s_free)
                            if t:
                                low(t - 1)
                    low(HID - 1)
                    for n in range(2):
                        dve.wait_ge(s_used, i * MLP_TILES + (A["tile"] + 32 + 16 * (n + 1)))
                        for b in range(4):
                            x = xT[:, 4 * n + b, :]
                            do(tt(x, x, ps[4 * ((A["group"] + n) % 2) + b][:, :], ALU.add), s_free)
                    sync()
                    order.leave()

            dve.wait_ge(s_in[0], 16)
            dve.wait_ge(s_in[1], 16)
            do(nc.vector.tensor_copy(ident_b[:], ident))
            do(nc.vector.tensor_copy(causal_b[:], cst[:, C_CAUSAL:C_CAUSAL + P]))
            do(nc.vector.tensor_copy(chunk_b[:], cst[:, C_CHUNK:C_CHUNK + P]))
            do(nc.vector.tensor_copy(ident_r[:], cst[:, 0:16]))
            do(vs(nsink[:], vec[:, V_SINK:V_SINK + 8], -1.0, None, ALU.mult), s_set)
            for n in range(2):
                a = V_LAM + 128 * n
                do(tt(fz[:, 0:64], vec[:, a:a + 64], vec[:, a + 64:a + 128], ALU.mult))
                sync()
                do(nc.vector.tensor_reduce(lam[:, n:n + 1], fz[:, 0:64], axis=AX.X, op=ALU.add), s_set if n else None)
                sync()
            for s in stages:
                if s.forget:
                    dve.wait_ge(s_seta, 2)
                    do(tt(wf_lo[:], wf_in[:], wf_hi[:].bitcast(F32), ALU.subtract))
                {"proj": proj, "attn": attention, "out": out_proj, "mlp": mlp}[s.kind](s)
                if s is stages[0]:
                    dve.wait_ge(s_seta, 1)
                    do(tt(lam[:, 5:6], lam[:, 3:4], lam[:, 2:3], ALU.subtract))
                    sync()
                    do(vs(lam[:, 4:5], lam[:, 5:6], -LAM_INIT, None, ALU.add))



def square_tiles(w, cols=None):
    out = []
    n = 0
    while n < w.shape[1]:
        width = TILE if (cols is None or cols[0] == TILE) else 256
        if cols is not None:
            cols = cols[1:]
        part = w[:, n:n + width]
        if width == TILE:
            out.append(part.reshape(-1, P, TILE))
        else:
            out.append(part.reshape(-1, 2, P, 256).transpose(0, 2, 1, 3).reshape(-1, P, TILE))
        n += width
    return out


def weight_stream(a):
    def mem_kv(l):
        return square_tiles(a["w_mem_kv_2"][l])

    def mlp(up, down):
        out = []
        for h in range(HALVES):
            w = FF // HALVES
            out += square_tiles(up[:, h * w:(h + 1) * w]) + square_tiles(down[h * w:(h + 1) * w])
        return out

    e = a["w_in_even"][0]
    aq, ak, av, bq, bk, bv = np.split(e, [512, 1024, 1536, 2048, 2176], axis=1)
    bq = bq.reshape(D, 2, 4, HD).transpose(0, 2, 1, 3).reshape(D, 512)
    o = a["w_in_odd"][0]
    b0 = a["a_w_in_2"][0]
    parts = mem_kv(0) + mem_kv(1)
    parts += square_tiles(np.concatenate([bk, bv], 1), [256]) + square_tiles(np.concatenate([aq, ak, bq, av], 1))
    parts += square_tiles(a["w_out_even"][0]) + mlp(a["w_up"][0], a["w_down"][0])
    parts += square_tiles(o[:, :3072]) + square_tiles(a["w_out_odd"][0]) + mlp(a["w_up"][1], a["w_down"][1])
    gate_b, gate_c, hv, qm = np.split(b0, [768, 1536, 2304], axis=1)
    parts += square_tiles(qm, [256]) + square_tiles(np.concatenate([gate_c, hv, gate_b], 1), [TILE] * 4 + [256])
    parts += square_tiles(a["w_o_2"][0]) + mlp(a["w_up_2"][0], a["w_down_2"][0])
    parts += square_tiles(a["w_kv_2"]) + square_tiles(a["b_w_q_2"][0])
    parts += square_tiles(a["w_o_2"][1]) + mlp(a["w_up_2"][1], a["w_down_2"][1])
    parts.append(parts[-1][:RING])
    w = np.concatenate(parts, 0)
    return np.ascontiguousarray(w.reshape(-1, 2, P, TILE).transpose(0, 2, 1, 3))


def kernel(**inputs):
    import concourse.bacc as _bacc
    from concourse import mybir as _mybir
    from concourse.bass_utils import run_bass_kernel_spmd as _run

    a = {k: np.asarray(v) for k, v in inputs.items()}

    def column(v):
        return v.reshape(-1, P).T

    def across(v):
        return np.broadcast_to(v.reshape(1, -1), (P, v.size))

    vecs = [column(a["g_mix"][0]), column(a["g_mix"][1]), column(a["g_mlp"][0]), column(a["g_mlp"][1]),
            column(a["norm_mix_2"][0]), column(a["norm_mix_2"][1]), column(a["norm_mlp_2"][0]),
            column(a["norm_mlp_2"][1]), column(a["kv_norm_2"]), column(a["mem_norm_2"]),
            column(a["a_conv_2"][0].reshape(-1)), column(a["b_subln_2"][0])]
    vecs += [across(v) for v in (
        a["a_q_gain"], a["a_k_gain"], a["b_q_gain"], a["b_k_gain"], a["c_q_gain"], a["c_k_gain"],
        a["b_q_norm_2"], a["k_norm_2"], a["mem_q_norm_2"][0], a["mem_q_norm_2"][1],
        a["mem_k_norm_2"][0], a["mem_k_norm_2"][1], a["b_sinks"], a["b_forget"], a["b_lam_2"])]
    arrays = {
        "in_weights": weight_stream(a),
        "in_forget": np.ascontiguousarray(
            a["w_in_odd"][0][:, 3072:].reshape(KT, P, 16).transpose(1, 0, 2).reshape(P, -1)),
        "in_x": np.ascontiguousarray(a["x"][0].T),
        "in_mem": np.ascontiguousarray(a["mem_2"][0].T),
        "in_consts": constants(),
        "in_vecs": np.ascontiguousarray(np.concatenate(vecs, 1)),
    }
    nc = _bacc.Bacc("TRN2", target_bir_lowering=False, num_devices=1)
    args = [nc.dram_tensor(n, x.shape, _mybir.dt.from_np(x.dtype), kind="ExternalInput").ap()
            for n, x in arrays.items()]
    out = nc.dram_tensor("out_xT", (D, SEQ), _mybir.dt.float32, kind="ExternalOutput").ap()
    build(nc, *args, out)
    r = _run(nc, [arrays], core_ids=[0])
    y = r.results[0]["out_xT"]
    return np.ascontiguousarray(y.T).reshape(1, SEQ, D)
```

```python
import numpy as np
import concourse.bass as bass
from concourse import mybir
from contextlib import ExitStack

F32 = mybir.dt.float32
F32R = mybir.dt.float32r
BF16 = mybir.dt.bfloat16
ALU = mybir.AluOpType
ACT = mybir.ActivationFunctionType
AX = mybir.AxisListType

P = 128
D = 1024
SEQ = 512
MEM = 256
FF = 4096
KT = D // P
TB = SEQ // P
HD = 64
TILE = 512
EPS = 1e-6
SUBLN_EPS = 1e-5
BIG = 1e30
LAM_INIT = 0.8 - 0.6 * float(np.exp(-0.3 * 1))
RING = 8
PAIRS = 4
HALVES = 2
HID = FF // HALVES // P

C_IDENT, C_MEAN, C_DELTA, C_LOGW, C_WIN, C_TRI, C_CAUSAL, C_CHUNK, C_COS, C_SIN = (
    0, 128, 256, 768, 1280, 1536, 2048, 2176, 2304, 2336)
C_ALL = 2368
V_GAIN = {n: 8 * i for i, n in enumerate(
    ["mix0", "mix1", "mlp0", "mlp1", "mixb0", "mixb1", "mlpb0", "mlpb1", "kv", "mem"])}
V_CONV = 80
V_SUB = 98
V_HEAD = {n: 99 + HD * i for i, n in enumerate(
    ["aq", "ak", "bq", "bk", "cq", "ck", "dq", "dk", "mq0", "mq1", "mk0", "mk1"])}
V_SINK = 99 + 12 * HD
V_FORGET = V_SINK + 8
V_LAM = V_FORGET + 16
V_ALL = V_LAM + 256
DILATIONS = ((128, 1), (512, 4), (2048, 16))


def constants():
    c = np.zeros((P, C_ALL), np.float32)
    p = np.arange(P)[:, None]
    c[:, C_IDENT:C_IDENT + P] = np.eye(P)
    c[:, C_MEAN:C_MEAN + P] = 1.0 / D
    dist = p - np.arange(512)[None] + 384
    c[:, C_DELTA:C_DELTA + 512] = dist
    times = sum(((dist % d == 0) & (dist <= w)).astype(np.float64) for w, d in DILATIONS)
    ok = (dist >= 0) & (times > 0)
    c[:, C_LOGW:C_LOGW + 512] = np.where(ok, -np.log(np.maximum(times, 1)), BIG)
    near = p - np.arange(256)[None] + 128
    c[:, C_WIN:C_WIN + 256] = np.where((near >= 0) & (near < 128), 0.0, BIG)
    c[:, C_TRI:C_TRI + 512] = p <= np.arange(512)[None]
    f = np.arange(P)[None]
    c[:, C_CAUSAL:C_CAUSAL + P] = np.where(f > p, BIG, 0.0)
    c[:, C_CHUNK:C_CHUNK + P] = np.where(f // 64 > p // 64, BIG, 0.0)
    half = 8
    inv = (1.0 / (np.float32(500000.0) ** (np.arange(0, 16, 2, dtype=np.float32) / np.float32(16)))).astype(np.float32)
    ang = (np.arange(SEQ, dtype=np.float32)[:, None] * inv[None]).astype(np.float32)
    for at, fn in ((C_COS, np.cos), (C_SIN, np.sin)):
        c[:, at:at + TB * half] = fn(ang).astype(np.float32).reshape(TB, P, half).transpose(1, 0, 2).reshape(P, -1)
    return c


class Group:

    def __init__(self, form, width=TILE, heads=0, gains=(), rope=0, qk=(), scale=1.0, v=None, t=None):
        self.form = form
        self.width = width
        self.slots = 8 if width == TILE else 4
        self.heads = heads
        self.gains = gains
        self.rope = rope
        self.qk = qk
        self.scale = scale
        self.v = v
        self.t = t


class Stage:
    def __init__(self, kind, **kw):
        self.kind = kind
        self.norm = kw.get("norm")
        self.groups = kw.get("groups", [])
        self.mem = kw.get("mem", False)
        self.rbc = kw.get("rbc", False)
        self.forget = kw.get("forget", False)
        self.heads = kw.get("heads", [])
        self.diff = kw.get("diff", False)
        self.z = kw.get("z", 0)
        self.last = kw.get("last", False)


class Head:

    def __init__(self, qs, ks, keys, v, tile=None, base=0, piece=None,
                 bias=None, slope=0.0, mask=None, sink=None, forget=None):
        self.qs, self.ks = qs, ks
        self.v = v
        self.tile, self.base = tile, base
        self.piece = piece
        self.bias, self.slope, self.mask, self.sink, self.forget = bias, slope, mask, sink, forget
        self.lo = [k[0] for k in keys]
        self.n = [P * (k[1] - k[0]) for k in keys]
        self.at_p = [sum(self.n[:i]) for i in range(TB)]
        last = max(k[1] for k in keys)
        self.queries = [[i for i, k in enumerate(keys) if k[0] <= j < k[1]] for j in range(last)]
        self.at_t = [P * sum(len(q) for q in self.queries[:j]) for j in range(last)]


MLP_TILES = 64
MLP_GROUPS = 6
TURN = dict(tile=MLP_TILES, group=MLP_GROUPS, free=24, stat=1, var=1, hid=HID, bc=1,
            rn=1)


def build(nc, w_all, w_f, x_t, mem_t, consts_d, vecs_d, out_t):
    ctx = ExitStack()
    with ctx:
        def sb(name, shape, dt=F32, where=ctx):
            return where.enter_context(nc.sbuf_tensor(name, shape, dt))

        def sem(name):
            return ctx.enter_context(nc.semaphore(name))

        xT = sb("xT", [P, KT, SEQ])
        stage_w = sb("stage_w", [P, PAIRS, 2, TILE])
        w_hi = sb("w_hi", [P, RING, TILE], F32R)
        w_lo = sb("w_lo", [P, RING, TILE], F32R)
        cst = sb("cst", [P, C_ALL])
        vec = sb("vec", [P, V_ALL])
        mem_kT = sb("mem_kT", [P, 2, 2, MEM])
        mem_v = sb("mem_v", [P, 2, 2, MEM])
        rms_bc = sb("rms_bc", [P, SEQ])
        ssum = sb("ssum", [P, SEQ])
        sqb = sb("sqb", [P, 2, SEQ])
        wf_in = sb("wf_in", [P, P])
        wf_hi = sb("wf_hi", [P, P], F32R)
        wf_lo = sb("wf_lo", [P, P], F32R)
        c_hi = sb("c_hi", [16, SEQ], F32R)
        c_lo = sb("c_lo", [16, SEQ], F32R)
        ident_r = sb("ident_r", [P, 16], F32R)
        ident_b = sb("ident_b", [P, P], BF16)
        causal_b = sb("causal_b", [P, P], BF16)
        chunk_b = sb("chunk_b", [P, P], BF16)
        rn = sb("rn", [P, TB])
        var = sb("var", [P, 32])
        root = sb("root", [P, 32])
        inv = sb("inv", [P, 32])
        newt = sb("newt", [P, 32])
        hsum = sb("hsum", [P, 32])
        fz = sb("fz", [P, 64])
        fa = sb("fa", [P, 64])
        fe = sb("fe", [P, 64])
        fl = sb("fl", [P, 64])
        mneg = sb("mneg", [P, 16])
        den = sb("den", [P, 16])
        rden = sb("rden", [P, 16])
        esink = sb("esink", [P, 16])
        nsink = sb("nsink", [P, 8])
        lam = sb("lam", [P, 8])
        h_hi = sb("h_hi", [P, KT, SEQ], F32R)
        h_lo = sb("h_lo", [P, KT, SEQ], F32R)
        only = ExitStack()
        hid_hi = sb("hid_hi", [P, HID, SEQ], F32R, only)
        hid_lo = sb("hid_lo", [P, HID, SEQ], F32R, only)
        relu = sb("relu", [P, 2, SEQ], F32, only)
        hsq = sb("hsq", [P, 2, SEQ], F32, only)
        only.close()
        arena = sb("arena", [P, 18 * 1024])
        qT = arena[:, 0:4096].rearrange("p (j n) -> p j n", j=KT)
        kT = arena[:, 4096:8192].rearrange("p (j n) -> p j n", j=KT)
        vN = arena[:, 8192:12288].rearrange("p (b n) -> p b n", b=TB)
        vD = arena[:, 8192:11264].rearrange("p (b n) -> p b n", b=TB)
        uP = arena[:, 8192:8192 + 6 * 514].rearrange("p (j n) -> p j n", j=6)
        rope_t = arena[:, 11264:12288].rearrange("p (k n) -> p k n", k=4)
        tn = arena[:, 12288:16384].rearrange("p (a b n) -> p a b n", a=2, b=TB)
        prob = arena[:, 12288:14848].rearrange("p (a n) -> p a n", a=2)
        probT = arena[:, 14848:17408].rearrange("p (a n) -> p a n", a=2)
        bias_t = arena[:, 17408:18432].rearrange("p (a n) -> p a n", a=2)
        pieces = [arena[:, a:a + 1024].rearrange("p (b n) -> p b n", b=TB) for a in (7168, 11264, 17408)]

        ps = [ctx.enter_context(nc.psum_tensor(f"ps{i}", [P, 512], F32)) for i in range(8)]

        ident = cst[:, C_IDENT:C_IDENT + P]
        mean_w = cst[:, C_MEAN:C_MEAN + P]

        s_in = [sem(f"s_in{i}") for i in range(6)]
        s_load = [sem(f"s_load{i}") for i in range(PAIRS)]
        s_whi = sem("s_whi")
        s_wlo = sem("s_wlo")
        s_used = sem("s_used")
        s_free = sem("s_free")
        s_hhi = sem("s_hhi")
        s_hlo = sem("s_hlo")
        s_sq = sem("s_sq")
        s_sqc = sem("s_sqc")
        s_stat = sem("s_stat")
        s_var = sem("s_var")
        s_root = sem("s_root")
        s_rn = sem("s_rn")
        s_diag = sem("s_diag")
        s_bc = sem("s_bc")
        s_rbc = sem("s_rbc")
        s_t = sem("s_t")
        s_tr = sem("s_tr")
        s_tra = sem("s_tra")
        s_trv = sem("s_trv")
        s_score = sem("s_score")
        s_max = sem("s_max")
        s_prob = sem("s_prob")
        s_pn = sem("s_pn")
        s_pt = sem("s_pt")
        s_pta = sem("s_pta")
        s_ptv = sem("s_ptv")
        s_pv = sem("s_pv")
        s_o = sem("s_o")
        s_y = sem("s_y")
        s_hsq = sem("s_hsq")
        s_hidhi = sem("s_hidhi")
        s_hid = sem("s_hid")
        s_wf = sem("s_wf")
        s_fmm = sem("s_fmm")
        s_fabs = sem("s_fabs")
        s_fln = sem("s_fln")
        s_flog = sem("s_flog")
        s_cmm = sem("s_cmm")
        s_z = sem("s_z")
        s_chi = sem("s_chi")
        s_clo = sem("s_clo")
        s_set = sem("s_set")
        s_seta = sem("s_seta")
        s_act = sem("s_act")
        s_dve = sem("s_dve")
        s_out = sem("s_out")

        def tiles(tensor, first, n):
            return [tensor[:, first + j, :] for j in range(n)]

        def v_to(first):
            return lambda b, w: vN[:, b, first:first + w]

        ATT = -(HD ** -0.5)
        stages = []
        stages.append(Stage("proj", norm="mem", mem=True, groups=[
            Group("N", heads=4, gains=((0, 4, f"mk{l}"),), qk=[mem_kT[:, l, c, :] for c in range(2)],
                  v=(lambda l: lambda b, w: mem_v[:, l, b, :])(l)) for l in range(2)]))
        stages.append(Stage("proj", norm="mix0", groups=[
            Group("N", heads=8, gains=((0, 8, "aq"),), qk=tiles(qT, 0, 4), scale=ATT),
            Group("N", heads=8, gains=((0, 8, "ak"),), qk=tiles(kT, 0, 4)),
            Group("N", heads=8, gains=((0, 8, "bq"),), qk=tiles(qT, 4, 4), scale=ATT),
            Group("N", width=256, heads=2, gains=((0, 2, "bk"),), qk=tiles(kT, 4, 1), v=v_to(512)),
            Group("N", v=v_to(0))]))

        def rows(tensor, tile, base):
            return tensor[base:base + HD, tile, :]

        causal = [(0, i + 1) for i in range(TB)]
        near = [(max(0, i - 1), i + 1) for i in range(TB)]
        slopes = [float(np.float32(2.0 ** (-8.0 * i / 16))) for i in range(1, 17)]

        def v_from(tensor, first, width=HD):
            return lambda j: tensor[:, j, first:first + width]

        heads = [Head([rows(qT, h // 2, HD * (h % 2))], [rows(kT, h // 2, HD * (h % 2))], causal,
                      v_from(vN, HD * h), h // 2, HD * (h % 2), bias="dilated", slope=slopes[8 + h])
                 for h in range(8)]
        heads += [Head([rows(qT, 4 + h % 4, HD * (h // 4))], [rows(kT, 4, HD * (h // 4))], near,
                       v_from(vN, 512 + HD * (h // 4)), 4 + h // 2, HD * (h % 2), bias="window",
                       slope=slopes[h], sink=h) for h in range(8)]
        stages.append(Stage("attn", heads=heads))
        stages.append(Stage("out"))
        stages.append(Stage("mlp", norm="mlp0"))
        stages.append(Stage("proj", norm="mix1", forget=True, groups=[
            Group("N", heads=8, gains=((0, 8, "cq"),), qk=tiles(qT, 0, 4), scale=ATT),
            Group("N", heads=8, gains=((0, 8, "cq"),), qk=tiles(qT, 4, 4), scale=ATT),
            Group("N", heads=8, gains=((0, 8, "ck"),), qk=tiles(kT, 0, 4)),
            Group("N", heads=8, gains=((0, 8, "ck"),), qk=tiles(kT, 4, 4)),
            Group("N", v=v_to(0)), Group("N", v=v_to(512))]))
        stages.append(Stage("attn", heads=[
            Head([rows(qT, h // 2, HD * (h % 2))], [rows(kT, h // 2, HD * (h % 2))], causal,
                 v_from(vN, HD * h), h // 2, HD * (h % 2), mask=causal_b, forget=h) for h in range(16)]))
        stages.append(Stage("out"))
        stages.append(Stage("mlp", norm="mlp1"))

        def memory_heads(layer):
            return [Head([rows(qT, 6 + h // 2, HD * (h % 2))],
                         [mem_kT[HD * (h % 2):HD * (h % 2) + HD, layer, h // 2, :]], [(0, 2)] * TB,
                         (lambda l, h: lambda j: mem_v[:, l, j, HD * h:HD * h + HD])(layer, h),
                         6 + h // 2, HD * (h % 2)) for h in range(4)]

        c_t = [("c", j) for j in range(6)] + [("h", j) for j in range(6)] + [("b", j) for j in range(6)]
        stages.append(Stage("proj", norm="mixb0", rbc=True, groups=[
            Group("N", width=256, heads=4, gains=((0, 4, "mq0"),), qk=tiles(qT, 6, 2), scale=ATT),
            Group("T", t=c_t[0:4]), Group("T", t=c_t[4:8]), Group("T", t=c_t[8:12]),
            Group("T", t=c_t[12:16]), Group("T", width=256, t=c_t[16:18])]))
        stages.append(Stage("attn", heads=memory_heads(0), z=6))
        stages.append(Stage("out"))
        stages.append(Stage("mlp", norm="mlpb0"))
        stages.append(Stage("proj", norm="mixb1", groups=[
            Group("N", heads=8, gains=((0, 8, "dq"),), rope=8, qk=tiles(qT, 0, 4), scale=ATT),
            Group("N", heads=8, gains=((0, 4, "dq"), (4, 4, "mq1")), rope=4, qk=tiles(qT, 4, 4), scale=ATT)]))
        stages.append(Stage("proj", norm="kv", groups=[
            Group("N", heads=8, gains=((0, 8, "dk"),), rope=8, qk=tiles(kT, 0, 4)),
            Group("N", heads=4, gains=((0, 4, "dk"),), rope=4, qk=tiles(kT, 4, 2),
                  v=lambda b, w: vD[:, b, 0:w]),
            Group("N", v=lambda b, w: vD[:, b, 256:256 + w])]))
        stages.append(Stage("attn", diff=True, heads=[
            Head([rows(qT, 3 * n + h // 2, HD * (h % 2)) for n in range(2)],
                 [rows(kT, 3 * n + h // 2, HD * (h % 2)) for n in range(2)], causal,
                 v_from(vD, P * h, P), piece=h, mask=chunk_b) for h in range(6)] + memory_heads(1)))
        stages.append(Stage("out"))
        stages.append(Stage("mlp", norm="mlpb1", last=True))

        at = dict(tile=0, group=0, free=0, hin=0, sq=0, stat=0, var=0, bc=0, t=0, tra=0, trv=0, rn=0,
                  sm=0, unit=0, head=0, pt=0, pta=0, ptv=0, hid=0, tr=0)
        carry = None
        x_free = 0
        for n, s in enumerate(stages):
            s.prev, s.next = (stages[n - 1] if n else None), (stages[n + 1] if n + 1 < len(stages) else None)
            s.at = dict(at)
            s.carry = carry
            s.x_free = x_free
            s.h_free = 0 if n < 2 else at["tile"] - (32 if s.prev.kind == "mlp" else 0)
            if s.norm:
                at["hin"] += 8
                at["sq"] += 8
            if carry:
                carry.sq0 = at["sq"]
                at["sq"] += carry.blocks
                carry = None
            if s.kind == "proj":
                at["stat"] += 1
                at["rn"] += 1
                at["var"] += 1
                at["bc"] += s.rbc
                for g in s.groups:
                    g.blocks = (len(g.t) if g.form == "T" else 2 if s.mem else TB)
                    g.tile0, g.grp, g.free0, g.var, g.t0 = at["tile"], at["group"], at["free"], at["var"], at["t"]
                    g.tra0, g.trv0, g.sq0, g.tr0 = at["tra"], at["trv"], at["sq"], at["tr"]
                    g.end = g.tile0 + g.slots
                    at["tile"] += g.slots
                    at["group"] += 1
                    at["free"] += g.blocks
                    if g.heads:
                        if g is s.groups[-1]:
                            carry = g
                        else:
                            at["sq"] += g.blocks
                        at["var"] += 1
                        at["t"] += 1
                        at["tr"] += 1
                        at["tra"] += (len(g.qk) + 1) // 2
                        at["trv"] += len(g.qk) // 2
                assert not carry or stages[n + 1].kind == "proj"
            elif s.kind == "attn":
                for place, h in enumerate(s.heads):
                    h.sm0, h.unit0, h.idx, h.pt0 = at["sm"], at["unit"], at["head"], at["pt"]
                    h.copied = []
                    for j in range(len(h.queries)):
                        at["pt"] += 1
                        at["ptv" if j % 2 else "pta"] += 1
                        h.copied.append((s_ptv, at["ptv"]) if j % 2 else (s_pta, at["pta"]))
                    at["sm"] += TB * len(h.qs)
                    at["unit"] += TB
                    at["head"] += 1
                    if h.piece is None and h.base:
                        at["hin"] += 1
                        h.hin = at["hin"] + min(place + 2, s.z)
                at["hin"] += s.z
                if s.diff:
                    at["sq"] += 6
                    at["var"] += 1
            elif s.kind == "out":
                if s.prev.diff:
                    at["hin"] += 6
                    at["tr"] += 6
                at["tile"] += 16
                at["group"] += 2
                at["free"] += 8
            else:
                for k, d in TURN.items():
                    if k in at:
                        at[k] += HALVES * d
            if s.kind in ("out", "mlp"):
                x_free = at["free"]
        TOTAL = at["tile"]
        LOADED = TOTAL + 8
        assert LOADED == w_all.shape[0] * 2, (LOADED, w_all.shape)

        class Order:

            def __init__(self, eng, step):
                self.eng, self.step, self.n, self.last = eng, step, {}, None

            def do(self, ins, signal=None):
                self.last = signal or self.step
                ins.then_inc(self.last, 1)
                self.n[id(self.last)] = self.n.get(id(self.last), 0) + 1

            def sync(self):
                self.eng.wait_ge(self.last, self.n[id(self.last)])

        block = ctx.enter_context(nc.Block())

        @block.sync
        def _(sp):
            sp.dma_start(vec[:, 0:V_CONV], vecs_d[:, 0:V_CONV]).then_inc(s_in[1], 16)
            for q in range(PAIRS):
                sp.dma_start(stage_w[:, q], w_all[q]).then_inc(s_load[q], 16)
            sp.dma_start(vec[:, V_CONV:], vecs_d[:, V_CONV:]).then_inc(s_in[5], 16)
            sp.dma_start(wf_in[:], w_f).then_inc(s_in[4], 16)
            whole = LOADED // RING
            with sp.Fori(1, whole) as c:
                for q in range(PAIRS):
                    sp.wait_ge(s_wlo, c * RING + (2 * q + 2 - RING))
                    sp.dma_start(stage_w[:, q], w_all[c * PAIRS + q]).then_inc(s_load[q], 16)
            for q in range((LOADED - whole * RING) // 2):
                sp.wait_ge(s_wlo, (whole - 1) * RING + 2 * q + 2)
                sp.dma_start(stage_w[:, q], w_all[whole * PAIRS + q]).then_inc(s_load[q], 16)
            for n in range(KT):
                sp.wait_ge(s_free, at["free"] - 8 + n + 1)
                sp.dma_start(out_t[n * P:(n + 1) * P, :], xT[:, n, :]).then_inc(s_out, 16)
            sp.wait_ge(s_out, 16 * KT)

        @block.gpsimd
        def _(pool):
            def low(slot, ready):
                pool.wait_ge(s_whi, ready)
                nc.gpsimd.tensor_tensor(w_lo[:, slot], stage_w[:, slot // 2, slot % 2],
                                        w_hi[:, slot].bitcast(F32), ALU.subtract).then_inc(s_wlo, 1)

            whole = LOADED // RING
            with pool.Fori(0, whole) as c:
                for j in range(RING):
                    low(j, c * RING + (j + 1))
            for j in range(LOADED - whole * RING):
                low(j, whole * RING + j + 1)

        @block.tensor
        def _(pe):
            mm = nc.tensor.matmul
            passes = ((0, 0), (0, 1), (1, 0))

            def bank(group, b):
                return ps[4 * (group % 2) + b]

            def wait_weights(n, i=None, d=0):
                pe.wait_ge(s_wlo, n + 1 if i is None else i * d + (n + 1))

            def group_mm(s, g, k, slot, part, first, last):
                w = (w_hi, w_lo)
                h = (hid_hi, hid_lo) if s.mem else (h_hi, h_lo)
                ins = None
                for b in range(g.blocks):
                    out = bank(g.grp, b)
                    for n, (a, m) in enumerate(passes):
                        st, en = first and n == 0, last and n == 2
                        if g.form == "T":
                            ins = mm(out[:, :], w[a][:, slot, part * 256 + b * P:part * 256 + b * P + P],
                                     h[m][:, k, :], start=st, stop=en)
                        else:
                            ins = mm(out[:, 0:g.width], h[a][:, k, b * P:(b + 1) * P],
                                     w[m][:, slot, part * 256:part * 256 + g.width], start=st, stop=en)
                return ins

            def stat_mm(s, to):
                ins = None
                for b in range(2 if s.mem else TB):
                    ins = mm(to[:, b:b + 1], ssum[:, b * P:(b + 1) * P], mean_w[:, 0:1], start=True, stop=True)
                ins.then_inc(s_stat, 1)

            def bc_mm(to):
                for b in range(TB):
                    ins = mm(to[:, b * P:(b + 1) * P], mean_w, rms_bc[:, b * P:(b + 1) * P],
                             start=True, stop=True)
                ins.then_inc(s_bc, 1)

            def transposes(g):
                pe.wait_ge(s_t, g.t0 + 1)
                pe.wait_ge(s_free, g.free0 + g.blocks)
                for c in range(len(g.qk)):
                    for b in range(g.blocks):
                        ins = nc.tensor.transpose(bank(g.grp, c)[:, b * P:(b + 1) * P],
                                                  tn[:, g.grp % 2, b, c * P:(c + 1) * P], ident)
                ins.then_inc(s_tr, 1)

            def proj(s):
                A = s.at
                other = s.groups[0].grp + 1
                for gi, g in enumerate(s.groups):
                    prev = s.groups[gi - 1] if gi else s.carry
                    before = (s.groups[gi - 2] if gi > 1 else s.carry if gi else
                              s.prev.groups[-2] if s.carry else None)
                    need = g.free0 - (prev.blocks if prev else 0)
                    if need:
                        pe.wait_ge(s_free, need)
                    if gi == 1:
                        pe.wait_ge(s_rn, A["rn"] + 1)
                        if s.rbc:
                            pe.wait_ge(s_rbc, A["bc"] + 1)
                        if s.forget:
                            pe.wait_ge(s_fabs, 1)
                    if before and before.heads:
                        pe.wait_ge(s_tra, before.tra0 + (len(before.qk) + 1) // 2)
                        if len(before.qk) > 1:
                            pe.wait_ge(s_trv, before.trv0 + len(before.qk) // 2)
                    parts = TILE // g.width
                    for j in range(g.slots):
                        wait_weights(g.tile0 + j)
                        for part in range(parts):
                            k = j * parts + part
                            if gi == 0:
                                pe.wait_ge(s_hlo, A["hin"] + k + 1)
                            ins = group_mm(s, g, k, (g.tile0 + j) % RING, part, k == 0, k == KT - 1)
                        ins.then_inc(s_used, 1)
                        if gi == 0 and j == g.slots // 2 - 1:
                            pe.wait_ge(s_sqc, A["sq"] + 8)
                            if s.carry:
                                pe.wait_ge(s_free, g.free0)
                            stat_mm(s, bank(other, 0))
                        if gi and prev.heads and j == g.slots * 3 // 4 - 1:
                            transposes(prev)
                        if s.forget and gi == 5 and j == 5:
                            pe.wait_ge(s_flog, 1)
                            pe.wait_ge(s_free, g.free0)
                            for b in range(TB):
                                cm = mm(bank(g.grp + 1, 0)[0:16, b * P:SEQ], fl[:, b * 16:(b + 1) * 16],
                                        cst[:, C_TRI:C_TRI + SEQ - b * P], start=b == 0, stop=b == TB - 1)
                            cm.then_inc(s_cmm, 1)
                    if gi == 0 and s.rbc:
                        pe.wait_ge(s_diag, A["bc"] + 1)
                        bc_mm(bank(other, 1))
                    if gi == 0 and s.forget:
                        pe.wait_ge(s_wf, 1)
                        for b in range(TB):
                            for k in range(KT):
                                for n, (a, m) in enumerate(passes):
                                    fm = mm(bank(other, 2)[:, b * 16:(b + 1) * 16],
                                            (h_hi, h_lo)[a][:, k, b * P:(b + 1) * P],
                                            (wf_hi, wf_lo)[m][:, k * 16:(k + 1) * 16],
                                            start=k == 0 and n == 0, stop=k == KT - 1 and n == 2)
                        fm.then_inc(s_fmm, 1)
                    if gi == 0 and s.carry:
                        pe.wait_ge(s_rn, A["rn"] + 1)
                        transposes(s.carry)

            def attention(s):
                A = s.at
                pe.wait_ge(s_free, A["free"])
                pe.wait_ge(s_tra, A["tra"])
                pe.wait_ge(s_trv, A["trv"])
                if s.heads[0].forget is not None:
                    pe.wait_ge(s_clo, 1)

                def scores(h, i, m):
                    sm = h.sm0 + i * len(h.qs) + m
                    n, first = h.n[i], h.lo[i] * P
                    out = ps[sm % 3]
                    if sm - 3 >= A["sm"]:
                        pe.wait_ge(s_prob, sm - 3 + 1)
                    plain = h.mask is None and h.forget is None
                    ins = mm(out[:, 0:n], h.qs[m][:, i * P:(i + 1) * P], h.ks[m][:, first:first + n],
                             start=True, stop=plain)
                    if h.forget is not None:
                        sel = ident_r[0:16, h.forget:h.forget + 1].to_broadcast([16, P])
                        for c in (c_hi, c_lo):
                            ins = mm(out[:, 0:n], sel, c[:, 0:n], start=False, stop=False)
                    if h.mask is not None:
                        ins = mm(out[:, n - P:n], ident_b[:], h.mask[:], start=False, stop=True)
                    ins.then_inc(s_score, 1)

                def turn(h, j):
                    if j == 0:
                        pe.wait_ge(s_pn, h.unit0 + TB)
                    if h.idx > A["head"]:
                        before = s.heads[h.idx - A["head"] - 1]
                        if j < len(before.queries):
                            pe.wait_ge(*before.copied[j])
                    for n, i in enumerate(h.queries[j]):
                        a = h.at_p[i] + (j - h.lo[i]) * P
                        ins = nc.tensor.transpose(ps[3 + j][:, n * P:(n + 1) * P], prob[:, h.idx % 2, a:a + P], ident)
                    ins.then_inc(s_pt, 1)

                def values(h, j):
                    pe.wait_ge(*h.copied[j])
                    if h.idx > A["head"] and j == 0:
                        before = s.heads[h.idx - A["head"] - 1]
                        if before.piece is not None:
                            pe.wait_ge(s_o, before.piece + 1)
                        elif before.base:
                            pe.wait_ge(s_hlo, before.hin)
                    q = h.queries[j]
                    t = probT[:, h.idx % 2, h.at_t[j]:h.at_t[j] + P * len(q)]
                    if h.piece is not None:
                        if j == len(h.queries) - 1:
                            for i in range(TB):
                                for k in range(i + 1):
                                    a = h.at_t[k] + (i - k) * P
                                    ins = mm(ps[7][:, i * P:(i + 1) * P], probT[:, h.idx % 2, a:a + P], h.v(k),
                                             start=k == 0, stop=k == i)
                            ins.then_inc(s_pv, 1)
                        return
                    out = ps[7][h.base:h.base + HD, :]
                    last = j == len(h.queries) - 1
                    if len(h.queries[0]) == TB:
                        ins = mm(out[:, q[0] * P:SEQ], h.v(j), t, start=j == 0, stop=last)
                    elif last:
                        for i in range(TB):
                            for k in range(h.lo[i], i + 1):
                                a = h.at_t[k] + (i - k) * P
                                ins = mm(out[:, i * P:(i + 1) * P], h.v(k), probT[:, h.idx % 2, a:a + P],
                                         start=k == h.lo[i], stop=k == i)
                    if last:
                        ins.then_inc(s_pv, 1)

                for n in range(len(s.heads) + 2):
                    new = s.heads[n] if n < len(s.heads) else None
                    mid = s.heads[n - 1] if 0 <= n - 1 < len(s.heads) else None
                    old = s.heads[n - 2] if n >= 2 else None
                    score = [(i, m) for i in range(TB) for m in range(len(new.qs))] if new else []
                    value = list(range(len(old.queries))) if old else []
                    turns = list(range(len(mid.queries))) if mid else []
                    many = len(score) > TB
                    for what, count in ((("s", 3), ("v", 1), ("s", 1), ("v", 1), ("s", 1), ("v", 9), ("s", 1), ("t", 1),
                                         ("s", 1), ("t", 9), ("s", 9)) if many else
                                        (("s", 1), ("v", 1), ("s", 1), ("v", 1), ("s", 1), ("v", 9), ("t", 9), ("s", 9))):
                        for _ in range(count):
                            if what == "s" and score:
                                scores(new, *score.pop(0))
                            elif what == "v" and value:
                                values(old, value.pop(0))
                            elif what == "t" and turns:
                                turn(mid, turns.pop(0))

            def out_proj(s):
                A = s.at
                g0 = A["group"]
                pe.wait_ge(s_hlo, A["hin"])
                if s.prev.diff:
                    pe.wait_ge(s_y, 1)
                    for c in range(6):
                        if c >= 4:
                            pe.wait_ge(s_hlo, A["hin"] + c - 4 + 1)
                        for b in range(TB):
                            ins = nc.tensor.transpose(bank(g0 + 1, c % 4)[:, b * P:(b + 1) * P],
                                                      pieces[c // 2][:, b, (c % 2) * P:(c % 2) * P + P], ident)
                        ins.then_inc(s_tr, 1)
                for gi in range(2):
                    for j in range(KT):
                        n = A["tile"] + gi * 8 + j
                        wait_weights(n)
                        if s.prev.diff:
                            pe.wait_ge(s_hlo, A["hin"] + (min(j + 1, 6) if gi == 0 else 6))
                        for b in range(4):
                            for m, (a, c) in enumerate(passes):
                                ins = mm(bank(g0 + gi, b)[:, :], (w_hi, w_lo)[a][:, n % RING, b * P:(b + 1) * P],
                                         (h_hi, h_lo)[c][:, j, :], start=j == 0 and m == 0,
                                         stop=j == KT - 1 and m == 2)
                        ins.then_inc(s_used, 1)

            def mlp(s):
                A = s.at
                g0 = A["group"]
                with pe.Fori(0, HALVES) as i:
                    for gi in range(MLP_GROUPS):
                        up = gi < 4
                        base = 8 * gi if up else 32 + 16 * (gi - 4)
                        for j in range(8 if up else 16):
                            t = base + j
                            n = A["tile"] + t
                            pe.wait_ge(s_wlo, i * MLP_TILES + (n + 1))
                            if gi == 0:
                                pe.wait_ge(s_hlo, A["hin"] + j + 1)
                            if gi == 4:
                                pe.wait_ge(s_hid, i * HID + (A["hid"] + j + 1))
                            src = (h_hi, h_lo) if up else (hid_hi, hid_lo)
                            for b in range(4):
                                if j == 0:
                                    pe.wait_ge(s_free, i * 24 + (A["free"] + 4 * gi - 8 + b + 1))
                                    if gi == 1 and b == 0:
                                        pe.wait_ge(s_rbc, i * 1 + (A["bc"] + 1))
                                for m, (a, c) in enumerate(passes):
                                    ins = mm(bank(g0 + gi, b)[:, :], (w_hi, w_lo)[a][:, n % RING, b * P:(b + 1) * P],
                                             src[c][:, j, :], start=j == 0 and m == 0,
                                             stop=j == (7 if up else 15) and m == 2)
                            ins.then_inc(s_used, 1)
                            if gi == 0 and j == 3:
                                pe.wait_ge(s_sqc, A["sq"] + 8)
                                pe.wait_ge(s_free, i * 24 + A["free"])
                                stat_mm(s, bank(g0 + 1, 0))
                            if gi == 0 and j == 7:
                                pe.wait_ge(s_diag, i * 1 + (A["bc"] + 1))
                                bc_mm(bank(g0 + 1, 1))

            pe.wait_ge(s_in[0], 16)
            pe.wait_ge(s_set, 1)
            for s in stages:
                {"proj": proj, "attn": attention, "out": out_proj, "mlp": mlp}[s.kind](s)

        def source(s):
            return (kT, MEM) if s.mem else (xT, SEQ)

        def hi_lo(s):
            return (hid_hi, hid_lo) if s.mem else (h_hi, h_lo)

        @block.scalar
        def _(act):
            order = Order(act, s_act)
            do, sync = order.do, order.sync
            act.dma_start(kT[:, :, 0:MEM], mem_t.rearrange("(k p) n -> p k n", p=P)).then_inc(s_in[2], 16)
            act.dma_start(xT[:], x_t.rearrange("(k p) n -> p k n", p=P)).then_inc(s_in[3], 16)
            act.dma_start(cst[:], consts_d).then_inc(s_in[0], 16)
            split = [0]

            def split_to(limit):
                while split[0] < min(limit, LOADED):
                    n = split[0]
                    act.wait_ge(s_load[n // 2 % PAIRS], 16 * (n // RING + 1))
                    if n >= RING:
                        act.wait_ge(s_used, n - RING + 1)
                    do(nc.scalar.activation(w_hi[:, n % RING], stage_w[:, n // 2 % PAIRS, n % 2], ACT.Copy), s_whi)
                    split[0] += 1

            def square(q, src, scale=1.0):
                if q >= 2:
                    act.wait_ge(s_sqc, q - 1)
                do(nc.scalar.activation(sqb[:, q % 2, 0:src.shape[-1]], src, ACT.Square, scale=scale), s_sq)

            def norm_input(s, tiles):
                A = s.at
                x, m = source(s)
                g = V_GAIN[s.norm]
                act.wait_ge(s_in[2] if s.mem else s_in[3], 16)
                if s.h_free:
                    act.wait_ge(s_used, s.h_free)
                for j in tiles:
                    if s.x_free:
                        act.wait_ge(s_free, s.x_free - KT + j + 1)
                    do(nc.scalar.activation(hi_lo(s)[0][:, j, 0:m], x[:, j, 0:m], ACT.Copy,
                                            scale=vec[:, g + j:g + j + 1]), s_hhi)
                    square(A["sq"] + j, x[:, j, 0:m])

            def take_root(v, w):
                act.wait_ge(s_var, v + 1)
                do(nc.scalar.activation(root[:, 0:w], var[:, 0:w], ACT.Sqrt), s_root)

            def head_squares(s, g):
                act.wait_ge(s_used, g.end)
                act.wait_ge(s_rn, s.at["rn"] + 1)
                for b in range(g.blocks):
                    square(g.sq0 + b, ps[4 * (g.grp % 2) + b][:, 0:HD * g.heads], rn[:, b:b + 1])
                take_root(g.var, g.heads * g.blocks)

            def transposed(g):
                for c in range(0, len(g.qk), 2):
                    act.wait_ge(s_tr, g.tr0 + 1)
                    do(nc.scalar.activation(g.qk[c], ps[4 * (g.grp % 2) + c][:, 0:P * g.blocks], ACT.Copy,
                                            scale=g.scale), s_tra)

            def proj(s):
                A = s.at
                split_to(A["tile"] + RING)
                if s.prev is None or s.prev.kind == "proj":
                    norm_input(s, range(KT))
                if s.carry:
                    head_squares(s.prev, s.carry)
                g0 = s.groups[0]
                split_to(g0.tile0 + g0.slots // 2 + RING)
                take_root(A["var"], 2 if s.mem else TB)
                if s.forget:
                    split_to(g0.end + RING)
                    act.wait_ge(s_fabs, 1)
                    do(nc.scalar.activation(fe[:], fa[:], ACT.Exp, scale=-1.0))
                    sync()
                    do(nc.scalar.activation(fl[:], fe[:], ACT.Ln, bias=1.0), s_fln)
                if s.carry:
                    split_to(g0.end + RING)
                    transposed(s.carry)
                for gi, g in enumerate(s.groups):
                    split_to(g.end + RING)
                    if not g.heads or (g is s.groups[-1]):
                        continue
                    head_squares(s, g)
                    nxt = s.groups[gi + 1]
                    split_to(nxt.tile0 + nxt.slots * 3 // 4 + RING)
                    transposed(g)
                if s.forget:
                    act.wait_ge(s_cmm, 1)
                    do(nc.scalar.activation(c_hi[:], ps[4 * ((s.groups[5].grp + 1) % 2)][0:16, :], ACT.Copy), s_chi)

            def attention(s):
                A = s.at
                split_to(A["tile"] + RING)

                def exps(h, i):
                    unit = h.unit0 + i
                    for m in range(len(h.qs)):
                        sm = h.sm0 + i * len(h.qs) + m
                        col = slice(sm % 16, sm % 16 + 1)
                        act.wait_ge(s_max, sm + 1)
                        if m == 1:
                            dst = sqb[:, unit % 2, 0:h.n[i]]
                            if unit - 2 >= A["unit"]:
                                act.wait_ge(s_pn, unit - 1)
                        else:
                            dst = prob[:, h.idx % 2, h.at_p[i]:h.at_p[i] + h.n[i]]
                            if h.idx - 2 >= A["head"]:
                                old = s.heads[h.idx - 2 - A["head"]]
                                act.wait_ge(s_pt, old.pt0 + len(old.queries))
                        if h.sink is not None:
                            do(nc.scalar.activation(esink[:, col], nsink[:, h.sink:h.sink + 1],
                                                    ACT.Exp, scale=-1.0, bias=mneg[:, col]))
                        src = dst if h.bias is not None else ps[sm % 3][:, 0:h.n[i]]
                        do(nc.scalar.activation(dst, src, ACT.Exp, scale=-1.0, bias=mneg[:, col],
                                                accum_out=den[:, col]), s_prob)

                def copies(h):
                    if h.idx - 2 >= A["head"]:
                        act.wait_ge(s_pv, h.idx - 1)
                    for j in range(0, len(h.queries), 2):
                        act.wait_ge(s_pt, h.pt0 + j + 1)
                        w = P * len(h.queries[j])
                        do(nc.scalar.activation(probT[:, h.idx % 2, h.at_t[j]:h.at_t[j] + w], ps[3 + j][:, 0:w],
                                                ACT.Copy), s_pta)

                def output(h):
                    if h.piece is not None:
                        act.wait_ge(s_pv, h.idx + 1)
                        p = pieces[h.piece // 2][:, :, (h.piece % 2) * P:(h.piece % 2) * P + P]
                        do(nc.scalar.activation(p, ps[7][:, :].rearrange("p (b d) -> p b d", b=TB), ACT.Copy), s_o)
                    elif h.base:
                        act.wait_ge(s_pv, h.idx + 1)
                        do(nc.scalar.activation(h_hi[:, h.tile, :], ps[7][:, :], ACT.Copy), s_hhi)

                for n in range(len(s.heads) + 2):
                    new = s.heads[n] if n < len(s.heads) else None
                    for i in range(3 if new else 0):
                        exps(new, i)
                    if n >= 2:
                        output(s.heads[n - 2])
                    if 0 <= n - 1 < len(s.heads):
                        copies(s.heads[n - 1])
                    if new:
                        exps(new, 3)
                    if n < s.z:
                        act.wait_ge(s_used, A["tile"])
                        act.wait_ge(s_z, n + 1)
                        do(nc.scalar.activation(h_hi[:, n, :], qT[:, n, :], ACT.Copy), s_hhi)
                if s.diff:
                    act.wait_ge(s_pn, s.heads[-1].unit0 + TB)
                    for n in range(6):
                        square(A["sq"] + n, pieces[n // 2][:, 2 * (n % 2):2 * (n % 2) + 2, :]
                               .rearrange("p b n -> p (b n)"))
                    take_root(A["var"], 24)

            def out_proj(s):
                A = s.at
                split_to(A["tile"] + RING)
                if s.prev.diff:
                    for c in range(6):
                        act.wait_ge(s_tr, A["tr"] + c + 1)
                        do(nc.scalar.activation(h_hi[:, c, :], ps[4 * ((A["group"] + 1) % 2) + c % 4][:, :], ACT.Copy,
                                                scale=vec[:, V_SUB:V_SUB + 1]), s_hhi)
                split_to(A["tile"] + 16 + RING)
                norm_input(s.next, range(KT))

            def mlp(s):
                A = s.at
                for half in range(HALVES):
                    t0 = A["tile"] + half * MLP_TILES
                    split_to(t0 + 4 + RING)
                    take_root(A["var"] + half, TB)
                    for u in range(4):
                        split_to(t0 + 8 * (u + 1) + RING)
                        for b in range(4):
                            t = 4 * u + b
                            hid = A["hid"] + half * HID + t
                            act.wait_ge(s_free, A["free"] + 24 * half + t + 1)
                            if hid >= 2:
                                act.wait_ge(s_hid, hid - 1)
                            do(nc.scalar.activation(hsq[:, t % 2], relu[:, t % 2], ACT.Square), s_hsq)
                            sync()
                            do(nc.scalar.activation(hid_hi[:, t], hsq[:, t % 2], ACT.Copy), s_hidhi)
                    early = half == HALVES - 1 and not s.last
                    if early:
                        split_to(t0 + 48 + RING)
                        norm_input(s.next, range(4))
                    split_to(t0 + MLP_TILES + RING)
                    if early:
                        norm_input(s.next, range(4, KT))

            act.wait_ge(s_in[1], 16)
            for s in stages:
                if s.forget:
                    act.wait_ge(s_in[4], 16)
                    do(nc.scalar.activation(wf_hi[:], wf_in[:], ACT.Copy), s_seta)
                {"proj": proj, "attn": attention, "out": out_proj, "mlp": mlp}[s.kind](s)
                if s is stages[0]:
                    act.wait_ge(s_set, 2)
                    do(nc.scalar.activation(lam[:, 2:4], lam[:, 0:2], ACT.Exp), s_seta)

        @block.vector
        def _(dve):
            order = Order(dve, s_dve)
            do, sync = order.do, order.sync
            vt, vs, stt, tt = (nc.vector.tensor_tensor, nc.vector.tensor_scalar,
                               nc.vector.scalar_tensor_tensor, nc.vector.tensor_tensor)

            def norm_input(s, tiles):
                A = s.at
                x, m = source(s)
                hi, lo = hi_lo(s)
                g = V_GAIN[s.norm]
                for j in tiles:
                    dve.wait_ge(s_hhi, A["hin"] + j + 1)
                    do(stt(lo[:, j, 0:m], x[:, j, 0:m], vec[:, g + j:g + j + 1], hi[:, j, 0:m].bitcast(F32),
                           ALU.mult, ALU.subtract), s_hlo)
                    q = A["sq"] + j
                    dve.wait_ge(s_sq, q + 1)
                    if j == 0:
                        do(nc.vector.tensor_copy(ssum[:, 0:m], sqb[:, q % 2, 0:m]), s_sqc)
                    else:
                        sync()
                        do(tt(ssum[:, 0:m], ssum[:, 0:m], sqb[:, q % 2, 0:m], ALU.add), s_sqc)

            def rsqrt(out, v, w, signal=None):
                dve.wait_ge(s_root, v + 1)
                do(nc.vector.reciprocal(inv[:, 0:w], root[:, 0:w]))
                sync()
                do(tt(newt[:, 0:w], inv[:, 0:w], inv[:, 0:w], ALU.mult))
                sync()
                do(tt(newt[:, 0:w], newt[:, 0:w], var[:, 0:w], ALU.mult))
                sync()
                do(vs(newt[:, 0:w], newt[:, 0:w], -0.5, 1.5, ALU.mult, ALU.add))
                sync()
                do(tt(out, inv[:, 0:w], newt[:, 0:w], ALU.mult), signal)
                sync()

            def token_norm(s, other, turn=0):
                A = s.at
                nb = 2 if s.mem else TB
                dve.wait_ge(s_stat, A["stat"] + turn + 1)
                do(vs(var[:, 0:nb], ps[4 * (other % 2)][:, 0:nb], EPS, None, ALU.add), s_var)
                rsqrt(rn[:, 0:nb], A["var"] + turn, nb, s_rn)
                if s.rbc or s.kind == "mlp":
                    for b in range(TB):
                        do(vs(rms_bc[:, b * P:(b + 1) * P], ident, rn[:, b:b + 1], float(D), ALU.mult, ALU.mult),
                           s_diag if b == TB - 1 else None)
                    dve.wait_ge(s_bc, A["bc"] + turn + 1)
                    do(nc.vector.tensor_copy(rms_bc[:], ps[4 * (other % 2) + 1][:, :]), s_rbc)
                    sync()

            def forget_gates(s):
                bank = ps[4 * ((s.groups[0].grp + 1) % 2) + 2]
                dve.wait_ge(s_fmm, 1)
                for b in range(TB):
                    do(stt(fz[:, 16 * b:16 * b + 16], bank[:, 16 * b:16 * b + 16], rn[:, b:b + 1],
                           vec[:, V_FORGET:V_FORGET + 16], ALU.mult, ALU.add))
                sync()
                do(stt(fa[:], fz[:], -1.0, fz[:], ALU.mult, ALU.max), s_fabs)
                dve.wait_ge(s_fln, 1)
                do(stt(fa[:], fz[:], 0.0, fl[:], ALU.min, ALU.subtract))
                sync()
                do(nc.vector.tensor_copy(fl[:], fa[:]), s_flog)

            def heads(s, g):
                nb, nh, par = g.blocks, g.heads, g.grp % 2
                w = nb * nh
                for b in range(nb):
                    q = g.sq0 + b
                    dve.wait_ge(s_sq, q + 1)
                    do(nc.vector.tensor_reduce(hsum[:, b * nh:(b + 1) * nh],
                                               sqb[:, q % 2, 0:nh * HD].rearrange("p (h d) -> p h d", d=HD),
                                               axis=AX.X, op=ALU.add), s_sqc)
                sync()
                do(vs(var[:, 0:w], hsum[:, 0:w], 1.0 / HD, EPS, ALU.mult, ALU.add), s_var)
                rsqrt(hsum[:, 0:w], g.var, w)
                do(tt(newt[:, 0:w].rearrange("p (b h) -> p b h", b=nb), hsum[:, 0:w].rearrange("p (b h) -> p b h", b=nb),
                      rn[:, 0:nb].unsqueeze(2).to_broadcast([P, nb, nh]), ALU.mult))
                sync()
                if g.tr0:
                    dve.wait_ge(s_tr, g.tr0)
                for b in range(nb):
                    bank = ps[4 * par + b]
                    do(tt(tn[:, par, b, 0:nh * HD].rearrange("p (h d) -> p h d", d=HD),
                          bank[:, 0:nh * HD].rearrange("p (h d) -> p h d", d=HD),
                          newt[:, b * nh:(b + 1) * nh].unsqueeze(2).to_broadcast([P, nh, HD]), ALU.mult),
                       None if g.v else s_free)
                    if g.v:
                        values(g, b)
                sync()
                for n, (first, count, name) in enumerate(g.gains):
                    t = tn[:, par, 0:nb, first * HD:(first + count) * HD].rearrange("p b (h d) -> p b h d", d=HD)
                    gain = vec[:, V_HEAD[name]:V_HEAD[name] + HD]
                    gain = gain.unsqueeze(1).unsqueeze(1).to_broadcast([P, nb, count, HD])
                    last = n == len(g.gains) - 1 and not g.rope
                    do(tt(t, t, gain, ALU.mult), s_t if last else None)
                if g.rope:
                    rope(g)

            def rope(g):
                sync()
                nr = g.rope
                t = tn[:, g.grp % 2, 0:TB, 0:nr * HD].rearrange("p b (h d) -> p b h d", d=HD)
                a, b = t[:, :, :, 0:8], t[:, :, :, 8:16]
                cos, sin = (cst[:, c:c + 32].rearrange("p (b d) -> p b d", b=TB).unsqueeze(2)
                            .to_broadcast([P, TB, nr, 8]) for c in (C_COS, C_SIN))
                m = [rope_t[:, k, 0:32 * nr].rearrange("p (b h d) -> p b h d", b=TB, h=nr) for k in range(4)]
                do(tt(m[0], a, cos, ALU.mult))
                do(tt(m[1], b, sin, ALU.mult))
                do(tt(m[2], a, sin, ALU.mult))
                do(tt(m[3], b, cos, ALU.mult))
                sync()
                do(tt(a, m[0], m[1], ALU.subtract))
                do(tt(b, m[2], m[3], ALU.add), s_t)

            def values(g, b):
                q = g.heads * HD
                do(vs(g.v(b, g.width - q), ps[4 * (g.grp % 2) + b][:, q:g.width], rn[:, b:b + 1], None, ALU.mult),
                   s_free)

            def features(g):
                for n, (kind, j) in enumerate(g.t):
                    bank = ps[4 * (g.grp % 2) + n]
                    if kind == "c":
                        do(tt(kT[:, j, :], bank[:, :], rms_bc[:], ALU.mult), s_free)
                        continue
                    tmp = relu[:, 0]
                    do(tt(tmp, bank[:, :], rms_bc[:], ALU.mult), s_free)
                    sync()
                    z = qT[:, j, :]
                    if kind == "b":
                        do(tt(z, z, tmp, ALU.mult), s_z)
                        sync()
                        continue
                    do(tt(uP[:, j, 2:514], tmp, kT[:, j, :], ALU.mult))
                    sync()
                    w = [vec[:, V_CONV + 6 * k + j:V_CONV + 6 * k + j + 1] for k in range(3)]
                    do(vs(z, uP[:, j, 0:512], w[0], None, ALU.mult))
                    sync()
                    for k in (1, 2):
                        do(stt(z, uP[:, j, k:k + 512], w[k], z, ALU.mult, ALU.add))
                        sync()

            def transposed(g):
                for c in range(1, len(g.qk), 2):
                    dve.wait_ge(s_tr, g.tr0 + 1)
                    do(vs(g.qk[c], ps[4 * (g.grp % 2) + c][:, 0:P * g.blocks], g.scale, None, ALU.mult), s_trv)

            def proj(s):
                A = s.at
                if s.prev is None or s.prev.kind == "proj":
                    norm_input(s, range(KT))
                if s.carry:
                    dve.wait_ge(s_used, s.carry.end)
                    heads(s.prev, s.carry)
                token_norm(s, s.groups[0].grp + 1)
                if s.forget:
                    forget_gates(s)
                if s.rbc:
                    do(nc.vector.memset(uP[:, :, 0:2], 0.0))
                    sync()
                if s.carry:
                    transposed(s.carry)
                for g in s.groups:
                    if g.heads and g is s.groups[-1]:
                        continue
                    dve.wait_ge(s_used, g.end)
                    if g.form == "T":
                        features(g)
                    elif g.heads:
                        heads(s, g)
                        transposed(g)
                    else:
                        for b in range(g.blocks):
                            values(g, b)
                if s.forget:
                    dve.wait_ge(s_chi, 1)
                    do(tt(c_lo[:], ps[4 * ((s.groups[5].grp + 1) % 2)][0:16, :], c_hi[:].bitcast(F32),
                          ALU.subtract), s_clo)

            def attention(s):
                A = s.at
                dve.wait_ge(s_tr, A["tr"])

                def row_min(h, i):
                    n = h.n[i]
                    bias = None
                    if h.bias:
                        w, log = (512, C_LOGW) if h.bias == "dilated" else (256, C_WIN)
                        bias = bias_t[:, h.idx % 2, w - (i + 1 - h.lo[i]) * P:w]
                        if i == 0:
                            sync()
                            do(stt(bias_t[:, h.idx % 2, 0:w], cst[:, C_DELTA + 512 - w:C_DELTA + 512], h.slope,
                                   cst[:, log:log + w], ALU.mult, ALU.add))
                            sync()
                    for m in range(len(h.qs)):
                        sm = h.sm0 + i * len(h.qs) + m
                        low = mneg[:, sm % 16:sm % 16 + 1]
                        dve.wait_ge(s_score, sm + 1)
                        src = ps[sm % 3][:, 0:n]
                        if bias is None:
                            do(nc.vector.tensor_reduce(low, src, axis=AX.X, op=ALU.min), s_max)
                            continue
                        if h.idx - 2 >= A["head"]:
                            old = s.heads[h.idx - 2 - A["head"]]
                            dve.wait_ge(s_pt, old.pt0 + len(old.queries))
                        do(nc.vector.tensor_tensor_reduce(
                            out=prob[:, h.idx % 2, h.at_p[i]:h.at_p[i] + n], in0=src, in1=bias, scale=1.0, scalar=3e38,
                            op0=ALU.add, op1=ALU.min, accum_out=low), None if h.sink is not None else s_max)
                        if h.sink is not None:
                            sync()
                            do(tt(low, low, nsink[:, h.sink:h.sink + 1], ALU.min), s_max)

                def normalise(h, i):
                    sm = h.sm0 + i * len(h.qs)
                    dve.wait_ge(s_prob, sm + len(h.qs))
                    c = [slice((sm + m) % 16, (sm + m) % 16 + 1) for m in range(len(h.qs))]
                    p1 = prob[:, h.idx % 2, h.at_p[i]:h.at_p[i] + h.n[i]]
                    if h.sink is not None:
                        do(tt(den[:, c[0]], den[:, c[0]], esink[:, c[0]], ALU.add))
                        sync()
                    for k in c:
                        do(nc.vector.reciprocal(rden[:, k], den[:, k]))
                    sync()
                    if len(c) == 1:
                        do(vs(p1, p1, rden[:, c[0]], None, ALU.mult), s_pn)
                        return
                    do(tt(esink[:, c[1]], rden[:, c[1]], lam[:, 4:5], ALU.mult))
                    do(vs(p1, p1, rden[:, c[0]], None, ALU.mult))
                    sync()
                    do(stt(p1, sqb[:, (h.unit0 + i) % 2, 0:h.n[i]], esink[:, c[1]], p1, ALU.mult, ALU.add), s_pn)

                def copies(h):
                    if len(h.queries) > 1 and h.idx - 2 >= A["head"]:
                        dve.wait_ge(s_pv, h.idx - 1)
                    for j in range(1, len(h.queries), 2):
                        dve.wait_ge(s_pt, h.pt0 + j + 1)
                        w = P * len(h.queries[j])
                        do(nc.vector.tensor_copy(probT[:, h.idx % 2, h.at_t[j]:h.at_t[j] + w], ps[3 + j][:, 0:w]), s_ptv)

                hin = [A["hin"]]

                def low_part(tile, src):
                    hin[0] += 1
                    dve.wait_ge(s_hhi, hin[0])
                    do(tt(h_lo[:, tile, :], src, h_hi[:, tile, :].bitcast(F32), ALU.subtract), s_hlo)

                for n in range(len(s.heads) + 2):
                    new = s.heads[n] if n < len(s.heads) else None
                    mid = s.heads[n - 1] if 0 <= n - 1 < len(s.heads) else None
                    if new:
                        row_min(new, 0)
                    if mid:
                        normalise(mid, 3)
                    if new:
                        row_min(new, 1)
                        normalise(new, 0)
                        row_min(new, 2)
                        normalise(new, 1)
                    if n >= 2 and s.heads[n - 2].piece is None and s.heads[n - 2].base:
                        low_part(s.heads[n - 2].tile, ps[7][:, :])
                    if mid:
                        copies(mid)
                    if new:
                        normalise(new, 2)
                        row_min(new, 3)
                    if n < s.z:
                        low_part(n, qT[:, n, :])
                if s.diff:
                    for n in range(6):
                        q = A["sq"] + n
                        dve.wait_ge(s_sq, q + 1)
                        do(nc.vector.tensor_reduce(hsum[:, 4 * n:4 * n + 4],
                                                   sqb[:, q % 2, :].rearrange("p (h d) -> p h d", d=P),
                                                   axis=AX.X, op=ALU.add), s_sqc)
                    sync()
                    do(vs(var[:, 0:24], hsum[:, 0:24], 1.0 / P, SUBLN_EPS, ALU.mult, ALU.add), s_var)
                    rsqrt(hsum[:, 0:24], A["var"], 24)
                    do(vs(newt[:, 0:24], hsum[:, 0:24], 1.0 - LAM_INIT, None, ALU.mult))
                    sync()
                    for n, piece in enumerate(pieces):
                        y = piece.rearrange("p b n -> p (b n)").rearrange("p (h d) -> p h d", d=P)
                        do(tt(y, y, newt[:, 8 * n:8 * n + 8].unsqueeze(2).to_broadcast([P, 8, P]), ALU.mult),
                           s_y if n == 2 else None)

            def residual(s, group, first):
                for b in range(4):
                    x = xT[:, first + b, :]
                    do(tt(x, x, ps[4 * (group % 2) + b][:, :], ALU.add), s_free)
                    yield b

            def out_proj(s):
                A = s.at
                if s.prev.diff:
                    for c in range(6):
                        dve.wait_ge(s_hhi, A["hin"] + c + 1)
                        do(stt(h_lo[:, c, :], ps[4 * ((A["group"] + 1) % 2) + c % 4][:, :], vec[:, V_SUB:V_SUB + 1],
                               h_hi[:, c, :].bitcast(F32), ALU.mult, ALU.subtract), s_hlo)
                dve.wait_ge(s_used, A["tile"] + 8)
                for b in residual(s, A["group"], 0):
                    pass
                dve.wait_ge(s_used, A["tile"] + 16)
                for b in residual(s, A["group"] + 1, 4):
                    norm_input(s.next, [b])
                norm_input(s.next, range(4, KT))

            def mlp(s):
                A = s.at
                for half in range(HALVES):
                    t0 = A["tile"] + half * MLP_TILES
                    hid = A["hid"] + half * HID
                    token_norm(s, A["group"] + 1, half)

                    def low(t):
                        dve.wait_ge(s_hidhi, hid + t + 1)
                        do(tt(hid_lo[:, t], hsq[:, t % 2], hid_hi[:, t].bitcast(F32), ALU.subtract), s_hid)

                    for u in range(4):
                        dve.wait_ge(s_used, t0 + 8 * (u + 1))
                        for b in range(4):
                            t = 4 * u + b
                            if hid + t >= 2:
                                dve.wait_ge(s_hsq, hid + t - 1)
                            do(stt(relu[:, t % 2], ps[4 * ((A["group"] + u) % 2) + b][:, :], 0.0, rms_bc[:],
                                   ALU.max, ALU.mult), s_free)
                            if t:
                                low(t - 1)
                    low(HID - 1)
                    early = half == HALVES - 1 and not s.last
                    dve.wait_ge(s_used, t0 + 48)
                    for b in residual(s, A["group"], 0):
                        pass
                    if early:
                        norm_input(s.next, range(4))
                    dve.wait_ge(s_used, t0 + MLP_TILES)
                    for b in residual(s, A["group"] + 1, 4):
                        if early:
                            norm_input(s.next, [4 + b])
                    sync()

            dve.wait_ge(s_in[0], 16)
            dve.wait_ge(s_in[1], 16)
            dve.wait_ge(s_in[5], 16)
            do(nc.vector.tensor_copy(ident_b[:], ident))
            do(nc.vector.tensor_copy(causal_b[:], cst[:, C_CAUSAL:C_CAUSAL + P]))
            do(nc.vector.tensor_copy(chunk_b[:], cst[:, C_CHUNK:C_CHUNK + P]))
            do(nc.vector.tensor_copy(ident_r[:], cst[:, 0:16]))
            do(vs(nsink[:], vec[:, V_SINK:V_SINK + 8], -1.0, None, ALU.mult), s_set)
            for n in range(2):
                a = V_LAM + 128 * n
                do(tt(fz[:, 0:64], vec[:, a:a + 64], vec[:, a + 64:a + 128], ALU.mult))
                sync()
                do(nc.vector.tensor_reduce(lam[:, n:n + 1], fz[:, 0:64], axis=AX.X, op=ALU.add), s_set if n else None)
                sync()
            for s in stages:
                if s.forget:
                    dve.wait_ge(s_seta, 2)
                    do(tt(wf_lo[:], wf_in[:], wf_hi[:].bitcast(F32), ALU.subtract), s_wf)
                {"proj": proj, "attn": attention, "out": out_proj, "mlp": mlp}[s.kind](s)
                if s is stages[0]:
                    dve.wait_ge(s_seta, 1)
                    do(tt(lam[:, 5:6], lam[:, 3:4], lam[:, 2:3], ALU.subtract))
                    sync()
                    do(vs(lam[:, 4:5], lam[:, 5:6], -LAM_INIT, None, ALU.add))



def square_tiles(w, cols=None):
    out = []
    n = 0
    while n < w.shape[1]:
        width = TILE if (cols is None or cols[0] == TILE) else 256
        if cols is not None:
            cols = cols[1:]
        part = w[:, n:n + width]
        if width == TILE:
            out.append(part.reshape(-1, P, TILE))
        else:
            out.append(part.reshape(-1, 2, P, 256).transpose(0, 2, 1, 3).reshape(-1, P, TILE))
        n += width
    return out


def weight_stream(a):
    def mem_kv(l):
        return square_tiles(a["w_mem_kv_2"][l])

    def mlp(up, down):
        out = []
        for h in range(HALVES):
            w = FF // HALVES
            out += square_tiles(up[:, h * w:(h + 1) * w]) + square_tiles(down[h * w:(h + 1) * w])
        return out

    e = a["w_in_even"][0]
    aq, ak, av, bq, bk, bv = np.split(e, [512, 1024, 1536, 2048, 2176], axis=1)
    bq = bq.reshape(D, 2, 4, HD).transpose(0, 2, 1, 3).reshape(D, 512)
    o = a["w_in_odd"][0]
    b0 = a["a_w_in_2"][0]
    parts = mem_kv(0) + mem_kv(1)
    parts += square_tiles(np.concatenate([aq, ak, bq, bk, bv, av], 1), [TILE] * 3 + [256, TILE])
    parts += square_tiles(a["w_out_even"][0]) + mlp(a["w_up"][0], a["w_down"][0])
    parts += square_tiles(o[:, :3072]) + square_tiles(a["w_out_odd"][0]) + mlp(a["w_up"][1], a["w_down"][1])
    gate_b, gate_c, hv, qm = np.split(b0, [768, 1536, 2304], axis=1)
    parts += square_tiles(qm, [256]) + square_tiles(np.concatenate([gate_c, hv, gate_b], 1), [TILE] * 4 + [256])
    parts += square_tiles(a["w_o_2"][0]) + mlp(a["w_up_2"][0], a["w_down_2"][0])
    parts += square_tiles(a["b_w_q_2"][0]) + square_tiles(a["w_kv_2"])
    parts += square_tiles(a["w_o_2"][1]) + mlp(a["w_up_2"][1], a["w_down_2"][1])
    parts.append(parts[-1][:RING])
    w = np.concatenate(parts, 0)
    return np.ascontiguousarray(w.reshape(-1, 2, P, TILE).transpose(0, 2, 1, 3))


def kernel(**inputs):
    import concourse.bacc as _bacc
    from concourse import mybir as _mybir
    from concourse.bass_utils import run_bass_kernel_spmd as _run

    a = {k: np.asarray(v) for k, v in inputs.items()}

    def column(v):
        return v.reshape(-1, P).T

    def across(v):
        return np.broadcast_to(v.reshape(1, -1), (P, v.size))

    vecs = [column(a["g_mix"][0]), column(a["g_mix"][1]), column(a["g_mlp"][0]), column(a["g_mlp"][1]),
            column(a["norm_mix_2"][0]), column(a["norm_mix_2"][1]), column(a["norm_mlp_2"][0]),
            column(a["norm_mlp_2"][1]), column(a["kv_norm_2"]), column(a["mem_norm_2"]),
            column(a["a_conv_2"][0].reshape(-1)), column(a["b_subln_2"][0])]
    vecs += [across(v) for v in (
        a["a_q_gain"], a["a_k_gain"], a["b_q_gain"], a["b_k_gain"], a["c_q_gain"], a["c_k_gain"],
        a["b_q_norm_2"], a["k_norm_2"], a["mem_q_norm_2"][0], a["mem_q_norm_2"][1],
        a["mem_k_norm_2"][0], a["mem_k_norm_2"][1], a["b_sinks"], a["b_forget"], a["b_lam_2"])]
    arrays = {
        "in_weights": weight_stream(a),
        "in_forget": np.ascontiguousarray(
            a["w_in_odd"][0][:, 3072:].reshape(KT, P, 16).transpose(1, 0, 2).reshape(P, -1)),
        "in_x": np.ascontiguousarray(a["x"][0].T),
        "in_mem": np.ascontiguousarray(a["mem_2"][0].T),
        "in_consts": constants(),
        "in_vecs": np.ascontiguousarray(np.concatenate(vecs, 1)),
    }
    nc = _bacc.Bacc("TRN2", target_bir_lowering=False, num_devices=1)
    args = [nc.dram_tensor(n, x.shape, _mybir.dt.from_np(x.dtype), kind="ExternalInput").ap()
            for n, x in arrays.items()]
    out = nc.dram_tensor("out_xT", (D, SEQ), _mybir.dt.float32, kind="ExternalOutput").ap()
    build(nc, *args, out)
    r = _run(nc, [arrays], core_ids=[0])
    y = r.results[0]["out_xT"]
    return np.ascontiguousarray(y.T).reshape(1, SEQ, D)
```

```python
import numpy as np
import concourse.bass as bass
from concourse import mybir
from contextlib import ExitStack

F32 = mybir.dt.float32
F32R = mybir.dt.float32r
BF16 = mybir.dt.bfloat16
ALU = mybir.AluOpType
ACT = mybir.ActivationFunctionType
AX = mybir.AxisListType

P = 128
D = 1024
SEQ = 512
MEM = 256
FF = 4096
KT = D // P
TB = SEQ // P
HD = 64
TILE = 512
EPS = 1e-6
SUBLN_EPS = 1e-5
BIG = 1e30
LAM_INIT = 0.8 - 0.6 * float(np.exp(-0.3 * 1))
RING = 8
PAIRS = 4
HALVES = 2
HID = FF // HALVES // P

C_IDENT, C_MEAN, C_DELTA, C_LOGW, C_WIN, C_TRI, C_CAUSAL, C_CHUNK, C_COS, C_SIN = (
    0, 128, 256, 768, 1280, 1536, 2048, 2176, 2304, 2336)
C_ALL = 2368
V_GAIN = {n: 8 * i for i, n in enumerate(
    ["mix0", "mix1", "mlp0", "mlp1", "mixb0", "mixb1", "mlpb0", "mlpb1", "kv", "mem"])}
V_CONV = 80
V_SUB = 98
V_HEAD = {n: 99 + HD * i for i, n in enumerate(
    ["aq", "ak", "bq", "bk", "cq", "ck", "dq", "dk", "mq0", "mq1", "mk0", "mk1"])}
V_SINK = 99 + 12 * HD
V_FORGET = V_SINK + 8
V_LAM = V_FORGET + 16
V_COLUMN = {n: V_LAM + 256 + i for i, n in enumerate(V_HEAD)}
V_ALL = V_LAM + 256 + len(V_COLUMN)
DILATIONS = ((128, 1), (512, 4), (2048, 16))


def constants():
    c = np.zeros((P, C_ALL), np.float32)
    p = np.arange(P)[:, None]
    c[:, C_IDENT:C_IDENT + P] = np.eye(P)
    c[:, C_MEAN:C_MEAN + P] = 1.0 / D
    dist = p - np.arange(512)[None] + 384
    c[:, C_DELTA:C_DELTA + 512] = dist
    times = sum(((dist % d == 0) & (dist <= w)).astype(np.float64) for w, d in DILATIONS)
    ok = (dist >= 0) & (times > 0)
    c[:, C_LOGW:C_LOGW + 512] = np.where(ok, -np.log(np.maximum(times, 1)), BIG)
    near = p - np.arange(256)[None] + 128
    c[:, C_WIN:C_WIN + 256] = np.where((near >= 0) & (near < 128), 0.0, BIG)
    c[:, C_TRI:C_TRI + 512] = p <= np.arange(512)[None]
    f = np.arange(P)[None]
    c[:, C_CAUSAL:C_CAUSAL + P] = np.where(f > p, BIG, 0.0)
    c[:, C_CHUNK:C_CHUNK + P] = np.where(f // 64 > p // 64, BIG, 0.0)
    half = 8
    inv = (1.0 / (np.float32(500000.0) ** (np.arange(0, 16, 2, dtype=np.float32) / np.float32(16)))).astype(np.float32)
    ang = (np.arange(SEQ, dtype=np.float32)[:, None] * inv[None]).astype(np.float32)
    for at, fn in ((C_COS, np.cos), (C_SIN, np.sin)):
        c[:, at:at + TB * half] = fn(ang).astype(np.float32).reshape(TB, P, half).transpose(1, 0, 2).reshape(P, -1)
    return c


class Group:

    def __init__(self, form, width=TILE, heads=0, gains=(), rope=0, qk=(), scale=1.0, v=None, t=None):
        self.form = form
        self.width = width
        self.slots = 8 if width == TILE else 4
        self.heads = heads
        self.gains = gains
        self.rope = rope
        self.qk = qk
        self.scale = scale
        self.ahead = None
        self.v = v
        self.t = t


class Stage:
    def __init__(self, kind, **kw):
        self.kind = kind
        self.norm = kw.get("norm")
        self.groups = kw.get("groups", [])
        self.mem = kw.get("mem", False)
        self.rbc = kw.get("rbc", False)
        self.forget = kw.get("forget", False)
        self.heads = kw.get("heads", [])
        self.diff = kw.get("diff", False)
        self.z = kw.get("z", 0)
        self.last = kw.get("last", False)


class Head:

    def __init__(self, qs, ks, row, keys, v, tile=None, base=0, piece=None,
                 shared=None, bias=None, slope=0.0, mask=None, sink=None, forget=None):
        self.qs, self.ks = qs, ks
        self.shared = shared
        self.row = row
        self.v = v
        self.tile, self.base = tile, base
        self.piece = piece
        self.bias, self.slope, self.mask, self.sink, self.forget = bias, slope, mask, sink, forget
        self.inverse = {}
        self.lo = [k[0] for k in keys]
        self.n = [P * (k[1] - k[0]) for k in keys]
        self.w = [n + (sink is not None) for n in self.n]
        self.at_p = [sum(self.w[:i]) for i in range(TB)]
        last = max(k[1] for k in keys)
        self.queries = [[i for i, k in enumerate(keys) if k[0] <= j < k[1]] for j in range(last)]
        self.at_t = [P * sum(len(q) for q in self.queries[:j]) for j in range(last)]


MLP_TILES = 64
MLP_GROUPS = 6
TURN = dict(tile=MLP_TILES, group=MLP_GROUPS, free=24, stat=1, var=1, hid=HID, bc=1,
            rn=1)


def build(nc, w_all, w_f, x_t, mem_t, consts_d, vecs_d, out_t):
    ctx = ExitStack()
    with ctx:
        def sb(name, shape, dt=F32, where=ctx):
            return where.enter_context(nc.sbuf_tensor(name, shape, dt))

        def sem(name):
            return ctx.enter_context(nc.semaphore(name))

        xT = sb("xT", [P, KT, SEQ])
        stage_w = sb("stage_w", [P, PAIRS, 2, TILE])
        w_hi = sb("w_hi", [P, RING, TILE], F32R)
        w_lo = sb("w_lo", [P, RING, TILE], F32R)
        cst = sb("cst", [P, C_ALL])
        vec = sb("vec", [P, V_ALL])
        mem_kT = sb("mem_kT", [P, 2, 2, MEM])
        mem_v = sb("mem_v", [P, 2, 2, MEM])
        only = ExitStack()
        norm_r = sb("norm_r", [P, 4, SEQ], F32R, only)
        only.close()
        rms_bc = sb("rms_bc", [P, SEQ])
        ssum = sb("ssum", [P, SEQ])
        sqb = sb("sqb", [P, 2, SEQ])
        wf_in = sb("wf_in", [P, P])
        wf_hi = sb("wf_hi", [P, P], F32R)
        wf_lo = sb("wf_lo", [P, P], F32R)
        c_hi = sb("c_hi", [16, SEQ], F32R)
        c_lo = sb("c_lo", [16, SEQ], F32R)
        ident_r = sb("ident_r", [P, 16], F32R)
        ident_b = sb("ident_b", [P, P], BF16)
        causal_b = sb("causal_b", [P, P], BF16)
        rn = sb("rn", [P, TB])
        var = sb("var", [P, 32])
        root = sb("root", [P, 32])
        inv = sb("inv", [P, 32])
        newt = sb("newt", [P, 32])
        hsum = sb("hsum", [P, 32])
        fz = sb("fz", [P, 64])
        fa = sb("fa", [P, 64])
        fe = sb("fe", [P, 64])
        fl = sb("fl", [P, 64])
        mneg = sb("mneg", [P, 16])
        den = sb("den", [P, 16])
        rden = sb("rden", [P, 16])
        lden = sb("lden", [P, 16])
        nsink = sb("nsink", [P, 8])
        lam = sb("lam", [P, 8])
        q_gain = sb("q_gain", [P, len(V_COLUMN)])
        h_hi = sb("h_hi", [P, KT, SEQ], F32R)
        h_lo = sb("h_lo", [P, KT, SEQ], F32R)
        only = ExitStack()
        hid_hi = sb("hid_hi", [P, HID, SEQ], F32R, only)
        hid_lo = sb("hid_lo", [P, HID, SEQ], F32R, only)
        relu = sb("relu", [P, 2, SEQ], F32, only)
        hsq = sb("hsq", [P, 2, SEQ], F32, only)
        only.close()
        only = ExitStack()
        arena_r = sb("arena_r", [P, 18, 1024], F32R, only)
        only.close()
        arena = sb("arena", [P, 18 * 1024])
        qT = arena[:, 0:4096].rearrange("p (j n) -> p j n", j=KT)
        kT = arena[:, 4096:8192].rearrange("p (j n) -> p j n", j=KT)
        vN = arena[:, 8192:12288].rearrange("p (b n) -> p b n", b=TB)
        vD = arena[:, 8192:11264].rearrange("p (b n) -> p b n", b=TB)
        uP = arena[:, 8192:8192 + 6 * 514].rearrange("p (j n) -> p j n", j=6)
        rope_t = arena[:, 11264:12288].rearrange("p (k n) -> p k n", k=4)
        tn = arena[:, 12288:16384].rearrange("p (a b n) -> p a b n", a=2, b=TB)
        prob = arena[:, 12288:14848].rearrange("p (a n) -> p a n", a=2)
        probT = arena[:, 14848:17408].rearrange("p (a n) -> p a n", a=2)
        bias_t = arena[:, 17408:18432].rearrange("p (a n) -> p a n", a=2)
        bias_f = cst[:, C_DELTA:C_DELTA + 2 * SEQ].rearrange("p (a n) -> p a n", a=2)
        bias_c = ssum
        second = [sqb[:, 0, :], sqb[:, 1, :], rms_bc]
        pieces = [arena[:, a:a + 1024].rearrange("p (b n) -> p b n", b=TB) for a in (7168, 11264, 17408)]

        ps = [ctx.enter_context(nc.psum_tensor(f"ps{i}", [P, 512], F32)) for i in range(8)]

        ident = cst[:, C_IDENT:C_IDENT + P]
        mean_w = cst[:, C_MEAN:C_MEAN + P]

        s_in = [sem(f"s_in{i}") for i in range(6)]
        s_mem = [sem(f"s_mem{i}") for i in range(PAIRS)]
        s_load = [sem(f"s_load{i}") for i in range(PAIRS)]
        s_whi = sem("s_whi")
        s_wlo = sem("s_wlo")
        s_used = sem("s_used")
        s_free = sem("s_free")
        s_hhi = sem("s_hhi")
        s_hlo = sem("s_hlo")
        s_sq = sem("s_sq")
        s_sqc = sem("s_sqc")
        s_stat = sem("s_stat")
        s_var = sem("s_var")
        s_root = sem("s_root")
        s_rn = sem("s_rn")
        s_diag = sem("s_diag")
        s_bc = sem("s_bc")
        s_rbc = sem("s_rbc")
        s_t = sem("s_t")
        s_tr = sem("s_tr")
        s_tra = sem("s_tra")
        s_trv = sem("s_trv")
        s_score = sem("s_score")
        s_qkhi = sem("s_qkhi")
        s_qklo = sem("s_qklo")
        s_k2 = sem("s_k2")
        s_max = sem("s_max")
        s_prob = sem("s_prob")
        s_pn = sem("s_pn")
        s_pt = sem("s_pt")
        s_pta = sem("s_pta")
        s_ptv = sem("s_ptv")
        s_pv = sem("s_pv")
        s_o = sem("s_o")
        s_yr = sem("s_yr")
        s_y = sem("s_y")
        s_hsq = sem("s_hsq")
        s_hidhi = sem("s_hidhi")
        s_hid = sem("s_hid")
        s_wf = sem("s_wf")
        s_fmm = sem("s_fmm")
        s_fabs = sem("s_fabs")
        s_fln = sem("s_fln")
        s_flog = sem("s_flog")
        s_fbc = sem("s_fbc")
        s_fb = sem("s_fb")
        s_cmm = sem("s_cmm")
        s_z = sem("s_z")
        s_chi = sem("s_chi")
        s_clo = sem("s_clo")
        s_set = sem("s_set")
        s_seta = sem("s_seta")
        s_act = sem("s_act")
        s_dve = sem("s_dve")
        s_pool = sem("s_pool")
        s_out = sem("s_out")

        def tiles(tensor, first, n):
            return [tensor[:, first + j, :] for j in range(n)]

        def v_to(first):
            return lambda b, w: vN[:, b, first:first + w]

        ATT = -(HD ** -0.5)
        def head_gain(g):
            c = V_COLUMN[g.gains[0][2]]
            if g.scale == 1.0:
                return vec[:, c:c + 1]
            return q_gain[:, c - V_LAM - 256:c - V_LAM - 255]

        stages = []
        stages.append(Stage("proj", norm="mem", mem=True, groups=[
            Group("N", heads=4, gains=((0, 4, f"mk{l}"),), qk=[mem_kT[:, l, c, :] for c in range(2)],
                  v=(lambda l: lambda b, w: mem_v[:, l, b, :])(l)) for l in range(2)]))
        stages.append(Stage("proj", norm="mix0", groups=[
            Group("N", heads=8, gains=((0, 8, "aq"),), qk=tiles(qT, 0, 4), scale=ATT),
            Group("N", heads=8, gains=((0, 8, "ak"),), qk=tiles(kT, 0, 4)),
            Group("N", heads=8, gains=((0, 8, "bq"),), qk=tiles(qT, 4, 4), scale=ATT),
            Group("N", width=256, heads=2, gains=((0, 2, "bk"),), qk=tiles(kT, 4, 1), v=v_to(512)),
            Group("N", v=v_to(0))]))

        def rows(tensor, tile, base):
            return tensor[base:base + HD, tile, :]

        causal = [(0, i + 1) for i in range(TB)]
        near = [(max(0, i - 1), i + 1) for i in range(TB)]
        slopes = [float(np.float32(2.0 ** (-8.0 * i / 16))) for i in range(1, 17)]

        def v_from(tensor, first, width=HD):
            return lambda j: tensor[:, j, first:first + width]

        heads = [Head([rows(qT, h // 2, HD * (h % 2))], [rows(kT, h // 2, HD * (h % 2))], HD * (h % 2), causal,
                      v_from(vN, HD * h), h // 2, HD * (h % 2), bias="dilated", slope=slopes[8 + h])
                 for h in range(8)]
        heads += [Head([rows(qT, 4 + h % 4, HD * (h // 4))], [rows(kT, 4, HD * (h // 4))], HD * (h // 4), near,
                       v_from(vN, 512 + HD * (h // 4)), 4 + h // 2, HD * (h % 2), bias="window",
                       slope=slopes[h], sink=h, shared=h // 4) for h in range(8)]
        stages.append(Stage("attn", heads=heads))
        stages.append(Stage("out"))
        stages.append(Stage("mlp", norm="mlp0"))
        stages.append(Stage("proj", norm="mix1", forget=True, groups=[
            Group("N", heads=8, gains=((0, 8, "cq"),), qk=tiles(qT, 0, 4), scale=ATT),
            Group("N", heads=8, gains=((0, 8, "cq"),), qk=tiles(qT, 4, 4), scale=ATT),
            Group("N", heads=8, gains=((0, 8, "ck"),), qk=tiles(kT, 0, 4)),
            Group("N", heads=8, gains=((0, 8, "ck"),), qk=tiles(kT, 4, 4)),
            Group("N", v=v_to(0)), Group("N", v=v_to(512))]))
        stages.append(Stage("attn", heads=[
            Head([rows(qT, h // 2, HD * (h % 2))], [rows(kT, h // 2, HD * (h % 2))], HD * (h % 2), causal,
                 v_from(vN, HD * h), h // 2, HD * (h % 2), mask=causal_b, bias="forget", forget=h) for h in range(16)]))
        stages.append(Stage("out"))
        stages.append(Stage("mlp", norm="mlp1"))

        def memory_heads(layer):
            return [Head([rows(qT, 6 + h // 2, HD * (h % 2))],
                         [mem_kT[HD * (h % 2):HD * (h % 2) + HD, layer, h // 2, :]], HD * (h % 2), [(0, 2)] * TB,
                         (lambda l, h: lambda j: mem_v[:, l, j, HD * h:HD * h + HD])(layer, h),
                         6 + h // 2, HD * (h % 2)) for h in range(4)]

        c_t = [("c", j) for j in range(6)] + [("h", j) for j in range(6)] + [("b", j) for j in range(6)]
        stages.append(Stage("proj", norm="mixb0", rbc=True, groups=[
            Group("T", t=c_t[0:4]),
            Group("N", width=256, heads=4, gains=((0, 4, "mq0"),), qk=tiles(qT, 6, 2), scale=ATT),
            Group("T", t=c_t[4:8]), Group("T", t=c_t[8:12]),
            Group("T", t=c_t[12:16]), Group("T", width=256, t=c_t[16:18])]))
        stages.append(Stage("attn", heads=memory_heads(0), z=6))
        stages.append(Stage("out"))
        stages.append(Stage("mlp", norm="mlpb0"))
        stages.append(Stage("proj", norm="mixb1", groups=[
            Group("N", heads=8, gains=((0, 8, "dq"),), rope=8, qk=tiles(qT, 0, 4), scale=ATT),
            Group("N", heads=8, gains=((0, 4, "dq"), (4, 4, "mq1")), rope=4, qk=tiles(qT, 4, 4), scale=ATT)]))
        stages.append(Stage("proj", norm="kv", groups=[
            Group("N", heads=8, gains=((0, 8, "dk"),), rope=8, qk=tiles(kT, 0, 4)),
            Group("N", heads=4, gains=((0, 4, "dk"),), rope=4, qk=tiles(kT, 4, 2),
                  v=lambda b, w: vD[:, b, 0:w]),
            Group("N", v=lambda b, w: vD[:, b, 256:256 + w])]))
        stages.append(Stage("attn", diff=True, heads=[
            Head([rows(qT, 3 * n + h // 2, HD * (h % 2)) for n in range(2)],
                 [rows(kT, 3 * n + h // 2, HD * (h % 2)) for n in range(2)], HD * (h % 2), causal,
                 v_from(vD, P * h, P), piece=h, bias="chunk") for h in range(6)] + memory_heads(1)))
        stages.append(Stage("out"))
        stages.append(Stage("mlp", norm="mlpb1", last=True))

        tiles_r = arena_r[:].rearrange("p a (b n) -> p (a b) n", b=2)
        for s in stages:
            if s.kind == "attn":
                two = 13 if s.heads[0].bias == "dilated" else 34
                free = ([t[:, j, :] for j in range(6) for t in (h_hi, h_lo)] if s.diff else
                        [tiles_r[:, two + j, :] for j in range(2)] + [norm_r[:, j, :] for j in (1, 2, 3, 0)])
                s.slots = [free[n:n + 3] for n in range(0, len(free), 3)]

        for n, s in enumerate(stages):
            s.late = s.kind == "attn" and (s.heads[0].bias == "dilated" or s.z > 0)
            s.early = s.kind == "attn" and not s.diff
            if s.early:
                before = stages[n - 1].groups
                g = [i for i, g in enumerate(before) if g.heads][-1]
                before[g].ahead = s
        at = dict(tile=0, group=0, free=0, hin=0, sq=0, stat=0, var=0, bc=0, t=0, tra=0, trv=0, rn=0,
                  sm=0, unit=0, head=0, split=0, k2=0, pt=0, pta=0, ptv=0, hid=0, tr=0)
        carry = None
        x_free = 0
        for n, s in enumerate(stages):
            s.prev, s.next = (stages[n - 1] if n else None), (stages[n + 1] if n + 1 < len(stages) else None)
            s.at = dict(at)
            s.carry = carry
            s.x_free = x_free
            s.h_free = 0 if n < 2 else at["tile"] - (32 if s.prev.kind == "mlp" else 0)
            if s.norm:
                at["hin"] += 8
                at["sq"] += 8
            if carry:
                carry.sq0 = at["sq"]
                at["sq"] += carry.blocks
                carry = None
            if s.kind == "proj":
                at["stat"] += 1
                at["rn"] += 1
                at["var"] += 1
                at["bc"] += s.rbc
                for g in s.groups:
                    g.blocks = (len(g.t) if g.form == "T" else 2 if s.mem else TB)
                    g.tile0, g.grp, g.free0, g.var, g.t0 = at["tile"], at["group"], at["free"], at["var"], at["t"]
                    g.tra0, g.trv0, g.sq0, g.tr0 = at["tra"], at["trv"], at["sq"], at["tr"]
                    g.end = g.tile0 + g.slots
                    at["tile"] += g.slots
                    at["group"] += 1
                    at["free"] += g.blocks
                    if g.heads:
                        if g is s.groups[-1]:
                            carry = g
                        else:
                            at["sq"] += g.blocks
                        at["var"] += 1
                        at["t"] += g.rope > 0
                        at["tr"] += 1
                        at["tra"] += (len(g.qk) + 1) // 2
                        at["trv"] += len(g.qk) // 2
                assert not carry or stages[n + 1].kind == "proj"
            elif s.kind == "attn":
                units = []
                uses = []

                def take(freed):
                    uses.append(freed)
                    k = len(uses) - 1
                    return k % 3, uses[k - 3] if k >= 3 else None

                for place, h in enumerate(s.heads):
                    h.sm0, h.unit0, h.idx, h.pt0 = at["sm"], at["unit"], at["head"], at["pt"]
                    if h.bias == "forget":
                        h.fb = place + 1
                        h.fbank = take((s_fb, h.fb))
                    h.bank = [take((s_max if h.bias else s_prob, h.sm0 + k + 1)) for k in range(TB * len(h.qs))]
                    h.copied = []
                    for j in range(len(h.queries)):
                        at["pt"] += 1
                        at["ptv" if j % 2 else "pta"] += 1
                        h.copied.append((s_ptv, at["ptv"]) if j % 2 else (s_pta, at["pta"]))
                    h.splits = []
                    for m in range(len(h.qs)):
                        u = len(units)
                        old = units[u - len(s.slots)] if u >= len(s.slots) else None
                        at["split"] += 1
                        same = bool(old) and h.shared is not None and old[1] == h.shared
                        at["k2"] += not same
                        h.splits.append(dict(copies=at["k2"], same=same, slot=s.slots[u % len(s.slots)], ready=at["split"],
                                             used=old[0] if old else None))
                        units.append((h.sm0 + (TB - 1) * len(h.qs) + m + 1, h.shared))
                    at["sm"] += TB * len(h.qs)
                    at["unit"] += TB
                    at["head"] += 1
                    if h.piece is None and h.base:
                        at["hin"] += 1
                        h.hin = at["hin"] + min(place + 3, s.z)
                at["hin"] += s.z
                if s.diff:
                    at["sq"] += 6
                    at["var"] += 1
            elif s.kind == "out":
                if s.prev.diff:
                    at["hin"] += 6
                    at["tr"] += 6
                at["tile"] += 16
                at["group"] += 2
                at["free"] += 8
            else:
                for k, d in TURN.items():
                    if k in at:
                        at[k] += HALVES * d
            if s.kind in ("out", "mlp"):
                x_free = at["free"]
        TOTAL = at["tile"]
        LOADED = TOTAL + 8
        assert LOADED == w_all.shape[0] * 2, (LOADED, w_all.shape)

        class Order:

            def __init__(self, eng, step):
                self.eng, self.step, self.n, self.last = eng, step, {}, None

            def do(self, ins, signal=None):
                self.last = signal or self.step
                ins.then_inc(self.last, 1)
                self.n[id(self.last)] = self.n.get(id(self.last), 0) + 1

            def mark(self):
                return self.last, self.n[id(self.last)]

            def sync(self):
                self.eng.wait_ge(self.last, self.n[id(self.last)])

        block = ctx.enter_context(nc.Block())

        @block.sync
        def _(sp):
            sp.dma_start(vec[:, 0:V_CONV], vecs_d[:, 0:V_CONV]).then_inc(s_in[1], 16)
            mem = mem_t.rearrange("(k p) n -> p k n", p=P)
            for q in range(PAIRS):
                sp.dma_start(kT[:, 2 * q:2 * q + 2, 0:MEM], mem[:, 2 * q:2 * q + 2, :]).then_inc(s_mem[q], 16)
                sp.dma_start(stage_w[:, q], w_all[q]).then_inc(s_load[q], 16)
            sp.dma_start(cst[:, 0:C_DELTA], consts_d[:, 0:C_DELTA]).then_inc(s_in[0], 16)
            whole = LOADED // RING
            x = x_t.rearrange("(k p) n -> p k n", p=P)
            for q in range(PAIRS):
                sp.wait_ge(s_wlo, 2 * q + 2)
                sp.dma_start(stage_w[:, q], w_all[PAIRS + q]).then_inc(s_load[q], 16)
            sp.dma_start(vec[:, V_CONV:], vecs_d[:, V_CONV:]).then_inc(s_in[5], 16)
            for q in range(PAIRS):
                sp.dma_start(xT[:, 2 * q:2 * q + 2, :], x[:, 2 * q:2 * q + 2, :]).then_inc(s_in[3], 16)
            sp.dma_start(cst[:, C_DELTA:], consts_d[:, C_DELTA:]).then_inc(s_in[2], 16)
            sp.dma_start(wf_in[:], w_f).then_inc(s_in[4], 16)
            with sp.Fori(2, whole) as c:
                for q in range(PAIRS):
                    sp.wait_ge(s_wlo, c * RING + (2 * q + 2 - RING))
                    sp.dma_start(stage_w[:, q], w_all[c * PAIRS + q]).then_inc(s_load[q], 16)
            for q in range((LOADED - whole * RING) // 2):
                sp.wait_ge(s_wlo, (whole - 1) * RING + 2 * q + 2)
                sp.dma_start(stage_w[:, q], w_all[whole * PAIRS + q]).then_inc(s_load[q], 16)
            for n in range(KT):
                sp.wait_ge(s_free, at["free"] - 8 + n + 1)
                sp.dma_start(out_t[n * P:(n + 1) * P, :], xT[:, n, :]).then_inc(s_out, 16)
            sp.wait_ge(s_out, 16 * KT)

        @block.gpsimd
        def _(pool):
            def low(slot, ready):
                pool.wait_ge(s_whi, ready)
                nc.gpsimd.tensor_tensor(w_lo[:, slot], stage_w[:, slot // 2, slot % 2],
                                        w_hi[:, slot].bitcast(F32), ALU.subtract).then_inc(s_wlo, 1)

            def lows(n, limit):
                while n < limit and n % RING:
                    low(n % RING, n + 1)
                    n += 1
                rounds = (limit - n) // RING
                if rounds > 1:
                    with pool.Fori(0, rounds) as c:
                        for j in range(RING):
                            low(j, c * RING + (n + j + 1))
                    n += rounds * RING
                for m in range(n, limit):
                    low(m % RING, m + 1)

            def split_lo(h, m):
                d = h.splits[m]
                q2, k2, klo = d["slot"]
                own, other = slice(h.row, h.row + HD), slice(HD - h.row, 2 * HD - h.row)
                nk = h.ks[m].shape[-1]
                pool.wait_ge(s_qkhi, d["ready"])
                if order.last:
                    sync()
                do(nc.gpsimd.tensor_tensor(q2[other, :], h.qs[m], q2[own, :].bitcast(F32), ALU.subtract),
                   s_qklo if d["same"] else None)
                sync()
                if not d["same"]:
                    do(nc.gpsimd.tensor_tensor(klo[own, 0:nk], h.ks[m], k2[own, 0:nk].bitcast(F32), ALU.subtract),
                       s_qklo)
                    sync()

            order = Order(pool, s_pool)
            do, sync = order.do, order.sync
            done = 0
            for s in stages:
                for gi, g in enumerate(s.groups):
                    if g.ahead:
                        nxt = s.groups[gi + 1]
                        limit = nxt.tile0 + nxt.slots * 3 // 4 + RING
                        lows(done, limit)
                        done = limit
                        pool.wait_ge(s_wlo, done)
                        split_lo(g.ahead.heads[0], 0)
                        sync()
                if s.kind == "attn":
                    lows(done, s.at["tile"] + RING)
                    done = s.at["tile"] + RING
                    pool.wait_ge(s_wlo, done)
                    for m in range(0 if s.early else len(s.heads[0].qs)):
                        split_lo(s.heads[0], m)
                    for h in s.heads[1:]:
                        for m in range(len(h.qs)):
                            split_lo(h, m)
                    sync()
                    if s.diff:
                        pool.wait_ge(s_yr, 1)
                        for k, piece in enumerate(pieces):
                            y = piece.rearrange("p b n -> p (b n)").rearrange("p (h d) -> p h d", d=P)
                            do(nc.gpsimd.tensor_tensor(
                                y, y, newt[:, 8 * k:8 * k + 8].unsqueeze(2).to_broadcast([P, 8, P]), ALU.mult), s_y)
            lows(done, LOADED)

        @block.tensor
        def _(pe):
            mm = nc.tensor.matmul
            passes = ((0, 0), (0, 1), (1, 0))

            def bank(group, b):
                return ps[4 * (group % 2) + b]

            def wait_weights(n, i=None, d=0):
                pe.wait_ge(s_wlo, n + 1 if i is None else i * d + (n + 1))

            def group_mm(s, g, k, slot, part, first, last):
                w = (w_hi, w_lo)
                h = (hid_hi, hid_lo) if s.mem else (h_hi, h_lo)
                ins = None
                for b in range(g.blocks):
                    out = bank(g.grp, b)
                    for n, (a, m) in enumerate(passes):
                        st, en = first and n == 0, last and n == 2
                        if g.form == "T":
                            ins = mm(out[:, :], w[a][:, slot, part * 256 + b * P:part * 256 + b * P + P],
                                     h[m][:, k, :], start=st, stop=en)
                        else:
                            ins = mm(out[:, 0:g.width], h[a][:, k, b * P:(b + 1) * P],
                                     w[m][:, slot, part * 256:part * 256 + g.width], start=st, stop=en)
                return ins

            def stat_mm(s, to):
                ins = None
                for b in range(2 if s.mem else TB):
                    ins = mm(to[:, b:b + 1], ssum[:, b * P:(b + 1) * P], mean_w[:, 0:1], start=True, stop=True)
                ins.then_inc(s_stat, 1)

            def bc_mm(to):
                for b in range(TB):
                    ins = mm(to[:, b * P:(b + 1) * P], mean_w, rms_bc[:, b * P:(b + 1) * P],
                             start=True, stop=True)
                ins.then_inc(s_bc, 1)

            def transposes(g):
                if g.rope:
                    pe.wait_ge(s_t, g.t0 + 1)
                pe.wait_ge(s_free, g.free0 + g.blocks)
                for c in range(len(g.qk)):
                    for b in range(g.blocks):
                        ins = nc.tensor.transpose(bank(g.grp, c)[:, b * P:(b + 1) * P],
                                                  tn[:, g.grp % 2, b, c * P:(c + 1) * P], ident)
                ins.then_inc(s_tr, 1)

            def proj(s):
                A = s.at
                other = s.groups[0].grp + 1
                for gi, g in enumerate(s.groups):
                    prev = s.groups[gi - 1] if gi else s.carry
                    before = (s.groups[gi - 2] if gi > 1 else s.carry if gi else
                              s.prev.groups[-2] if s.carry else None)
                    need = g.free0 - (prev.blocks if prev else 4 if s.prev else 0)
                    if need:
                        pe.wait_ge(s_free, need)
                    if gi == 1:
                        pe.wait_ge(s_rn, A["rn"] + 1)
                        if s.rbc:
                            pe.wait_ge(s_rbc, A["bc"] + 1)
                        if s.forget:
                            pe.wait_ge(s_fabs, 1)
                    if before and before.heads:
                        pe.wait_ge(s_tra, before.tra0 + (len(before.qk) + 1) // 2)
                        if len(before.qk) > 1:
                            pe.wait_ge(s_trv, before.trv0 + len(before.qk) // 2)
                    parts = TILE // g.width
                    for j in range(g.slots):
                        wait_weights(g.tile0 + j)
                        for part in range(parts):
                            k = j * parts + part
                            if gi == 0:
                                pe.wait_ge(s_hlo, A["hin"] + k + 1)
                            ins = group_mm(s, g, k, (g.tile0 + j) % RING, part, k == 0, k == KT - 1)
                        ins.then_inc(s_used, 1)
                        if gi == 0 and j == g.slots * 3 // 4 - 1:
                            pe.wait_ge(s_sqc, A["sq"] + 8)
                            if s.prev:
                                pe.wait_ge(s_free, g.free0)
                            else:
                                pe.wait_ge(s_in[0], 16)
                            stat_mm(s, bank(other, 0))
                        if gi and prev.heads and j == g.slots * 3 // 4 - 1:
                            transposes(prev)
                        if s.forget and gi == 5 and j == 2:
                            pe.wait_ge(s_flog, 1)
                            pe.wait_ge(s_free, g.free0)
                            for b in range(TB):
                                cm = mm(bank(g.grp + 1, 0)[0:16, b * P:SEQ], fl[:, b * 16:(b + 1) * 16],
                                        cst[:, C_TRI:C_TRI + SEQ - b * P], start=b == 0, stop=b == TB - 1)
                            cm.then_inc(s_cmm, 1)
                    if gi == 0 and s.rbc:
                        pe.wait_ge(s_diag, A["bc"] + 1)
                        bc_mm(bank(other, 3))
                    if gi == 0 and s.forget:
                        pe.wait_ge(s_wf, 1)
                        for b in range(TB):
                            for k in range(KT):
                                for n, (a, m) in enumerate(passes):
                                    fm = mm(bank(other, 2)[:, b * 16:(b + 1) * 16],
                                            (h_hi, h_lo)[a][:, k, b * P:(b + 1) * P],
                                            (wf_hi, wf_lo)[m][:, k * 16:(k + 1) * 16],
                                            start=k == 0 and n == 0, stop=k == KT - 1 and n == 2)
                        fm.then_inc(s_fmm, 1)
                    if gi == 0 and s.carry:
                        pe.wait_ge(s_rn, A["rn"] + 1)
                        transposes(s.carry)

            def attention(s):
                A = s.at
                pe.wait_ge(s_set, 1)
                pe.wait_ge(s_free, A["free"])
                pe.wait_ge(s_tra, A["tra"])
                pe.wait_ge(s_trv, A["trv"])
                if s.heads[0].forget is not None:
                    pe.wait_ge(s_clo, 1)

                def scores(h, i, m):
                    sm = h.sm0 + i * len(h.qs) + m
                    n, first = h.n[i], h.lo[i] * P
                    at_bank, freed = h.bank[sm - h.sm0]
                    out = ps[at_bank]
                    if freed:
                        pe.wait_ge(*freed)
                    plain = h.mask is None
                    d = h.splits[m]
                    q2, k2, klo = d["slot"]
                    own = slice(h.row, h.row + HD)
                    pe.wait_ge(s_qklo, d["ready"])
                    pe.wait_ge(s_k2, d["copies"])
                    mm(out[:, 0:n], q2[:, i * P:(i + 1) * P], k2[:, first:first + n], start=True, stop=False)
                    ins = mm(out[:, 0:n], q2[own, i * P:(i + 1) * P], klo[own, first:first + n],
                             start=False, stop=plain)
                    if h.sink is not None:
                        ins = mm(out[:, n:n + 1], ident, nsink[:, h.sink:h.sink + 1], start=True, stop=True)
                    if h.mask is not None:
                        ins = mm(out[:, n - P:n], ident_b[:], h.mask[:], start=False, stop=True)
                    ins.then_inc(s_score, 1)

                def forget_bias(h):
                    at_bank, freed = h.fbank
                    if freed:
                        pe.wait_ge(*freed)
                    sel = ident_r[0:16, h.forget:h.forget + 1].to_broadcast([16, P])
                    mm(ps[at_bank][:, :], sel, c_hi[:], start=True, stop=False)
                    mm(ps[at_bank][:, :], sel, c_lo[:], start=False, stop=True).then_inc(s_fbc, 1)

                def turn(h, j):
                    if j == 0:
                        pe.wait_ge(s_pn, h.unit0 + TB)
                    if h.idx > A["head"]:
                        before = s.heads[h.idx - A["head"] - 1]
                        if j < len(before.queries):
                            pe.wait_ge(*before.copied[j])
                    for n, i in enumerate(h.queries[j]):
                        a = h.at_p[i] + (j - h.lo[i]) * P
                        ins = nc.tensor.transpose(ps[3 + j][:, n * P:(n + 1) * P], prob[:, h.idx % 2, a:a + P], ident)
                    ins.then_inc(s_pt, 1)

                def free_output(h):
                    if h.idx > A["head"]:
                        before = s.heads[h.idx - A["head"] - 1]
                        if before.piece is not None:
                            pe.wait_ge(s_o, before.piece + 1)
                        else:
                            pe.wait_ge(s_hlo, before.hin)

                def piece_values(h):
                    for j in range(TB):
                        pe.wait_ge(*h.copied[j])
                    free_output(h)
                    for i in range(TB):
                        for k in range(i + 1):
                            a = h.at_t[k] + (i - k) * P
                            ins = mm(ps[7][:, i * P:(i + 1) * P], probT[:, h.idx % 2, a:a + P], h.v(k),
                                     start=k == 0, stop=k == i)
                    ins.then_inc(s_pv, 1)

                def values(pair, j):
                    last = j == len(pair[0].queries) - 1
                    for h in pair:
                        pe.wait_ge(*h.copied[j])
                    if j == 0:
                        free_output(pair[0])
                    if len(pair[0].queries[0]) == TB:
                        for h in pair:
                            q = h.queries[j]
                            t = probT[:, h.idx % 2, h.at_t[j]:h.at_t[j] + P * len(q)]
                            ins = mm(ps[7][h.base:h.base + HD, q[0] * P:SEQ], h.v(j), t, start=j == 0, stop=last)
                            if last:
                                ins.then_inc(s_pv, 1)
                    elif last:
                        for i in range(TB):
                            for k in range(pair[0].lo[i], i + 1):
                                for h in pair:
                                    a = h.at_t[k] + (i - k) * P
                                    ins = mm(ps[7][h.base:h.base + HD, i * P:(i + 1) * P], h.v(k),
                                             probT[:, h.idx % 2, a:a + P], start=k == h.lo[i], stop=k == i)
                                    if i == k == TB - 1:
                                        ins.then_inc(s_pv, 1)

                for n in range(len(s.heads) + 2):
                    new = s.heads[n] if n < len(s.heads) else None
                    mid = s.heads[n - 1] if 0 <= n - 1 < len(s.heads) else None
                    old = s.heads[n - 2] if n >= 2 else None
                    score = [(i, m) for i in range(TB) for m in range(len(new.qs))] if new else []
                    if old is None or (old.piece is None and not old.base):
                        value = []
                    elif old.piece is not None:
                        value = [lambda: piece_values(old)]
                    else:
                        pair = (s.heads[n - 3], old)
                        value = [(lambda pair, j: lambda: values(pair, j))(pair, j) for j in range(len(old.queries))]
                    turns = list(range(len(mid.queries))) if mid else []
                    if n == 0 and new.bias == "forget":
                        forget_bias(new)
                    bias = s.heads[n + 1:n + 2] if n + 1 < len(s.heads) and s.heads[n + 1].bias == "forget" else []
                    if s.late:
                        parts = (("s", 2), ("v", 1), ("s", 1), ("v", 1), ("s", 1), ("v", 9), ("t", 9))
                    elif len(score) > TB:
                        parts = (("s", 3), ("v", 1), ("s", 1), ("v", 1), ("s", 1), ("v", 9), ("s", 1),
                                         ("t", 1), ("s", 1), ("t", 9), ("s", 9))
                    else:
                        parts = (("s", 1), ("v", 1), ("s", 1), ("v", 1), ("s", 1), ("v", 9), ("t", 9),
                                         ("s", 9), ("f", 1))
                    for what, count in parts:
                        for _ in range(count):
                            if what == "s" and score:
                                scores(new, *score.pop(0))
                            elif what == "v" and value:
                                value.pop(0)()
                            elif what == "f" and bias:
                                forget_bias(bias.pop(0))
                            elif what == "t" and turns:
                                turn(mid, turns.pop(0))

            def out_proj(s):
                A = s.at
                g0 = A["group"]
                pe.wait_ge(s_hlo, A["hin"])
                if s.prev.diff:
                    for c in range(6):
                        pe.wait_ge(s_y, c // 2 + 1)
                        if c >= 4:
                            pe.wait_ge(s_hlo, A["hin"] + c - 4 + 1)
                        for b in range(TB):
                            ins = nc.tensor.transpose(bank(g0 + 1, c % 4)[:, b * P:(b + 1) * P],
                                                      pieces[c // 2][:, b, (c % 2) * P:(c % 2) * P + P], ident)
                        ins.then_inc(s_tr, 1)
                for gi in range(2):
                    for j in range(KT):
                        n = A["tile"] + gi * 8 + j
                        wait_weights(n)
                        if s.prev.diff:
                            pe.wait_ge(s_hlo, A["hin"] + (min(j + 1, 6) if gi == 0 else 6))
                        for b in range(4):
                            for m, (a, c) in enumerate(passes):
                                ins = mm(bank(g0 + gi, b)[:, :], (w_hi, w_lo)[a][:, n % RING, b * P:(b + 1) * P],
                                         (h_hi, h_lo)[c][:, j, :], start=j == 0 and m == 0,
                                         stop=j == KT - 1 and m == 2)
                        ins.then_inc(s_used, 1)

            def mlp(s):
                A = s.at
                g0 = A["group"]
                with pe.Fori(0, HALVES) as i:
                    for gi in range(MLP_GROUPS):
                        up = gi < 4
                        base = 8 * gi if up else 32 + 16 * (gi - 4)
                        for j in range(8 if up else 16):
                            t = base + j
                            n = A["tile"] + t
                            pe.wait_ge(s_wlo, i * MLP_TILES + (n + 1))
                            if gi == 0:
                                pe.wait_ge(s_hlo, A["hin"] + j + 1)
                            if gi == 4:
                                pe.wait_ge(s_hid, i * HID + (A["hid"] + j + 1))
                            src = (h_hi, h_lo) if up else (hid_hi, hid_lo)
                            for b in range(4):
                                if j == 0:
                                    pe.wait_ge(s_free, i * 24 + (A["free"] + 4 * gi - 8 + b + 1))
                                    if gi == 1 and b == 3:
                                        pe.wait_ge(s_rbc, i * 1 + (A["bc"] + 1))
                                for m, (a, c) in enumerate(passes):
                                    ins = mm(bank(g0 + gi, b)[:, :], (w_hi, w_lo)[a][:, n % RING, b * P:(b + 1) * P],
                                             src[c][:, j, :], start=j == 0 and m == 0,
                                             stop=j == (7 if up else 15) and m == 2)
                            ins.then_inc(s_used, 1)
                            if gi == 0 and j == 4:
                                pe.wait_ge(s_sqc, A["sq"] + 8)
                                pe.wait_ge(s_free, i * 24 + A["free"])
                                stat_mm(s, bank(g0 + 1, 0))
                            if gi == 0 and j == 7:
                                pe.wait_ge(s_diag, i * 1 + (A["bc"] + 1))
                                bc_mm(bank(g0 + 1, 3))

            for s in stages:
                {"proj": proj, "attn": attention, "out": out_proj, "mlp": mlp}[s.kind](s)

        def source(s):
            return (kT, MEM) if s.mem else (xT, SEQ)

        def hi_lo(s):
            return (hid_hi, hid_lo) if s.mem else (h_hi, h_lo)

        @block.scalar
        def _(act):
            order = Order(act, s_act)
            do, sync = order.do, order.sync
            split = [0]

            def split_to(limit):
                while split[0] < min(limit, LOADED):
                    n = split[0]
                    act.wait_ge(s_load[n // 2 % PAIRS], 16 * (n // RING + 1))
                    if n >= RING:
                        act.wait_ge(s_used, n - RING + 1)
                    do(nc.scalar.activation(w_hi[:, n % RING], stage_w[:, n // 2 % PAIRS, n % 2], ACT.Copy), s_whi)
                    split[0] += 1

            def square(q, src, scale=1.0):
                if q >= 2:
                    act.wait_ge(s_sqc, q - 1)
                do(nc.scalar.activation(sqb[:, q % 2, 0:src.shape[-1]], src, ACT.Square, scale=scale), s_sq)

            def norm_input(s, tiles):
                A = s.at
                x, m = source(s)
                g = V_GAIN[s.norm]
                if not s.mem:
                    act.wait_ge(s_in[3], 16 * PAIRS)
                if s.h_free and s.prev.kind == "mlp":
                    act.wait_ge(s_used, s.h_free)
                for j in tiles:
                    if s.mem:
                        act.wait_ge(s_mem[j // 2], 16)
                    if s.h_free and s.prev.kind != "mlp":
                        act.wait_ge(s_used, s.h_free - KT + j + 1)
                    if s.x_free:
                        act.wait_ge(s_free, s.x_free - KT + j + 1)
                    do(nc.scalar.activation(hi_lo(s)[0][:, j, 0:m], x[:, j, 0:m], ACT.Copy,
                                            scale=vec[:, g + j:g + j + 1]), s_hhi)
                    square(A["sq"] + j, x[:, j, 0:m])

            def take_root(v, w):
                act.wait_ge(s_var, v + 1)
                do(nc.scalar.activation(root[:, 0:w], var[:, 0:w], ACT.Sqrt), s_root)

            def head_squares(s, g):
                act.wait_ge(s_used, g.end)
                act.wait_ge(s_rn, s.at["rn"] + 1)
                for b in range(g.blocks):
                    square(g.sq0 + b, ps[4 * (g.grp % 2) + b][:, 0:HD * g.heads], rn[:, b:b + 1])
                take_root(g.var, g.heads * g.blocks)

            def split_hi(h):
                for m, d in enumerate(h.splits):
                    q2, k2, _ = d["slot"]
                    own = slice(h.row, h.row + HD)
                    if d["used"]:
                        act.wait_ge(s_score, d["used"])
                    do(nc.scalar.activation(q2[own, :], h.qs[m], ACT.Copy), s_act if not d["same"] else s_qkhi)
                    if not d["same"]:
                        do(nc.scalar.activation(k2[own, 0:h.ks[m].shape[-1]], h.ks[m], ACT.Copy), s_qkhi)
            def transposed(g):
                act.wait_ge(s_in[5], 16)
                if g.scale != 1.0:
                    act.wait_ge(s_set, 1)
                for c in range(0, len(g.qk), 2):
                    act.wait_ge(s_tr, g.tr0 + 1)
                    do(nc.scalar.activation(g.qk[c], ps[4 * (g.grp % 2) + c][:, 0:P * g.blocks], ACT.Copy,
                                            scale=g.scale if g.rope else head_gain(g)), s_tra)

            def proj(s):
                A = s.at
                if s.prev is None:
                    for k in range(KT):
                        norm_input(s, [k])
                        split_to(k + 1)
                if s.prev and s.prev.kind == "proj":
                    for k in range(KT):
                        norm_input(s, [k])
                        split_to(A["tile"] - KT + k + 1 + RING)
                split_to(A["tile"] + RING)
                if s.carry:
                    head_squares(s.prev, s.carry)
                g0 = s.groups[0]
                split_to(g0.tile0 + g0.slots * 3 // 4 + RING)
                take_root(A["var"], 2 if s.mem else TB)
                if s.forget:
                    split_to(g0.end + RING)
                    act.wait_ge(s_fabs, 1)
                    do(nc.scalar.activation(fe[:], fa[:], ACT.Exp, scale=-1.0))
                    sync()
                    do(nc.scalar.activation(fl[:], fe[:], ACT.Ln, bias=1.0), s_fln)
                if s.carry:
                    split_to(g0.end + RING)
                    transposed(s.carry)
                for gi, g in enumerate(s.groups):
                    if s.forget and gi == 5:
                        split_to(g.tile0 + 3 + RING)
                        act.wait_ge(s_cmm, 1)
                        do(nc.scalar.activation(c_hi[:], ps[4 * ((g.grp + 1) % 2)][0:16, :], ACT.Copy), s_chi)
                    if g.heads and g is s.groups[-1]:
                        continue
                    split_to(g.end + RING)
                    if not g.heads:
                        continue
                    head_squares(s, g)
                    nxt = s.groups[gi + 1]
                    split_to(2 * RING if s.mem else nxt.tile0 + nxt.slots * 3 // 4 + RING)
                    transposed(g)
                    if g.ahead:
                        act.wait_ge(s_trv, g.ahead.at["trv"])
                        act.wait_ge(s_sqc, g.ahead.at["sq"])
                        sync()
                        split_hi(g.ahead.heads[0])

            def attention(s):
                A = s.at
                split_to(A["tile"] + RING)

                def exps(h, i):
                    unit = h.unit0 + i
                    for m in range(len(h.qs)):
                        sm = h.sm0 + i * len(h.qs) + m
                        col = slice(sm % 16, sm % 16 + 1)
                        act.wait_ge(s_max, sm + 1)
                        if m == 1:
                            dst = second[unit % 3][:, 0:h.w[i]]
                            if unit - 3 >= A["unit"]:
                                act.wait_ge(s_pn, unit - 2)
                        else:
                            dst = prob[:, h.idx % 2, h.at_p[i]:h.at_p[i] + h.w[i]]
                            if h.idx - 2 >= A["head"]:
                                old = s.heads[h.idx - 2 - A["head"]]
                                act.wait_ge(s_pt, old.pt0 + len(old.queries))
                        src = dst if h.bias is not None else ps[h.bank[sm - h.sm0][0]][:, 0:h.w[i]]
                        do(nc.scalar.activation(dst, src, ACT.Exp, scale=-1.0, bias=mneg[:, col],
                                                accum_out=den[:, col]), s_prob)

                def forget_copy(h):
                    act.wait_ge(s_fbc, h.fb)
                    if h.fb > 2:
                        act.wait_ge(s_max, h.sm0 - TB)
                    do(nc.scalar.activation(bias_f[:, h.idx % 2], ps[h.fbank[0]][:, :], ACT.Copy), s_fb)

                def copies(h):
                    if h.idx - 2 >= A["head"]:
                        act.wait_ge(s_pv, h.idx - 1)
                    for j in range(0, len(h.queries), 2):
                        act.wait_ge(s_pt, h.pt0 + j + 1)
                        w = P * len(h.queries[j])
                        do(nc.scalar.activation(probT[:, h.idx % 2, h.at_t[j]:h.at_t[j] + w], ps[3 + j][:, 0:w],
                                                ACT.Copy), s_pta)

                def output(h):
                    if h.piece is not None:
                        act.wait_ge(s_pv, h.idx + 1)
                        p = pieces[h.piece // 2][:, :, (h.piece % 2) * P:(h.piece % 2) * P + P]
                        do(nc.scalar.activation(p, ps[7][:, :].rearrange("p (b d) -> p b d", b=TB), ACT.Copy), s_o)
                    elif h.base:
                        act.wait_ge(s_pv, h.idx + 1)
                        do(nc.scalar.activation(h_hi[:, h.tile, :], ps[7][:, :], ACT.Copy), s_hhi)

                if not s.diff:
                    act.wait_ge(s_free, A["free"])
                act.wait_ge(s_used, A["tile"])
                act.wait_ge(s_trv, A["trv"])
                act.wait_ge(s_sqc, A["sq"])
                sync()
                if not s.early:
                    split_hi(s.heads[0])
                if s.heads[0].bias == "forget":
                    forget_copy(s.heads[0])
                for n in range(len(s.heads) + 2):
                    new = s.heads[n] if n < len(s.heads) else None
                    if n + 1 < len(s.heads):
                        split_hi(s.heads[n + 1])
                    for i in range(3 if new else 0):
                        exps(new, i)
                    if not s.late:
                        if s.diff and n >= 2:
                            output(s.heads[n - 2])
                        if 0 <= n - 1 < len(s.heads):
                            copies(s.heads[n - 1])
                    if new:
                        exps(new, 3)
                    if n + 1 < len(s.heads) and s.heads[n + 1].bias == "forget":
                        forget_copy(s.heads[n + 1])
                    if s.diff and 2 <= n < 8:
                        k = n - 2
                        if k >= 2:
                            act.wait_ge(s_sqc, A["sq"] + k - 1)
                        act.wait_ge(s_o, k + 1)
                        do(nc.scalar.activation(bias_f[:, k % 2].rearrange("p (b d) -> p b d", b=TB),
                                                pieces[k // 2][:, :, (k % 2) * P:(k % 2) * P + P], ACT.Square), s_sq)
                    if s.diff and n == 8:
                        take_root(A["var"], 24)
                    if n < s.z:
                        act.wait_ge(s_used, A["tile"])
                        act.wait_ge(s_z, n + 1)
                        do(nc.scalar.activation(h_hi[:, n, :], qT[:, n, :], ACT.Copy), s_hhi)
                    if n >= 2 and not s.diff:
                        output(s.heads[n - 2])
                    if s.late and 0 <= n - 1 < len(s.heads):
                        copies(s.heads[n - 1])

            def out_proj(s):
                A = s.at
                split_to(A["tile"] + RING)
                if s.prev.diff:
                    for c in range(6):
                        act.wait_ge(s_tr, A["tr"] + c + 1)
                        do(nc.scalar.activation(h_hi[:, c, :], ps[4 * ((A["group"] + 1) % 2) + c % 4][:, :], ACT.Copy,
                                                scale=vec[:, V_SUB:V_SUB + 1]), s_hhi)
                split_to(A["tile"] + 8 + RING)
                for j in range(4):
                    split_to(A["tile"] + 8 + j + 1 + RING)
                    norm_input(s.next, [j])
                split_to(A["tile"] + 16 + RING)
                norm_input(s.next, range(4, KT))

            def mlp(s):
                A = s.at
                for half in range(HALVES):
                    t0 = A["tile"] + half * MLP_TILES
                    split_to(t0 + 5 + RING)
                    take_root(A["var"] + half, TB)
                    for u in range(4):
                        split_to(t0 + 8 * (u + 1) + RING)
                        for b in range(4):
                            t = 4 * u + b
                            hid = A["hid"] + half * HID + t
                            act.wait_ge(s_free, A["free"] + 24 * half + t + 1)
                            if hid >= 2:
                                act.wait_ge(s_hid, hid - 1)
                            do(nc.scalar.activation(hsq[:, t % 2], relu[:, t % 2], ACT.Square), s_hsq)
                            sync()
                            do(nc.scalar.activation(hid_hi[:, t], hsq[:, t % 2], ACT.Copy), s_hidhi)
                    early = half == HALVES - 1 and not s.last
                    if early:
                        split_to(t0 + 48 + RING)
                        norm_input(s.next, range(4))
                    split_to(t0 + MLP_TILES + RING)
                    if early:
                        norm_input(s.next, range(4, KT))

            act.wait_ge(s_in[1], 16)
            for s in stages:
                if s.forget:
                    act.wait_ge(s_in[4], 16)
                    do(nc.scalar.activation(wf_hi[:], wf_in[:], ACT.Copy), s_seta)
                {"proj": proj, "attn": attention, "out": out_proj, "mlp": mlp}[s.kind](s)
                if s is stages[1]:
                    act.wait_ge(s_set, 2)
                    do(nc.scalar.activation(lam[:, 2:4], lam[:, 0:2], ACT.Exp), s_seta)

        @block.vector
        def _(dve):
            order = Order(dve, s_dve)
            do, sync = order.do, order.sync
            vt, vs, stt, tt = (nc.vector.tensor_tensor, nc.vector.tensor_scalar,
                               nc.vector.scalar_tensor_tensor, nc.vector.tensor_tensor)

            def norm_input(s, tiles):
                A = s.at
                x, m = source(s)
                hi, lo = hi_lo(s)
                g = V_GAIN[s.norm]
                for j in tiles:
                    dve.wait_ge(s_hhi, A["hin"] + j + 1)
                    do(stt(lo[:, j, 0:m], x[:, j, 0:m], vec[:, g + j:g + j + 1], hi[:, j, 0:m].bitcast(F32),
                           ALU.mult, ALU.subtract), s_hlo)
                    q = A["sq"] + j
                    dve.wait_ge(s_sq, q + 1)
                    if j == 0:
                        do(nc.vector.tensor_copy(ssum[:, 0:m], sqb[:, q % 2, 0:m]), s_sqc)
                    else:
                        sync()
                        do(tt(ssum[:, 0:m], ssum[:, 0:m], sqb[:, q % 2, 0:m], ALU.add), s_sqc)

            def rsqrt(out, v, w, signal=None):
                dve.wait_ge(s_root, v + 1)
                do(nc.vector.reciprocal(inv[:, 0:w], root[:, 0:w]))
                sync()
                do(tt(newt[:, 0:w], inv[:, 0:w], inv[:, 0:w], ALU.mult))
                sync()
                do(tt(newt[:, 0:w], newt[:, 0:w], var[:, 0:w], ALU.mult))
                sync()
                do(vs(newt[:, 0:w], newt[:, 0:w], -0.5, 1.5, ALU.mult, ALU.add))
                sync()
                do(tt(out, inv[:, 0:w], newt[:, 0:w], ALU.mult), signal)
                sync()

            def token_norm(s, other, turn=0):
                A = s.at
                nb = 2 if s.mem else TB
                dve.wait_ge(s_stat, A["stat"] + turn + 1)
                do(vs(var[:, 0:nb], ps[4 * (other % 2)][:, 0:nb], EPS, None, ALU.add), s_var)
                rsqrt(rn[:, 0:nb], A["var"] + turn, nb, s_rn)
                if s.rbc or s.kind == "mlp":
                    for b in range(TB):
                        do(vs(rms_bc[:, b * P:(b + 1) * P], ident, rn[:, b:b + 1], float(D), ALU.mult, ALU.mult),
                           s_diag if b == TB - 1 else None)
                    dve.wait_ge(s_bc, A["bc"] + turn + 1)
                    do(nc.vector.tensor_copy(rms_bc[:], ps[4 * (other % 2) + 3][:, :]), s_rbc)
                    sync()

            def forget_gates(s):
                bank = ps[4 * ((s.groups[0].grp + 1) % 2) + 2]
                dve.wait_ge(s_fmm, 1)
                for b in range(TB):
                    do(stt(fz[:, 16 * b:16 * b + 16], bank[:, 16 * b:16 * b + 16], rn[:, b:b + 1],
                           vec[:, V_FORGET:V_FORGET + 16], ALU.mult, ALU.add))
                sync()
                do(stt(fa[:], fz[:], -1.0, fz[:], ALU.mult, ALU.max), s_fabs)
                dve.wait_ge(s_fln, 1)
                do(stt(fa[:], fz[:], 0.0, fl[:], ALU.min, ALU.subtract))
                sync()
                do(nc.vector.tensor_copy(fl[:], fa[:]), s_flog)

            def heads(s, g):
                nb, nh, par = g.blocks, g.heads, g.grp % 2
                w = nb * nh
                for b in range(nb):
                    q = g.sq0 + b
                    dve.wait_ge(s_sq, q + 1)
                    do(nc.vector.tensor_reduce(hsum[:, b * nh:(b + 1) * nh],
                                               sqb[:, q % 2, 0:nh * HD].rearrange("p (h d) -> p h d", d=HD),
                                               axis=AX.X, op=ALU.add), s_sqc)
                sync()
                do(vs(var[:, 0:w], hsum[:, 0:w], 1.0 / HD, EPS, ALU.mult, ALU.add), s_var)
                rsqrt(hsum[:, 0:w], g.var, w)
                do(tt(newt[:, 0:w].rearrange("p (b h) -> p b h", b=nb), hsum[:, 0:w].rearrange("p (b h) -> p b h", b=nb),
                      rn[:, 0:nb].unsqueeze(2).to_broadcast([P, nb, nh]), ALU.mult))
                sync()
                if g.tr0:
                    dve.wait_ge(s_tr, g.tr0)
                for b in range(nb):
                    bank = ps[4 * par + b]
                    do(tt(tn[:, par, b, 0:nh * HD].rearrange("p (h d) -> p h d", d=HD),
                          bank[:, 0:nh * HD].rearrange("p (h d) -> p h d", d=HD),
                          newt[:, b * nh:(b + 1) * nh].unsqueeze(2).to_broadcast([P, nh, HD]), ALU.mult),
                       None if g.v else s_free)
                    if g.v:
                        values(g, b)
                if not g.rope:
                    return
                sync()
                for n, (first, count, name) in enumerate(g.gains):
                    t = tn[:, par, 0:nb, first * HD:(first + count) * HD].rearrange("p b (h d) -> p b h d", d=HD)
                    gain = vec[:, V_HEAD[name]:V_HEAD[name] + HD]
                    gain = gain.unsqueeze(1).unsqueeze(1).to_broadcast([P, nb, count, HD])
                    do(tt(t, t, gain, ALU.mult))
                rope(g)

            def rope(g):
                sync()
                nr = g.rope
                t = tn[:, g.grp % 2, 0:TB, 0:nr * HD].rearrange("p b (h d) -> p b h d", d=HD)
                a, b = t[:, :, :, 0:8], t[:, :, :, 8:16]
                cos, sin = (cst[:, c:c + 32].rearrange("p (b d) -> p b d", b=TB).unsqueeze(2)
                            .to_broadcast([P, TB, nr, 8]) for c in (C_COS, C_SIN))
                m = [rope_t[:, k, 0:32 * nr].rearrange("p (b h d) -> p b h d", b=TB, h=nr) for k in range(4)]
                do(tt(m[0], a, cos, ALU.mult))
                do(tt(m[1], b, sin, ALU.mult))
                do(tt(m[2], a, sin, ALU.mult))
                do(tt(m[3], b, cos, ALU.mult))
                sync()
                do(tt(a, m[0], m[1], ALU.subtract))
                do(tt(b, m[2], m[3], ALU.add), s_t)

            def values(g, b):
                q = g.heads * HD
                do(vs(g.v(b, g.width - q), ps[4 * (g.grp % 2) + b][:, q:g.width], rn[:, b:b + 1], None, ALU.mult),
                   s_free)

            def features(g):
                for n, (kind, j) in enumerate(g.t):
                    bank = ps[4 * (g.grp % 2) + n]
                    if kind == "c":
                        do(tt(kT[:, j, :], bank[:, :], rms_bc[:], ALU.mult), s_free)
                        continue
                    tmp = relu[:, 0]
                    do(tt(tmp, bank[:, :], rms_bc[:], ALU.mult), s_free)
                    sync()
                    z = qT[:, j, :]
                    if kind == "b":
                        do(tt(z, z, tmp, ALU.mult), s_z)
                        sync()
                        continue
                    do(tt(uP[:, j, 2:514], tmp, kT[:, j, :], ALU.mult))
                    sync()
                    w = [vec[:, V_CONV + 6 * k + j:V_CONV + 6 * k + j + 1] for k in range(3)]
                    do(vs(z, uP[:, j, 0:512], w[0], None, ALU.mult))
                    sync()
                    for k in (1, 2):
                        do(stt(z, uP[:, j, k:k + 512], w[k], z, ALU.mult, ALU.add))
                        sync()

            def make_bias(h, first=False):
                w, log = (512, C_LOGW) if h.bias == "dilated" else (256, C_WIN)
                if not first:
                    dve.wait_ge(s_max, h.sm0 - TB)
                if h.sink is not None:
                    do(nc.vector.memset(bias_t[:, h.idx % 2, w:w + 1], 0.0))
                do(stt(bias_t[:, h.idx % 2, 0:w], cst[:, C_DELTA + 512 - w:C_DELTA + 512], h.slope,
                       cst[:, log:log + w], ALU.mult, ALU.add))

            def key_again(h):
                for m, d in enumerate(h.splits):
                    if not d["same"]:
                        if d["used"]:
                            dve.wait_ge(s_score, d["used"])
                        do(nc.vector.tensor_copy(d["slot"][1][HD - h.row:2 * HD - h.row, 0:h.ks[m].shape[-1]],
                                                 h.ks[m]), s_k2)

            def transposed(g):
                for c in range(1, len(g.qk), 2):
                    dve.wait_ge(s_tr, g.tr0 + 1)
                    do(vs(g.qk[c], ps[4 * (g.grp % 2) + c][:, 0:P * g.blocks],
                          g.scale if g.rope else head_gain(g), None, ALU.mult), s_trv)

            def small_constants():
                dve.wait_ge(s_in[0], 16)
                dve.wait_ge(s_in[2], 16)
                do(nc.vector.tensor_copy(ident_b[:], ident))
                do(nc.vector.tensor_copy(causal_b[:], cst[:, C_CAUSAL:C_CAUSAL + P]))
                do(nc.vector.tensor_copy(ident_r[:], cst[:, 0:16]))
                do(vs(nsink[:], vec[:, V_SINK:V_SINK + 8], -1.0, None, ALU.mult))
                do(vs(q_gain[:], vec[:, V_LAM + 256:V_ALL], ATT, None, ALU.mult), s_set)
                for n in range(2):
                    a = V_LAM + 128 * n
                    do(tt(fz[:, 0:64], vec[:, a:a + 64], vec[:, a + 64:a + 128], ALU.mult))
                    sync()
                    do(nc.vector.tensor_reduce(lam[:, n:n + 1], fz[:, 0:64], axis=AX.X, op=ALU.add), s_set if n else None)
                    sync()

            def proj(s):
                A = s.at
                if s.prev is None or s.prev.kind == "proj":
                    norm_input(s, range(KT))
                if s.prev is None:
                    dve.wait_ge(s_in[5], 16)
                elif s.prev.mem:
                    small_constants()
                if s.carry:
                    dve.wait_ge(s_used, s.carry.end)
                    heads(s.prev, s.carry)
                token_norm(s, s.groups[0].grp + 1)
                if s.forget:
                    forget_gates(s)
                if s.rbc:
                    do(nc.vector.memset(uP[:, :, 0:2], 0.0))
                    sync()
                if s.carry:
                    transposed(s.carry)
                for gi, g in enumerate(s.groups):
                    if g.heads and g is s.groups[-1]:
                        continue
                    if s.forget and gi == 5:
                        dve.wait_ge(s_chi, 1)
                        do(tt(c_lo[:], ps[4 * ((g.grp + 1) % 2)][0:16, :], c_hi[:].bitcast(F32), ALU.subtract), s_clo)
                    soon = s.next.diff and g is s.groups[-1]
                    if soon:
                        do(nc.vector.memset(bias_c[:, 0:SEQ - P], 0.0))
                        do(nc.vector.tensor_copy(bias_c[:, SEQ - P:SEQ], cst[:, C_CHUNK:C_CHUNK + P]))
                    dve.wait_ge(s_used, g.end)
                    if soon:
                        dve.wait_ge(s_tra, s.next.at["tra"])
                        sync()
                        key_again(s.next.heads[0])
                    if g.form == "T":
                        features(g)
                    elif g.heads:
                        heads(s, g)
                        transposed(g)
                        if g.ahead:
                            dve.wait_ge(s_tra, g.ahead.at["tra"])
                            sync()
                            key_again(g.ahead.heads[0])
                            if g.ahead.heads[0].bias == "dilated":
                                make_bias(g.ahead.heads[0], first=True)
                                sync()
                    else:
                        for b in range(g.blocks):
                            values(g, b)

            def attention(s):
                A = s.at
                dve.wait_ge(s_tr, A["tr"])
                dve.wait_ge(s_tra, A["tra"])
                dve.wait_ge(s_used, A["tile"])
                sync()

                def row_min(h, i):
                    n = h.w[i]
                    bias = None
                    if h.bias:
                        w = 257 if h.bias == "window" else 512
                        if h.bias == "forget":
                            dve.wait_ge(s_fb, h.fb)
                            bias = bias_f[:, h.idx % 2, 0:n]
                        else:
                            bias = (bias_c if h.bias == "chunk" else bias_t[:, h.idx % 2])[:, w - n:w]
                    for m in range(len(h.qs)):
                        sm = h.sm0 + i * len(h.qs) + m
                        low = mneg[:, sm % 16:sm % 16 + 1]
                        dve.wait_ge(s_score, sm + 1)
                        src = ps[h.bank[sm - h.sm0][0]][:, 0:n]
                        if bias is None:
                            do(nc.vector.tensor_reduce(low, src, axis=AX.X, op=ALU.min), s_max)
                            continue
                        if h.idx - 2 >= A["head"]:
                            old = s.heads[h.idx - 2 - A["head"]]
                            dve.wait_ge(s_pt, old.pt0 + len(old.queries))
                        dst = prob[:, h.idx % 2, h.at_p[i]:h.at_p[i] + n]
                        if m == 1:
                            unit = h.unit0 + i
                            dst = second[unit % 3][:, 0:n]
                            if unit - 3 >= A["unit"]:
                                dve.wait_ge(s_pn, unit - 2)
                        do(nc.vector.tensor_tensor_reduce(
                            out=dst, in0=src, in1=bias, scale=1.0, scalar=3e38,
                            op0=ALU.add, op1=ALU.min, accum_out=low), s_max)

                def invert(h, i):
                    sm = h.sm0 + i * len(h.qs)
                    dve.wait_ge(s_prob, sm + len(h.qs))
                    c = [slice((sm + m) % 16, (sm + m) % 16 + 1) for m in range(len(h.qs))]
                    for k in c:
                        do(nc.vector.reciprocal(rden[:, k], den[:, k]))
                    h.inverse[i] = order.mark()

                def normalise(h, i):
                    sm = h.sm0 + i * len(h.qs)
                    c = [slice((sm + m) % 16, (sm + m) % 16 + 1) for m in range(len(h.qs))]
                    p1 = prob[:, h.idx % 2, h.at_p[i]:h.at_p[i] + h.w[i]]
                    dve.wait_ge(*h.inverse[i])
                    if len(c) == 1:
                        do(vs(p1, p1, rden[:, c[0]], None, ALU.mult), s_pn)
                        return
                    do(tt(lden[:, c[1]], rden[:, c[1]], lam[:, 4:5], ALU.mult))
                    do(vs(p1, p1, rden[:, c[0]], None, ALU.mult))
                    sync()
                    do(stt(p1, second[(h.unit0 + i) % 3][:, 0:h.n[i]], lden[:, c[1]], p1, ALU.mult, ALU.add), s_pn)

                def copies(h):
                    if len(h.queries) > 1 and h.idx - 2 >= A["head"]:
                        dve.wait_ge(s_pv, h.idx - 1)
                    for j in range(1, len(h.queries), 2):
                        dve.wait_ge(s_pt, h.pt0 + j + 1)
                        w = P * len(h.queries[j])
                        do(nc.vector.tensor_copy(probT[:, h.idx % 2, h.at_t[j]:h.at_t[j] + w], ps[3 + j][:, 0:w]), s_ptv)

                hin = [A["hin"]]

                def low_part(tile, src):
                    hin[0] += 1
                    dve.wait_ge(s_hhi, hin[0])
                    do(tt(h_lo[:, tile, :], src, h_hi[:, tile, :].bitcast(F32), ALU.subtract), s_hlo)

                for n in range(len(s.heads) + 2):
                    new = s.heads[n] if n < len(s.heads) else None
                    mid = s.heads[n - 1] if 0 <= n - 1 < len(s.heads) else None
                    if n and new and new.bias in ("dilated", "window"):
                        sync()
                    if n + 1 < len(s.heads):
                        key_again(s.heads[n + 1])
                    old = s.heads[n - 3] if n >= 3 else None
                    if new:
                        row_min(new, 0)
                    if mid:
                        invert(mid, 3)
                    if new:
                        row_min(new, 1)
                    if mid:
                        normalise(mid, 3)
                    if new:
                        invert(new, 0)
                        row_min(new, 2)
                        normalise(new, 0)
                        invert(new, 1)
                    if old and old.piece is None and old.base:
                        low_part(old.tile, ps[7][:, :])
                    if mid and not s.late:
                        copies(mid)
                    if new:
                        normalise(new, 1)
                        invert(new, 2)
                        row_min(new, 3)
                        normalise(new, 2)
                    if mid and s.late:
                        copies(mid)
                    if new:
                        if n + 1 < len(s.heads) and new.bias in ("dilated", "window"):
                            make_bias(s.heads[n + 1], first=n == 0)
                    if n < s.z:
                        low_part(n, qT[:, n, :])
                    if s.diff and 2 <= n < 8:
                        k = n - 2
                        dve.wait_ge(s_sq, A["sq"] + k + 1)
                        sums = hsum[:, 0:24].rearrange("p (c b t) -> p c b t", b=TB, t=2)[:, k // 2, :, k % 2]
                        do(nc.vector.tensor_reduce(sums, bias_f[:, k % 2].rearrange("p (b d) -> p b d", b=TB),
                                                   axis=AX.X, op=ALU.add), s_sqc)
                    if s.diff and n == 7:
                        sync()
                        do(vs(var[:, 0:24], hsum[:, 0:24], 1.0 / P, SUBLN_EPS, ALU.mult, ALU.add), s_var)
                    if s.diff and n == 9:
                        rsqrt(hsum[:, 0:24], A["var"], 24)
                        do(vs(newt[:, 0:24], hsum[:, 0:24], 1.0 - LAM_INIT, None, ALU.mult), s_yr)
                low_part(s.heads[-1].tile, ps[7][:, :])

            def residual(s, group, first):
                for b in range(4):
                    x = xT[:, first + b, :]
                    do(tt(x, x, ps[4 * (group % 2) + b][:, :], ALU.add), s_free)
                    yield b

            def out_proj(s):
                A = s.at
                if s.prev.diff:
                    for c in range(6):
                        dve.wait_ge(s_hhi, A["hin"] + c + 1)
                        do(stt(h_lo[:, c, :], ps[4 * ((A["group"] + 1) % 2) + c % 4][:, :], vec[:, V_SUB:V_SUB + 1],
                               h_hi[:, c, :].bitcast(F32), ALU.mult, ALU.subtract), s_hlo)
                dve.wait_ge(s_used, A["tile"] + 8)
                for b in residual(s, A["group"], 0):
                    pass
                norm_input(s.next, range(4))
                dve.wait_ge(s_used, A["tile"] + 16)
                for b in residual(s, A["group"] + 1, 4):
                    norm_input(s.next, [4 + b])

            def mlp(s):
                A = s.at
                for half in range(HALVES):
                    t0 = A["tile"] + half * MLP_TILES
                    hid = A["hid"] + half * HID
                    token_norm(s, A["group"] + 1, half)

                    def low(t):
                        dve.wait_ge(s_hidhi, hid + t + 1)
                        do(tt(hid_lo[:, t], hsq[:, t % 2], hid_hi[:, t].bitcast(F32), ALU.subtract), s_hid)

                    for u in range(4):
                        dve.wait_ge(s_used, t0 + 8 * (u + 1))
                        for b in range(4):
                            t = 4 * u + b
                            if hid + t >= 2:
                                dve.wait_ge(s_hsq, hid + t - 1)
                            do(stt(relu[:, t % 2], ps[4 * ((A["group"] + u) % 2) + b][:, :], 0.0, rms_bc[:],
                                   ALU.max, ALU.mult), s_free)
                            if t:
                                low(t - 1)
                    low(HID - 1)
                    early = half == HALVES - 1 and not s.last
                    dve.wait_ge(s_used, t0 + 48)
                    for b in residual(s, A["group"], 0):
                        pass
                    if early:
                        norm_input(s.next, range(4))
                    dve.wait_ge(s_used, t0 + MLP_TILES)
                    for b in residual(s, A["group"] + 1, 4):
                        if early:
                            norm_input(s.next, [4 + b])
                    sync()

            dve.wait_ge(s_in[1], 16)
            for s in stages:
                if s.forget:
                    dve.wait_ge(s_seta, 2)
                    do(tt(wf_lo[:], wf_in[:], wf_hi[:].bitcast(F32), ALU.subtract), s_wf)
                {"proj": proj, "attn": attention, "out": out_proj, "mlp": mlp}[s.kind](s)
                if s is stages[1]:
                    dve.wait_ge(s_seta, 1)
                    do(tt(lam[:, 5:6], lam[:, 3:4], lam[:, 2:3], ALU.subtract))
                    sync()
                    do(vs(lam[:, 4:5], lam[:, 5:6], -LAM_INIT, None, ALU.add))



def square_tiles(w, cols=None):
    out = []
    n = 0
    while n < w.shape[1]:
        width = TILE if (cols is None or cols[0] == TILE) else 256
        if cols is not None:
            cols = cols[1:]
        part = w[:, n:n + width]
        if width == TILE:
            out.append(part.reshape(-1, P, TILE))
        else:
            out.append(part.reshape(-1, 2, P, 256).transpose(0, 2, 1, 3).reshape(-1, P, TILE))
        n += width
    return out


def weight_stream(a):
    def mem_kv(l):
        return square_tiles(a["w_mem_kv_2"][l])

    def mlp(up, down):
        out = []
        for h in range(HALVES):
            w = FF // HALVES
            out += square_tiles(up[:, h * w:(h + 1) * w]) + square_tiles(down[h * w:(h + 1) * w])
        return out

    e = a["w_in_even"][0]
    aq, ak, av, bq, bk, bv = np.split(e, [512, 1024, 1536, 2048, 2176], axis=1)
    bq = bq.reshape(D, 2, 4, HD).transpose(0, 2, 1, 3).reshape(D, 512)
    o = a["w_in_odd"][0]
    b0 = a["a_w_in_2"][0]
    parts = mem_kv(0) + mem_kv(1)
    parts += square_tiles(np.concatenate([aq, ak, bq, bk, bv, av], 1), [TILE] * 3 + [256, TILE])
    parts += square_tiles(a["w_out_even"][0]) + mlp(a["w_up"][0], a["w_down"][0])
    parts += square_tiles(o[:, :3072]) + square_tiles(a["w_out_odd"][0]) + mlp(a["w_up"][1], a["w_down"][1])
    gate_b, gate_c, hv, qm = np.split(b0, [768, 1536, 2304], axis=1)
    parts += square_tiles(np.concatenate([gate_c[:, :TILE], qm, gate_c[:, TILE:], hv, gate_b], 1),
                          [TILE, 256] + [TILE] * 3 + [256])
    parts += square_tiles(a["w_o_2"][0]) + mlp(a["w_up_2"][0], a["w_down_2"][0])
    parts += square_tiles(a["b_w_q_2"][0]) + square_tiles(a["w_kv_2"])
    parts += square_tiles(a["w_o_2"][1]) + mlp(a["w_up_2"][1], a["w_down_2"][1])
    parts.append(parts[-1][:RING])
    w = np.concatenate(parts, 0)
    return np.ascontiguousarray(w.reshape(-1, 2, P, TILE).transpose(0, 2, 1, 3))


def kernel(**inputs):
    import concourse.bacc as _bacc
    from concourse import mybir as _mybir
    from concourse.bass_utils import run_bass_kernel_spmd as _run

    a = {k: np.asarray(v) for k, v in inputs.items()}

    def column(v):
        return v.reshape(-1, P).T

    def across(v):
        return np.broadcast_to(v.reshape(1, -1), (P, v.size))

    vecs = [column(a["g_mix"][0]), column(a["g_mix"][1]), column(a["g_mlp"][0]), column(a["g_mlp"][1]),
            column(a["norm_mix_2"][0]), column(a["norm_mix_2"][1]), column(a["norm_mlp_2"][0]),
            column(a["norm_mlp_2"][1]), column(a["kv_norm_2"]), column(a["mem_norm_2"]),
            column(a["a_conv_2"][0].reshape(-1)), column(a["b_subln_2"][0])]
    vecs += [across(v) for v in (
        a["a_q_gain"], a["a_k_gain"], a["b_q_gain"], a["b_k_gain"], a["c_q_gain"], a["c_k_gain"],
        a["b_q_norm_2"], a["k_norm_2"], a["mem_q_norm_2"][0], a["mem_q_norm_2"][1],
        a["mem_k_norm_2"][0], a["mem_k_norm_2"][1], a["b_sinks"], a["b_forget"], a["b_lam_2"])]
    vecs += [column(np.concatenate([v, v], axis=None)) for v in (
        a["a_q_gain"], a["a_k_gain"], a["b_q_gain"], a["b_k_gain"], a["c_q_gain"], a["c_k_gain"],
        a["b_q_norm_2"], a["k_norm_2"], a["mem_q_norm_2"][0], a["mem_q_norm_2"][1],
        a["mem_k_norm_2"][0], a["mem_k_norm_2"][1])]
    arrays = {
        "in_weights": weight_stream(a),
        "in_forget": np.ascontiguousarray(
            a["w_in_odd"][0][:, 3072:].reshape(KT, P, 16).transpose(1, 0, 2).reshape(P, -1)),
        "in_x": np.ascontiguousarray(a["x"][0].T),
        "in_mem": np.ascontiguousarray(a["mem_2"][0].T),
        "in_consts": constants(),
        "in_vecs": np.ascontiguousarray(np.concatenate(vecs, 1)),
    }
    nc = _bacc.Bacc("TRN2", target_bir_lowering=False, num_devices=1)
    args = [nc.dram_tensor(n, x.shape, _mybir.dt.from_np(x.dtype), kind="ExternalInput").ap()
            for n, x in arrays.items()]
    out = nc.dram_tensor("out_xT", (D, SEQ), _mybir.dt.float32, kind="ExternalOutput").ap()
    build(nc, *args, out)
    r = _run(nc, [arrays], core_ids=[0])
    y = r.results[0]["out_xT"]
    return np.ascontiguousarray(y.T).reshape(1, SEQ, D)
```
